# Optimizing a Trainium2 kernel written in Bass

```python
import math
import jax, jax.numpy as jnp
from jax import lax
import numpy as np

D_MODEL = 1024
BATCH = 1
SEQ = 128
DEPTH = 1
DEC_BATCH = 1
DEC_SEQ = 1024
PAST_LEN = 128

GRID_W = 64
ATT_HEADS = 4
QK_DIM = 64
V_DIM = 2 * QK_DIM
D_QK = ATT_HEADS * 2 * QK_DIM
D_ATT = ATT_HEADS * V_DIM
ROPE_BASE = 10000.0
Q_BLOCK = 128
D_SSM = D_MODEL // 2
SSM_HEADDIM = 64
SSM_HEADS = D_SSM // SSM_HEADDIM
SSM_GROUPS = 2
D_STATE = 128
CONV_W = 5
CHUNK = 128
XBC_DIM = D_SSM + 2 * SSM_GROUPS * D_STATE
MIX_W = D_ATT + D_SSM
IN_COLS = 2 * D_QK + D_ATT + D_SSM + XBC_DIM + 2 * SSM_HEADS
N_GROUPS = 4
EXPERTS_PER_GROUP = 4
N_EXPERTS = N_GROUPS * EXPERTS_PER_GROUP
TOP_K_IN_GROUP = 2
EXPERT_FF = 256
EPS = 1e-6

kernel_name = "hybrid_diffattn_ssd_hmoe_prefix_dit_step"

def rms_norm(x, g):
    xf = x.astype(jnp.float32)
    y = xf * lax.rsqrt(jnp.mean(xf * xf, axis=-1, keepdims=True) + EPS)
    return y.astype(x.dtype) * g

def ada_mod(cond, w, b):
    mod = (jax.nn.silu(cond) @ w + b)[..., None, :]
    return jnp.split(mod, 6, axis=-1)

def lambda_init(layer):
    return 0.8 - 0.6 * math.exp(-0.3 * layer)

def axial_rope(x, row_ids, col_ids):
    n_freq = QK_DIM // 4
    freqs = ROPE_BASE ** (-jnp.arange(n_freq, dtype=jnp.float32) / n_freq)

    def rotate(xa, pos):
        ang = pos[:, None] * freqs
        cos = jnp.cos(ang)[None, :, None, None, :].astype(xa.dtype)
        sin = jnp.sin(ang)[None, :, None, None, :].astype(xa.dtype)
        x1, x2 = jnp.split(xa, 2, axis=-1)
        return jnp.concatenate([x1 * cos - x2 * sin, x1 * sin + x2 * cos], axis=-1)

    half = QK_DIM // 2
    return jnp.concatenate([rotate(x[..., :half], row_ids), rotate(x[..., half:], col_ids)], axis=-1)

def diff_attention(q, k, v, lam):
    b, tq = q.shape[:2]
    nblk = tq // Q_BLOCK
    qb = jnp.moveaxis(q.reshape(b, nblk, Q_BLOCK, ATT_HEADS, 2, QK_DIM), 1, 0)
    scale = QK_DIM ** -0.5

    def block(qblk):
        s = jnp.einsum('bqhmd,bkhmd->bhmqk', qblk, k).astype(jnp.float32) * scale
        p = jax.nn.softmax(s, axis=-1)
        a = (p[:, :, 0] - lam * p[:, :, 1]).astype(v.dtype)
        return jnp.einsum('bhqk,bkhd->bqhd', a, v)

    o = lax.map(block, qb)
    return jnp.moveaxis(o, 0, 1).reshape(b, tq, ATT_HEADS, V_DIM)

def centred_dwconv(x, w, bias):
    pad = CONV_W // 2
    y = lax.conv_general_dilated(x, w[:, None, :], window_strides=(1,), padding=[(pad, pad)],
                                 dimension_numbers=('NWC', 'WIO', 'NWC'),
                                 feature_group_count=x.shape[-1])
    return y + bias

def ssd_chunked(x, dt, a, bm, cm, h0):
    b, l, h, p = x.shape
    n = bm.shape[-1]
    nc = l // CHUNK
    xd = (x * dt[..., None]).reshape(b, nc, CHUNK, h, p)
    la = (dt * a).reshape(b, nc, CHUNK, h)
    bc = bm.reshape(b, nc, CHUNK, h, n)
    cc = cm.reshape(b, nc, CHUNK, h, n)
    cum = jnp.cumsum(la, axis=2)
    causal = jnp.tril(jnp.ones((CHUNK, CHUNK), dtype=bool))
    seg = cum[:, :, :, None, :] - cum[:, :, None, :, :]
    decay_ij = jnp.exp(jnp.where(causal[None, None, :, :, None], seg, -jnp.inf))
    scores = jnp.einsum('bcihn,bcjhn->bcijh', cc, bc) * decay_ij
    y_diag = jnp.einsum('bcijh,bcjhp->bcihp', scores, xd)
    to_end = jnp.exp(cum[:, :, -1:, :] - cum)
    chunk_states = jnp.einsum('bclhn,bclh,bclhp->bchpn', bc, to_end, xd)
    chunk_decay = jnp.exp(cum[:, :, -1, :])

    def step(state, inp):
        dec, st = inp
        return state * dec[:, :, None, None] + st, state

    final, prev = lax.scan(step, h0, (jnp.moveaxis(chunk_decay, 1, 0), jnp.moveaxis(chunk_states, 1, 0)))
    prev = jnp.moveaxis(prev, 0, 1)
    y_off = jnp.einsum('bclhn,bchpn->bclhp', cc, prev) * jnp.exp(cum)[..., None]
    return (y_diag + y_off).reshape(b, l, h, p), final

def bidir_ssd(xbc_raw, z, dt_raw, lw, h0f, h0b):
    b, l, _ = xbc_raw.shape
    xbc = jax.nn.silu(centred_dwconv(xbc_raw, lw['conv_w'], lw['conv_b']))
    xs, bm, cm = jnp.split(xbc, [D_SSM, D_SSM + SSM_GROUPS * D_STATE], axis=-1)
    xs = xs.reshape(b, l, SSM_HEADS, SSM_HEADDIM)
    rep = SSM_HEADS // SSM_GROUPS
    bm = jnp.repeat(bm.reshape(b, l, SSM_GROUPS, D_STATE), rep, axis=2)
    cm = jnp.repeat(cm.reshape(b, l, SSM_GROUPS, D_STATE), rep, axis=2)
    dtf_raw, dtb_raw = jnp.split(dt_raw, 2, axis=-1)
    dt_f = jax.nn.softplus(dtf_raw + lw['dt_bias_fwd'])
    dt_b = jax.nn.softplus(dtb_raw + lw['dt_bias_bwd'])
    y_f, hf = ssd_chunked(xs, dt_f, -jnp.exp(lw['a_log_fwd']), bm, cm, h0f)
    flip = lambda t: jnp.flip(t, axis=1)
    y_b, hb = ssd_chunked(flip(xs), flip(dt_b), -jnp.exp(lw['a_log_bwd']), flip(bm), flip(cm), h0b)
    y = (y_f + flip(y_b) + xs * lw['ssm_d'][:, None]).reshape(b, l, D_SSM)
    y = rms_norm(y * jax.nn.silu(z), lw['ssm_norm_g'])
    return y, hf, hb

def token_mixer(h, lw, layer, rope_pos, ctx_k, ctx_v, h0f, h0b):
    b, t, _ = h.shape
    splits = [D_QK, 2 * D_QK, 2 * D_QK + D_ATT, 2 * D_QK + D_ATT + D_SSM,
              2 * D_QK + D_ATT + D_SSM + XBC_DIM]
    q, k, v, z, xbc, dt_raw = jnp.split(h @ lw['w_in'], splits, axis=-1)
    q = q.reshape(b, t, ATT_HEADS, 2, QK_DIM)
    k = k.reshape(b, t, ATT_HEADS, 2, QK_DIM)
    v = v.reshape(b, t, ATT_HEADS, V_DIM)
    if rope_pos is None:
        k_all, v_all = k, v
    else:
        q = axial_rope(q, *rope_pos)
        k = axial_rope(k, *rope_pos)
        k_all = jnp.concatenate([k, ctx_k], axis=1)
        v_all = jnp.concatenate([v, ctx_v], axis=1)
    lam0 = lambda_init(layer)
    lam = (jnp.exp(jnp.sum(lw['lambda_q1'] * lw['lambda_k1']).astype(jnp.float32))
           - jnp.exp(jnp.sum(lw['lambda_q2'] * lw['lambda_k2']).astype(jnp.float32)) + lam0)
    o = diff_attention(q, k_all, v_all, lam)
    att = (rms_norm(o, lw['attn_subln_g']) * (1.0 - lam0)).reshape(b, t, D_ATT)
    ssm, hf, hb = bidir_ssd(xbc, z, dt_raw, lw, h0f, h0b)
    out = jnp.concatenate([att, ssm], axis=-1) @ lw['w_out']
    return out, k, v, hf, hb

def hier_moe(h, lw):
    shape = h.shape
    hf = h.reshape(-1, D_MODEL)
    n = hf.shape[0]
    g_logits = (hf @ lw['w_group_router'] + lw['b_group_router']).astype(jnp.float32)
    g_prob = jax.nn.softmax(g_logits, axis=-1)
    g_idx = jnp.argmax(g_logits, axis=-1)
    p_g = jnp.take_along_axis(g_prob, g_idx[:, None], axis=-1)
    e_logits = (hf @ lw['w_expert_router'] + lw['b_expert_router']).astype(jnp.float32)
    e_logits = e_logits.reshape(n, N_GROUPS, EXPERTS_PER_GROUP)
    e_sel = jnp.take_along_axis(e_logits, g_idx[:, None, None], axis=1)[:, 0]
    top_l, top_i = lax.top_k(e_sel, TOP_K_IN_GROUP)
    weights = p_g * jax.nn.softmax(top_l, axis=-1)
    expert_ids = g_idx[:, None] * EXPERTS_PER_GROUP + top_i
    combine = jnp.sum(jax.nn.one_hot(expert_ids, N_EXPERTS, dtype=jnp.float32) * weights[..., None], axis=1)
    hidden = (jax.nn.silu(jnp.einsum('nd,edf->nef', hf, lw['w_exp_gate']))
              * jnp.einsum('nd,edf->nef', hf, lw['w_exp_up']))
    y = jnp.einsum('nef,efd->nd', hidden * combine.astype(hf.dtype)[..., None], lw['w_exp_down'])
    return y.reshape(shape)

def trunk_layer(x, mods, lw, layer, rope_pos, ctx_k, ctx_v, h0f, h0b):
    shift1, scale1, gate1, shift2, scale2, gate2 = mods
    h = rms_norm(x, lw['norm_mix_g']) * (1 + scale1) + shift1
    mix, k, v, hf, hb = token_mixer(h, lw, layer, rope_pos, ctx_k, ctx_v, h0f, h0b)
    x = x + gate1 * mix
    h = rms_norm(x, lw['norm_ffn_g']) * (1 + scale2) + shift2
    x = x + gate2 * hier_moe(h, lw)
    return x, k, v, hf, hb

def setup_inputs(seed: int = 0) -> dict:
    key = jax.random.key(seed)
    ks = iter(jax.random.split(key, 48))
    nrm = lambda shape, scale: jax.random.normal(next(ks), shape, jnp.float32) * scale
    gain = lambda shape: 1.0 + nrm(shape, 0.02)

    def a_log(shape):
        return jnp.log(jax.random.uniform(next(ks), shape, jnp.float32, minval=1.0, maxval=16.0))

    def dt_bias(shape):
        dt = jnp.exp(jax.random.uniform(next(ks), shape, jnp.float32,
                                        minval=math.log(1e-3), maxval=math.log(1e-1)))
        return dt + jnp.log(-jnp.expm1(-dt))

    return {
        "x_prompt": nrm((BATCH, SEQ, D_MODEL), 1.0),
        "x_sample": nrm((DEC_BATCH, DEC_SEQ, D_MODEL), 1.0),
        "cache_k": nrm((DEC_BATCH, DEPTH, PAST_LEN, ATT_HEADS, 2, QK_DIM), 1.0),
        "cache_v": nrm((DEC_BATCH, DEPTH, PAST_LEN, ATT_HEADS, V_DIM), 1.0),
        "state_ssm_fwd": nrm((DEC_BATCH, DEPTH, SSM_HEADS, SSM_HEADDIM, D_STATE), 0.5),
        "state_ssm_bwd": nrm((DEC_BATCH, DEPTH, SSM_HEADS, SSM_HEADDIM, D_STATE), 0.5),
        "c": nrm((DEC_BATCH, D_MODEL), 1.0),
        "c_ctx": nrm((D_MODEL,), 1.0),
        "w_ada": nrm((DEPTH, D_MODEL, 6 * D_MODEL), 0.5 * D_MODEL ** -0.5),
        "b_ada": nrm((DEPTH, 6 * D_MODEL), 0.02),
        "norm_mix_g": gain((DEPTH, D_MODEL)),
        "w_in": nrm((DEPTH, D_MODEL, IN_COLS), D_MODEL ** -0.5),
        "w_out": nrm((DEPTH, MIX_W, D_MODEL), MIX_W ** -0.5),
        "lambda_q1": nrm((DEPTH, QK_DIM), 0.1),
        "lambda_k1": nrm((DEPTH, QK_DIM), 0.1),
        "lambda_q2": nrm((DEPTH, QK_DIM), 0.1),
        "lambda_k2": nrm((DEPTH, QK_DIM), 0.1),
        "attn_subln_g": gain((DEPTH, V_DIM)),
        "conv_w": nrm((DEPTH, CONV_W, XBC_DIM), CONV_W ** -0.5),
        "conv_b": nrm((DEPTH, XBC_DIM), 0.02),
        "a_log_fwd": a_log((DEPTH, SSM_HEADS)),
        "a_log_bwd": a_log((DEPTH, SSM_HEADS)),
        "dt_bias_fwd": dt_bias((DEPTH, SSM_HEADS)),
        "dt_bias_bwd": dt_bias((DEPTH, SSM_HEADS)),
        "ssm_d": gain((DEPTH, SSM_HEADS)),
        "ssm_norm_g": gain((DEPTH, D_SSM)),
        "norm_ffn_g": gain((DEPTH, D_MODEL)),
        "w_group_router": nrm((DEPTH, D_MODEL, N_GROUPS), D_MODEL ** -0.5),
        "b_group_router": nrm((DEPTH, N_GROUPS), 0.01),
        "w_expert_router": nrm((DEPTH, D_MODEL, N_EXPERTS), D_MODEL ** -0.5),
        "b_expert_router": nrm((DEPTH, N_EXPERTS), 0.01),
        "w_exp_gate": nrm((DEPTH, N_EXPERTS, D_MODEL, EXPERT_FF), D_MODEL ** -0.5),
        "w_exp_up": nrm((DEPTH, N_EXPERTS, D_MODEL, EXPERT_FF), D_MODEL ** -0.5),
        "w_exp_down": nrm((DEPTH, N_EXPERTS, EXPERT_FF, D_MODEL), EXPERT_FF ** -0.5),
        "final_norm_g": gain((D_MODEL,)),
    }

def reference(x_prompt, x_sample, cache_k, cache_v, state_ssm_fwd, state_ssm_bwd, c, c_ctx,
              w_ada, b_ada, norm_mix_g, w_in, w_out, lambda_q1, lambda_k1, lambda_q2, lambda_k2,
              attn_subln_g, conv_w, conv_b, a_log_fwd, a_log_bwd, dt_bias_fwd, dt_bias_bwd,
              ssm_d, ssm_norm_g, norm_ffn_g, w_group_router, b_group_router, w_expert_router,
              b_expert_router, w_exp_gate, w_exp_up, w_exp_down, final_norm_g):
    rows = x_sample.shape[1] // GRID_W
    row_ids = jnp.repeat(jnp.arange(rows, dtype=jnp.float32), GRID_W)
    col_ids = jnp.tile(jnp.arange(GRID_W, dtype=jnp.float32), rows)

    xp, xs = x_prompt, x_sample
    bp = x_prompt.shape[0]
    new_k, new_v, new_hf, new_hb = [], [], [], []
    for l in range(DEPTH):
        lw = dict(norm_mix_g=norm_mix_g[l], w_in=w_in[l], w_out=w_out[l],
                  lambda_q1=lambda_q1[l], lambda_k1=lambda_k1[l],
                  lambda_q2=lambda_q2[l], lambda_k2=lambda_k2[l], attn_subln_g=attn_subln_g[l],
                  conv_w=conv_w[l], conv_b=conv_b[l], a_log_fwd=a_log_fwd[l], a_log_bwd=a_log_bwd[l],
                  dt_bias_fwd=dt_bias_fwd[l], dt_bias_bwd=dt_bias_bwd[l], ssm_d=ssm_d[l],
                  ssm_norm_g=ssm_norm_g[l], norm_ffn_g=norm_ffn_g[l],
                  w_group_router=w_group_router[l], b_group_router=b_group_router[l],
                  w_expert_router=w_expert_router[l], b_expert_router=b_expert_router[l],
                  w_exp_gate=w_exp_gate[l], w_exp_up=w_exp_up[l], w_exp_down=w_exp_down[l])
        zeros_state = jnp.zeros((bp, SSM_HEADS, SSM_HEADDIM, D_STATE), xp.dtype)
        mods_ctx = ada_mod(c_ctx[None], w_ada[l], b_ada[l])
        xp, ck, cv, hf, hb = trunk_layer(xp, mods_ctx, lw, l, None, None, None, zeros_state, zeros_state)
        new_k.append(ck)
        new_v.append(cv)
        new_hf.append(hf)
        new_hb.append(hb)
        mods_lat = ada_mod(c, w_ada[l], b_ada[l])
        xs, _, _, _, _ = trunk_layer(xs, mods_lat, lw, l, (row_ids, col_ids), cache_k[:, l], cache_v[:, l],
                                     state_ssm_fwd[:, l], state_ssm_bwd[:, l])
    y_prompt = rms_norm(xp, final_norm_g)
    y_sample = rms_norm(xs, final_norm_g)
    return (y_prompt, y_sample, jnp.stack(new_k, axis=1), jnp.stack(new_v, axis=1),
            jnp.stack(new_hf, axis=1), jnp.stack(new_hb, axis=1))


_drawn_inputs = setup_inputs


def setup_inputs(seed=0):
    import zlib

    import numpy as np

    out = dict(_drawn_inputs(seed))
    spreads = {}
    factors = {'cache_k': 5.117,
     'cache_v': 4.372,
     'lambda_q1': 7.356,
     'lambda_k1': 8.0,
     'lambda_q2': 7.281,
     'lambda_k2': 8.0,
     'attn_subln_g': 8.0,
     'ssm_d': 8.0,
     'ssm_norm_g': 8.0,
     'norm_ffn_g': 6.301,
     'b_group_router': 8.0,
     'b_expert_router': 8.0,
     'final_norm_g': 2.849}
    for name, (base, spread) in spreads.items():
        noise = np.random.default_rng([zlib.crc32(name.encode()), seed]).standard_normal(out[name].shape)
        drawn = base * np.exp(spread * noise) if base else spread * noise
        out[name] = __import__('jax').numpy.asarray(drawn.astype(out[name].dtype))
    for name, factor in factors.items():
        out[name] = (out[name] * factor).astype(out[name].dtype)
    return out
```

```python
import math
from contextlib import ExitStack

import numpy as np

import concourse.bass as bass
from concourse import mybir

P = 128
D = 1024
KT = D // P
TILES = 9
STILES = 8
HEADS = 4
QKD = 64
DQK = 512
DATT = 512
DSSM = 512
SH = 8
SG = 2
HG = SH // SG
XBC = 1024
NXBC = XBC // P
IN_COLS = 2 * DQK + DATT + DSSM + XBC + 2 * SH
CONV = 5
NG = 4
EPG = 4
NE = NG * EPG
FF = 256
EPS = 1e-6
LAM0 = 0.8 - 0.6 * math.exp(-0.0)
SCALE = QKD ** -0.5
BLOCKS = 2 * TILES + NE - 1
SLOTS = BLOCKS * P
CIN = 2 + P + 2 + STILES * P + 2
COUT = CIN - 4
SHIFT1, SCALE1, GATE1, SHIFT2, SCALE2, GATE2 = range(6)

ALU = mybir.AluOpType
ACT = mybir.ActivationFunctionType
F32 = mybir.dt.float32
I32 = mybir.dt.int32
U32 = mybir.dt.uint32
AX = mybir.AxisListType.X


class Scope:

    def __init__(self, nc, ctx, tag):
        self.nc, self.ctx, self.tag, self.sems = nc, ctx, tag, []
        ctx.callback(self.close)

    def sb(self, name, shape, dt=F32, side=None):
        return self.ctx.enter_context(self.nc.sbuf_tensor(f"{self.tag}_{name}", shape, dt, side=side))

    def ps(self, name, cols=512):
        return self.ctx.enter_context(self.nc.psum_tensor(f"{self.tag}_{name}_ps", [P, cols], F32))

    def sem(self, name):
        self.sems.append(self.nc.alloc_semaphore(name=f"{self.tag}_{name}"))
        return self.sems[-1]

    def close(self):
        if self.sems:
            self.nc.clear_and_free_semaphores(self.sems)
            self.nc.all_engine_barrier()


class Step:

    def __init__(self, i, c):
        self.i, self.c = i, c
        self.buf = c % 2
        self.n = i * 2 + c if not isinstance(i, int) else 2 * i + c
        self.nth = i + c // 2

    def next(self):
        return Step(self.i, self.c + 1)


def bcast(ap, n, axis):
    shape = list(ap.shape)
    shape.insert(axis, n)
    return ap.unsqueeze(axis).to_broadcast(shape)


def row_bcast(row, n=P):
    return row.unsqueeze(0).to_broadcast([n, row.shape[0]])


def ada_stage(nc, I, C, W, M):
    NB, W_COLS = 3, 512
    CB = 6 * D // W_COLS
    w_ada = I["w_ada"][0].rearrange("(p j) n -> p j n", j=KT)
    with ExitStack() as ctx:
        s = Scope(nc, ctx, "ada")
        raw, cond = s.sb("raw", [P, 2, KT]), s.sb("cond", [P, KT, 2])
        w = s.sb("w", [P, NB, KT, W_COLS])
        rows = s.sb("rows", [2, 6 * D])
        acc = [s.ps(f"acc{u}") for u in range(NB)]
        in_sem, w_in_sems = s.sem("cond_in"), [s.sem(f"w_in{u}") for u in range(NB)]
        silu_done = s.sem("silu_done")
        mm_done, row_done, stored = s.sem("mm_done"), s.sem("row_done"), s.sem("stored")
        block = ctx.enter_context(nc.Block())

        @block.sync
        def _(sp):
            sp.dma_start(raw[:, 0], I["c_ctx"].rearrange("(p j) -> p j", j=KT)).then_inc(in_sem, 16)
            sp.dma_start(raw[:, 1], I["c"][0].rearrange("(p j) -> p j", j=KT)).then_inc(in_sem, 16)
            sp.dma_start(rows[:], row_bcast(I["b_ada"][0], 2)).then_inc(in_sem, 16)
            with sp.Fori(0, CB // NB) as i:
                for u in range(NB):
                    sp.wait_ge(mm_done, i * NB + (u + 1))
                    sp.dma_start(w[:, u], w_ada[:, :, bass.ds((i * NB + u) * W_COLS, W_COLS)]).then_inc(w_in_sems[u], 16)
            sp.wait_ge(row_done, CB + NB)
            sp.dma_start(M["mods"], rows[:]).then_inc(stored, 16)
            sp.wait_ge(stored, 16)

        @block.gpsimd
        def _(pool):
            for k in range(KT):
                pool.dma_start(W["w_in"][:, k, :], I["w_in"][0, k * P:(k + 1) * P, :]).then_inc(W["w_in_sem"], 16)

        @block.scalar
        def _(act):
            act.wait_ge(in_sem, 48)
            act.activation(cond[:].rearrange("p k c -> p c k"), raw[:], ACT.Silu).then_inc(silu_done, 1)

        @block.tensor
        def _(pe):
            pe.sem_inc(mm_done, NB)
            pe.wait_ge(silu_done, 1)
            with pe.Fori(0, CB // NB) as i:
                for u in range(NB):
                    pe.wait_ge(w_in_sems[u], i * 16 + 16)
                    pe.wait_ge(row_done, i * NB + (u + 1))
                    for k in range(KT):
                        mm = pe.matmul(acc[u][0:2, :], cond[:, k, :], w[:, u, k, :], start=(k == 0), stop=(k == KT - 1))
                    mm.then_inc(mm_done, 1)

        @block.vector
        def _(dve):
            dve.wait_ge(in_sem, 48)
            dve.sem_inc(row_done, NB)
            with dve.Fori(0, CB // NB) as i:
                for u in range(NB):
                    dve.wait_ge(mm_done, i * NB + (u + 1 + NB))
                    cols = rows[:, bass.ds((i * NB + u) * W_COLS, W_COLS)]
                    dve.tensor_tensor(cols, acc[u][0:2, :], cols, ALU.add).then_inc(row_done, 1)


def projection_stage(nc, I, C, W, M):
    with ExitStack() as ctx:
        s = Scope(nc, ctx, "proj")
        amul, aadd = s.sb("amul", [P, 2, D]), s.sb("aadd", [P, 2, D])
        rope = s.sb("rope", [P, 2, 2, QKD])
        x = s.sb("x", [P, 2, D])
        h = s.sb("h", [P, 2, D])
        gain = h[:, 0]
        hT = s.sb("hT", [P, 2, KT, P])
        stage = s.sb("stage", [P, 3, 512])
        q_out, k_rot = s.sb("q_out", [P, 512]), s.sb("k_rot", [P, 512])
        swap = W["kT"][:, :, TILES * P:(TILES + 1) * P]
        ssq, std, rstd = s.sb("ssq", [P, 2]), s.sb("std", [P, 2]), s.sb("rstd", [P, 2])
        epsc = s.sb("epsc", [P, 1])
        turned = s.ps("turned", 1024)
        acc = [s.ps(f"acc{u}") for u in range(4)]
        k_turned = s.ps("k_turned")
        dt_acc = s.ps("dt_acc")
        w_in = W["w_in"]

        mods_in, x_in, rope_in = s.sem("mods_in"), [s.sem(f"x_in{u}") for u in range(2)], [s.sem(f"rope_in{u}") for u in range(2)]
        mods_done, std_done, h_done = s.sem("mods_done"), s.sem("std_done"), s.sem("h_done")
        turn_done, hT_done = s.sem("turn_done"), s.sem("hT_done")
        acc_done = [s.sem(f"acc_done{u}") for u in range(4)]
        acc_read = [s.sem(f"acc_read{u}") for u in range(4)]
        dt_done, dt_read = s.sem("dt_done"), s.sem("dt_read")
        q_rot_done, q_turn_done, qT_done = s.sem("q_rot_done"), s.sem("q_turn_done"), s.sem("qT_done")
        k_rot_done, k_turn_done, kT_done = s.sem("k_rot_done"), s.sem("k_turn_done"), s.sem("kT_done")
        staged, stored = [s.sem(f"staged{u}") for u in range(3)], [s.sem(f"stored{u}") for u in range(3)]
        ctx_in, ctx_kin, new_stored = s.sem("ctx_in"), s.sem("ctx_kin"), [s.sem(f"new_stored{u}") for u in range(2)]
        block = ctx.enter_context(nc.Block())
        qT, kT, v_tok, dt_tok = W["qT"], W["kT"], W["v_tok"], W["dt_tok"]
        Q, K, V, Z, X0, X1 = range(6)
        BANK = {Q: 0, K: 1, V: 2, Z: 3, X0: 0, X1: 1}

        @block.sync
        def _(sp):
            for cond in range(2):
                sp.dma_start(amul[:, cond], row_bcast(M["mods"][cond, SCALE1 * D:(SCALE1 + 1) * D])).then_inc(mods_in, 16)
                sp.dma_start(aadd[:, cond], row_bcast(M["mods"][cond, SHIFT1 * D:(SHIFT1 + 1) * D])).then_inc(mods_in, 16)
            sp.dma_start(gain, row_bcast(I["norm_mix_g"][0])).then_inc(mods_in, 16)

            def load(t, src):
                sp.wait_ge(h_done, t.n + 1)
                sp.dma_start(x[:, t.buf], src).then_inc(x_in[t.buf], 16)
                sp.wait_ge(k_rot_done, t.n + 1)
                sp.dma_start(rope[:, t.buf], I["rope"][t.n]).then_inc(rope_in[t.buf], 16)

            def sample_rows(t):
                return I["x_sample"][0, bass.ds((t.n - 1) * P, P), :]

            def store(t):
                for u, dst in ((0, M["z"][bass.ds(t.n * P, P), :]), (1, M["xbc"][bass.ds(t.n * P, P), 0:512]),
                               (2, M["xbc"][bass.ds(t.n * P, P), 512:1024])):
                    sp.wait_ge(staged[u], t.n + 2)
                    sp.dma_start(dst, stage[:, u]).then_inc(stored[u], 16)

            load(Step(0, 0), I["x_prompt"][0])
            load(Step(0, 1), sample_rows(Step(0, 1)))
            load(Step(0, 2), sample_rows(Step(0, 2)))
            sp.wait_ge(k_rot_done, 3)
            sp.dma_start(I["new_k"][0, 0].rearrange("t h m d -> t (h m d)"), k_rot[:]).then_inc(new_stored[0], 16)
            sp.wait_ge(staged[0], 2)
            sp.dma_start(I["new_v"][0, 0].rearrange("t h d -> t (h d)"), v_tok[:, 0, :]).then_inc(new_stored[1], 16)
            store(Step(0, 0))
            with sp.Fori(0, STILES // 2 - 1) as i:
                for c in (1, 2):
                    load(Step(i, c + 2), sample_rows(Step(i, c + 2)))
                    store(Step(i, c))
            store(Step(0, TILES - 2))
            store(Step(0, TILES - 1))
            sp.wait_ge(kT_done, TILES + 1)
            sp.dma_start(k_rot[:], I["cache_k"][0, 0].rearrange("t h m d -> t (h m d)")).then_inc(ctx_kin, 16)
            sp.dma_start(v_tok[:, TILES, :], I["cache_v"][0, 0].rearrange("t h d -> t (h d)")).then_inc(ctx_in, 16)
            sp.wait_ge(ctx_in, 16)
            for u in range(3):
                sp.wait_ge(stored[u], 16 * (TILES + 1))
            for u in range(2):
                sp.wait_ge(new_stored[u], 16)

        @block.scalar
        def _(act):
            for u in range(3):
                act.sem_inc(staged[u], 1)
                act.sem_inc(stored[u], 16)
            act.sem_inc(acc_read[2], 1)
            act.sem_inc(hT_done, 1)

            def norm(t):
                act.wait_ge(x_in[t.buf], t.nth * 16 + 16)
                act.wait_ge(turn_done, t.n + 1)
                act.activation(h[:, t.buf], x[:, t.buf], ACT.Square, accum_out=ssq[:, t.buf:t.buf + 1])
                act.drain()
                act.activation(std[:, t.buf:t.buf + 1], ssq[:, t.buf:t.buf + 1], ACT.Sqrt, bias=epsc[:, 0:1],
                               scale=1.0 / D).then_inc(std_done, 1)

            def turn_out(t):
                act.wait_ge(turn_done, t.n + 3)
                act.wait_ge(dt_done, t.n + 1)
                act.copy(hT[:, t.buf].rearrange("p k t -> p (k t)"), turned[:]).then_inc(hT_done, 1)

            def out(t):
                act.wait_ge(acc_done[2], t.n + 1)
                act.copy(v_tok[:, t.n, :], acc[2][:]).then_inc(acc_read[2], 1)
                act.wait_ge(acc_done[3], t.n + 1)
                act.wait_ge(stored[0], t.n * 16 + 16)
                act.copy(stage[:, 0], acc[3][:]).then_inc(staged[0], 1)
                act.wait_ge(acc_done[0], t.n * 2 + 2)
                act.wait_ge(stored[1], t.n * 16 + 16)
                act.copy(stage[:, 1], acc[0][:]).then_inc(staged[1], 1)
                act.wait_ge(acc_done[1], t.n * 2 + 2)
                act.wait_ge(stored[2], t.n * 16 + 16)
                act.copy(stage[:, 2], acc[1][:]).then_inc(staged[2], 1)

            act.wait_ge(mods_done, 1)
            norm(Step(0, 0))
            turn_out(Step(0, 0))
            norm(Step(0, 1))
            turn_out(Step(0, 1))
            out(Step(0, 0))
            with act.Fori(0, STILES // 2 - 1) as i:
                for c in (1, 2):
                    norm(Step(i, c + 1))
                    turn_out(Step(i, c + 1))
                    out(Step(i, c))
            norm(Step(0, TILES - 1))
            turn_out(Step(0, TILES - 1))
            out(Step(0, TILES - 2))
            out(Step(0, TILES - 1))

        @block.vector
        def _(dve):
            dve.memset(epsc[:], EPS)
            dve.wait_ge(mods_in, 80)
            for cond in range(2):
                op = dve.scalar_tensor_tensor(out=amul[:, cond], in0=amul[:, cond], scalar=1.0, in1=gain,
                                              op0=ALU.add, op1=ALU.mult)
            op.then_inc(mods_done, 1)
            dve.wait_ge(mods_done, 1)
            dve.sem_inc(h_done, 2)
            dve.sem_inc(k_rot_done, 2)
            dve.sem_inc(kT_done, 1)
            dve.sem_inc(q_rot_done, 1)
            dve.sem_inc(dt_read, 1)

            def norm(t, cond):
                dve.wait_ge(std_done, t.n + 1)
                r = rstd[:, t.buf:t.buf + 1]
                dve.reciprocal(r, std[:, t.buf:t.buf + 1])
                dve.drain()
                dve.scalar_tensor_tensor(out=h[:, t.buf], in0=x[:, t.buf], scalar=r, in1=amul[:, cond],
                                         op0=ALU.mult, op1=ALU.mult)
                dve.drain()
                dve.tensor_tensor(h[:, t.buf], h[:, t.buf], aadd[:, cond], ALU.add).then_inc(h_done, 1)

            def rotate(dst, src, t, done):
                cos = bcast(rope[:, t.buf, 0, :], 8, 1)
                sin = rope[:, t.buf, 1, :].rearrange("p (a s f) -> p a s f", a=2, s=2)
                v = src.rearrange("p (h m a s f) -> p h m a s f", h=HEADS, m=2, a=2, s=2)
                w = swap.rearrange("p h (m a s f) -> p h m a s f", m=2, a=2, s=2)
                for half in range(2):
                    for axis in range(2):
                        dve.tensor_tensor(w[:, :, :, axis, half, :], v[:, :, :, axis, 1 - half, :],
                                          bcast(bcast(sin[:, axis, half, :], 2, 1), HEADS, 1), ALU.mult)
                dve.tensor_tensor(dst.rearrange("p (g f) -> p g f", g=8), src.rearrange("p (g f) -> p g f", g=8),
                                  cos, ALU.mult)
                dve.drain()
                dve.tensor_tensor(dst.rearrange("p (h d) -> p h d", h=HEADS), dst.rearrange("p (h d) -> p h d", h=HEADS), swap,
                                  ALU.add).then_inc(done, 1)
                dve.drain()

            def out(t):
                dve.wait_ge(rope_in[t.buf], t.nth * 16 + 16)
                dve.wait_ge(acc_done[0], t.n * 2 + 1)
                dve.wait_ge(q_turn_done, t.n + 1)
                rotate(q_out[:], acc[0][:], t, q_rot_done)
                dve.wait_ge(q_turn_done, t.n + 2)
                dve.tensor_copy(qT[:, :, bass.ds(t.n * P, P)], k_turned[:].rearrange("p (h t) -> p h t", h=HEADS)).then_inc(qT_done, 1)
                dve.wait_ge(acc_done[1], t.n * 2 + 1)
                dve.wait_ge(k_turn_done, t.n + 1)
                rotate(k_rot[:], acc[1][:], t, k_rot_done)
                dve.wait_ge(k_turn_done, t.n + 2)
                dve.tensor_copy(kT[:, :, bass.ds(t.n * P, P)], k_turned[:].rearrange("p (h t) -> p h t", h=HEADS)).then_inc(kT_done, 1)
                dve.wait_ge(dt_done, t.n + 3)
                dve.tensor_copy(dt_tok[:, t.n, :], dt_acc[:, 0:2 * SH]).then_inc(dt_read, 1)

            norm(Step(0, 0), 0)
            norm(Step(0, 1), 1)
            out(Step(0, 0))
            dve.wait_ge(new_stored[0], 16)
            with dve.Fori(0, STILES // 2 - 1) as i:
                for c in (1, 2):
                    norm(Step(i, c + 1), 1)
                    out(Step(i, c))
            norm(Step(0, TILES - 1), 1)
            out(Step(0, TILES - 2))
            out(Step(0, TILES - 1))
            dve.wait_ge(k_turn_done, TILES + 2)
            dve.tensor_copy(kT[:, :, TILES * P:(TILES + 1) * P], k_turned[:].rearrange("p (h t) -> p h t", h=HEADS)).then_inc(kT_done, 1)

        @block.tensor
        def _(pe):
            ident = C["ident"]
            pe.sem_inc(turn_done, 2)
            pe.sem_inc(dt_done, 2)
            pe.sem_inc(k_turn_done, 1)
            pe.sem_inc(q_turn_done, 1)
            pe.wait_ge(W["w_in_sem"], 16 * KT)

            def turn(t):
                pe.wait_ge(h_done, t.n + 3)
                pe.wait_ge(hT_done, t.n + 1)
                for k in range(KT):
                    mm = pe.transpose(turned[:, k * P:(k + 1) * P], h[:, t.buf, k * P:(k + 1) * P], ident[:])
                mm.then_inc(turn_done, 1)

            def product(t, b):
                for k in range(KT):
                    mm = pe.matmul(acc[BANK[b]][:], hT[:, t.buf, k, :], w_in[:, k, b * 512:(b + 1) * 512],
                                   start=(k == 0), stop=(k == KT - 1))
                mm.then_inc(acc_done[BANK[b]], 1)

            def products(t, turn_next):
                pe.wait_ge(hT_done, t.n + 2)
                pe.wait_ge(staged[1], t.n + 1)
                product(t, Q)
                pe.wait_ge(staged[2], t.n + 1)
                product(t, K)
                if turn_next:
                    turn(t.next())
                pe.wait_ge(acc_read[2], t.n + 1)
                product(t, V)
                pe.wait_ge(staged[0], t.n + 1)
                product(t, Z)
                pe.wait_ge(q_rot_done, t.n + 2)
                pe.wait_ge(kT_done, t.n + 1)
                for hd in range(HEADS):
                    mm = pe.transpose(k_turned[:, hd * P:(hd + 1) * P], q_out[:, hd * P:(hd + 1) * P], ident[:])
                mm.then_inc(q_turn_done, 1)
                product(t, X0)
                pe.wait_ge(k_rot_done, t.n + 3)
                pe.wait_ge(qT_done, t.n + 1)
                for hd in range(HEADS):
                    mm = pe.transpose(k_turned[:, hd * P:(hd + 1) * P], k_rot[:, hd * P:(hd + 1) * P], ident[:])
                mm.then_inc(k_turn_done, 1)
                product(t, X1)
                pe.wait_ge(dt_read, t.n + 1)
                for k in range(KT):
                    mm = pe.matmul(dt_acc[:, 0:2 * SH], hT[:, t.buf, k, :], w_in[:, k, 3072:IN_COLS],
                                   start=(k == 0), stop=(k == KT - 1))
                mm.then_inc(dt_done, 1)

            turn(Step(0, 0))
            products(Step(0, 0), True)
            with pe.Fori(0, STILES // 2 - 1) as i:
                for c in (1, 2):
                    products(Step(i, c), True)
            products(Step(0, TILES - 2), True)
            products(Step(0, TILES - 1), False)
            pe.wait_ge(ctx_kin, 16)
            pe.wait_ge(kT_done, TILES + 1)
            for hd in range(HEADS):
                mm = pe.transpose(k_turned[:, hd * P:(hd + 1) * P], k_rot[:, hd * P:(hd + 1) * P], ident[:])
            mm.then_inc(k_turn_done, 1)


def conv_stage(nc, I, C, W, M):
    w = W
    with ExitStack() as ctx:
        s = Scope(nc, ctx, "conv")
        dt_bias, a_neg = s.sb("dt_bias", [P, 2 * SH]), s.sb("a_neg", [P, 2 * SH])
        d_row = s.sb("d_row", [P, SH])
        taps_row = s.sb("taps_row", [CONV + 1, XBC])
        taps = s.sb("taps", [P, NXBC, CONV + 1])
        ones = s.sb("ones", [P, P])
        t1, t2, t3, t4 = (s.sb(f"t{i}", [P, TILES, 2 * SH]) for i in range(4))
        la = s.sb("la", [P, TILES, 2 * SH])
        raw = s.sb("raw", [P, 2, TILES, P])
        xin = s.sb("xin", [P, 2, CIN])
        acc = s.sb("acc", [P, COUT])
        smooth = s.sb("smooth", [P, 2, COUT])
        turned_in, turned_out = s.ps("turned_in", 1536), s.ps("turned_out", 1536)
        sums = s.ps("sums")
        small_in, raw_in = s.sem("small_in"), [s.sem(f"raw_in{u}") for u in range(2)]
        exp_done, ln_done, a_done, pre_done = s.sem("exp_done"), s.sem("ln_done"), s.sem("a_done"), s.sem("pre_done")
        la_done, sums_done, cum_done, expo_done = s.sem("la_done"), s.sem("sums_done"), s.sem("cum_done"), s.sem("expo_done")
        taps_turned, taps_done = s.sem("taps_turned"), s.sem("taps_done")
        cumT_turned, cumT_done = s.sem("cumT_turned"), s.sem("cumT_done")
        zeroed, turn_done, xin_done = s.sem("zeroed"), s.sem("turn_done"), s.sem("xin_done")
        acc_done, smooth_done, back_done, tok_done = s.sem("acc_done"), s.sem("smooth_done"), s.sem("back_done"), s.sem("tok_done")
        kept, skip_done = s.sem("kept"), s.sem("skip_done")
        block = ctx.enter_context(nc.Block())
        tok, xbcT, y_tok, dt_tok = w["tok"], w["xbcT"], w["y_tok"], w["dt_tok"]
        cum, tot, ecum, dte, dec, cumT = (w[k] for k in ("cum", "tot", "ecum", "dte", "dec", "cumT"))
        xbc_dram = M["xbc"].rearrange("(t p) c -> p t c", p=P)

        @block.sync
        def _(sp):
            for half, (bias, alog) in enumerate((("dt_bias_fwd", "a_log_fwd"), ("dt_bias_bwd", "a_log_bwd"))):
                sp.dma_start(dt_bias[:, half * SH:(half + 1) * SH], row_bcast(I[bias][0])).then_inc(small_in, 16)
                sp.dma_start(a_neg[:, half * SH:(half + 1) * SH], row_bcast(I[alog][0])).then_inc(small_in, 16)
            sp.dma_start(d_row[:], row_bcast(I["ssm_d"][0])).then_inc(small_in, 16)
            sp.dma_start(taps_row[0:CONV, :], I["conv_w"][0]).then_inc(small_in, 16)
            sp.dma_start(taps_row[CONV:CONV + 1, :], I["conv_b"]).then_inc(small_in, 16)
            with sp.Fori(0, NXBC // 2) as i:
                for u in range(2):
                    sp.wait_ge(turn_done, i * 2 + (u + 1))
                    sp.dma_start(raw[:, u], xbc_dram[:, :, bass.ds((i * 2 + u) * P, P)]).then_inc(raw_in[u], 16)

        @block.gpsimd
        def _(pool):
            pool.memset(ones[:], 1.0).then_inc(zeroed, 1)
            pool.memset(xin[:], 0.0).then_inc(zeroed, 1)
            pool.sem_inc(kept, 2 + 4)
            with pool.Fori(0, 2) as i:
                for u in range(2):
                    pool.wait_ge(smooth_done, i * 2 + (u + 7))
                    pool.tensor_copy(xbcT[:, i * 2 + u, :], smooth[:, u]).then_inc(kept, 1)
            pool.wait_ge(tok_done, NXBC + 1)
            xs = tok[:, :, 0:DSSM].rearrange("p t (h d) -> p t h d", h=SH)
            for t in range(3):
                r = slice(3 * t, 3 * t + 3)
                pool.tensor_tensor(y_tok[:, r].rearrange("p t (h d) -> p t h d", h=SH), xs[:, r],
                                   bcast(bcast(d_row[:], 64, 2), 3, 1), ALU.mult).then_inc(skip_done, 1)
            pool.wait_ge(skip_done, 3)

        @block.scalar
        def _(act):
            act.wait_ge(small_in, 16 * 7)
            act.activation(a_neg[:], a_neg[:], ACT.Exp).then_inc(a_done, 1)
            act.wait_ge(pre_done, 1)
            act.activation(t2[:], t2[:], ACT.Exp).then_inc(exp_done, 1)
            act.wait_ge(pre_done, 2)
            act.activation(t4[:], t3[:], ACT.Ln).then_inc(ln_done, 1)
            act.wait_ge(cum_done, 1)
            act.activation(ecum[:], cum[:], ACT.Exp)
            act.activation(dec[:], tot[:], ACT.Exp)
            act.activation(t1[:], t1[:], ACT.Exp).then_inc(expo_done, 1)
            act.wait_ge(cumT_turned, 1)
            act.copy(cumT[:], turned_out[0:2 * SH, 0:TILES * P]).then_inc(cumT_done, 1)
            act.sem_inc(xin_done, 1)
            act.sem_inc(smooth_done, 2)
            act.sem_inc(tok_done, 1)
            act.wait_ge(zeroed, 2)
            with act.Fori(0, NXBC // 2) as i:
                for u in range(2):
                    act.wait_ge(turn_done, i * 2 + (u + 3))
                    act.wait_ge(acc_done, i * 2 + (u + 1))
                    act.copy(xin[:, u, 2:2 + P], turned_in[:, 0:P])
                    act.copy(xin[:, u, 4 + P:4 + TILES * P], turned_in[:, P:TILES * P]).then_inc(xin_done, 1)
                    act.wait_ge(acc_done, i * 2 + (u + 3))
                    act.wait_ge(back_done, i * 2 + (u + 1))
                    act.wait_ge(kept, i * 2 + (u + 1))
                    act.activation(smooth[:, u], acc[:], ACT.Silu).then_inc(smooth_done, 1)
                    act.wait_ge(back_done, i * 2 + (u + 3))
                    act.copy(tok[:, :, bass.ds((i * 2 + u) * P, P)],
                             turned_out[:, 0:TILES * P].rearrange("p (t c) -> p t c", t=TILES)).then_inc(tok_done, 1)

        @block.vector
        def _(dve):
            dve.sem_inc(acc_done, 2)
            dve.wait_ge(small_in, 16 * 7)
            dve.tensor_tensor(t1[:], dt_tok[:], bcast(dt_bias[:], TILES, 1), ALU.add)
            dve.drain()
            dve.tensor_scalar(t3[:], t1[:], -1.0, None, ALU.mult)
            dve.drain()
            dve.tensor_tensor(t2[:], t1[:], t3[:], ALU.min).then_inc(pre_done, 1)
            dve.wait_ge(exp_done, 1)
            dve.tensor_scalar(t3[:], t2[:], 1.0, None, ALU.add).then_inc(pre_done, 1)
            dve.tensor_scalar(t1[:], t1[:], 0.0, None, ALU.max)
            dve.wait_ge(ln_done, 1)
            dve.tensor_scalar(la[:], t3[:], 1.0, None, ALU.is_equal)
            dve.drain()
            dve.scalar_tensor_tensor(out=t3[:], in0=t3[:], scalar=-1.0, in1=la[:], op0=ALU.add, op1=ALU.add)
            dve.tensor_tensor(t4[:], t4[:], la[:], ALU.add)
            dve.drain()
            dve.reciprocal(t3[:], t3[:])
            dve.tensor_tensor(t4[:], t4[:], t2[:], ALU.mult)
            dve.drain()
            dve.tensor_tensor(t4[:], t4[:], t3[:], ALU.mult)
            dve.drain()
            dve.tensor_tensor(dt_tok[:], t1[:], t4[:], ALU.add)
            dve.drain()
            dve.wait_ge(a_done, 1)
            dve.scalar_tensor_tensor(out=la[:], in0=dt_tok[:], scalar=-1.0, in1=bcast(a_neg[:], TILES, 1),
                                     op0=ALU.mult, op1=ALU.mult).then_inc(la_done, 1)
            dve.wait_ge(sums_done, 1)
            n = TILES * SH
            for half in range(2):
                dve.tensor_copy(cum[:, :, half * SH:(half + 1) * SH],
                                sums[:, half * n:(half + 1) * n].rearrange("p (t h) -> p t h", t=TILES))
            dve.tensor_copy(tot[:], sums[:, 2 * n:4 * n].rearrange("p (t h) -> p t h", t=TILES))
            dve.drain()
            dve.tensor_tensor(t1[:], tot[:], cum[:], ALU.subtract).then_inc(cum_done, 1)
            dve.wait_ge(expo_done, 1)
            dve.tensor_tensor(dte[:], dt_tok[:], t1[:], ALU.mult)
            dve.wait_ge(taps_turned, 1)
            dve.tensor_copy(taps[:], turned_in[:, 0:NXBC * (CONV + 1)].rearrange("p (c k) -> p c k", c=NXBC)).then_inc(taps_done, 1)
            dve.wait_ge(taps_done, 1)
            with dve.Fori(0, NXBC // 2) as i:
                for u in range(2):
                    dve.wait_ge(xin_done, i * 2 + (u + 2))
                    dve.wait_ge(smooth_done, i * 2 + (u + 2))
                    ct = i * 2 + u
                    dve.tensor_scalar(acc[:], xin[:, u, 0:COUT], taps[:, ct, 0:1], taps[:, ct, CONV:CONV + 1], ALU.mult, ALU.add)
                    for k in range(1, CONV):
                        dve.drain()
                        op = dve.scalar_tensor_tensor(out=acc[:], in0=xin[:, u, k:k + COUT], scalar=taps[:, ct, k:k + 1],
                                                      in1=acc[:], op0=ALU.mult, op1=ALU.add)
                    op.then_inc(acc_done, 1)

        @block.tensor
        def _(pe):
            ident = C["ident"]
            pe.wait_ge(small_in, 16 * 7)
            for c in range(NXBC):
                mm = pe.transpose(turned_in[:, c * (CONV + 1):(c + 1) * (CONV + 1)], taps_row[:, c * P:(c + 1) * P],
                                  ident[0:CONV + 1, 0:CONV + 1])
            mm.then_inc(taps_turned, 1)
            pe.wait_ge(la_done, 1)
            pe.wait_ge(zeroed, 1)
            n = TILES * SH
            pe.matmul(sums[:, 0:n], C["tri_le"][:], la[:, :, 0:SH], start=True, stop=True)
            pe.matmul(sums[:, n:2 * n], C["tri_ge"][:], la[:, :, SH:2 * SH], start=True, stop=True)
            pe.matmul(sums[:, 2 * n:4 * n], ones[:], la[:], start=True, stop=True).then_inc(sums_done, 1)
            pe.wait_ge(cum_done, 1)
            for t in range(TILES):
                mm = pe.transpose(turned_out[0:2 * SH, t * P:(t + 1) * P], cum[:, t, :], ident[:])
            mm.then_inc(cumT_turned, 1)
            pe.wait_ge(cumT_done, 1)
            pe.wait_ge(taps_done, 1)
            pe.sem_inc(turn_done, 2)
            pe.sem_inc(back_done, 2)
            with pe.Fori(0, NXBC // 2) as i:
                for u in range(2):
                    pe.wait_ge(raw_in[u], i * 16 + 16)
                    pe.wait_ge(xin_done, i * 2 + (u + 1))
                    for t in range(TILES):
                        mm = pe.transpose(turned_in[:, t * P:(t + 1) * P], raw[:, u, t, :], ident[:])
                    mm.then_inc(turn_done, 1)
                    pe.wait_ge(smooth_done, i * 2 + (u + 3))
                    pe.wait_ge(tok_done, i * 2 + (u + 1))
                    for t in range(TILES):
                        col = 0 if t == 0 else 2 + t * P
                        mm = pe.transpose(turned_out[:, t * P:(t + 1) * P], smooth[:, u, col:col + P], ident[:])
                    mm.then_inc(back_done, 1)


def ssd_stage(nc, I, C, W, tag, steps, tiles_of, col_of):
    w = W
    with ExitStack() as ctx:
        s = Scope(nc, ctx, tag)
        bc, bt = s.sb("bc", [P, 2, 4, P]), s.sb("bt", [P, 2, SG * P])
        xd, xe = s.sb("xd", [P, 2, DSSM]), s.sb("xe", [P, 2, DSSM])
        sdec = s.sb("sdec", [P, 2, DSSM])
        sc, gm = s.sb("sc", [P, 2, SH * P]), s.sb("gm", [P, 2, SG * P])
        yo = s.sb("yo", [P, DSSM])
        cum_ps = [s.ps(f"cum{d}", SH * P) for d in range(2)]
        g_ps, o_ps, y_ps, s_ps = s.ps("g"), s.ps("o"), s.ps("y"), s.ps("s")
        bc_done, x_done, sdec_done = s.sem("bc_done"), s.sem("x_done"), s.sem("sdec_done")
        cumb_done, g_done, o_done, s_done, y_done = (s.sem(k) for k in ("cumb_done", "g_done", "o_done", "s_done", "y_done"))
        seg_done, exp_done, gm_done, sc_done = (s.sem(k) for k in ("seg_done", "exp_done", "gm_done", "sc_done"))
        yo_done, state_done, yadd_done = s.sem("yo_done"), s.sem("state_done"), s.sem("yadd_done")
        block = ctx.enter_context(nc.Block())
        tok, xbcT, y_tok, dt_tok, state, pick = (w[k] for k in ("tok", "xbcT", "y_tok", "dt_tok", "state", "pick"))
        cum, ecum, dte, dec, cumT = (w[k] for k in ("cum", "ecum", "dte", "dec", "cumT"))
        mask = (C["tri_le"], C["tri_ge"])

        def heads(ap):
            return ap.rearrange("p (h d) -> p h d", h=SH)

        def loop(eng, body):
            if steps == 1:
                body(0)
            else:
                with eng.Fori(0, steps) as i:
                    body(i)

        @block.gpsimd
        def _(pool):
            def body(i):
                for d in range(2):
                    n, t, col = i * 2 + d, tiles_of(i, d), col_of(i, d)
                    h = slice(d * SH, (d + 1) * SH)
                    pool.wait_ge(y_done, n + 1)
                    pool.tensor_copy(bc[:, d], xbcT[:, :, bass.ds(col, P)])
                    pool.tensor_copy(bt[:, d], tok[:, t, DSSM:DSSM + SG * P]).then_inc(bc_done, 1)
                    xs = heads(tok[:, t, 0:DSSM])
                    pool.tensor_tensor(heads(xd[:, d]), xs, bcast(dt_tok[:, t, h], 64, 2), ALU.mult)
                    pool.tensor_tensor(heads(xe[:, d]), xs, bcast(dte[:, t, h], 64, 2), ALU.mult).then_inc(x_done, 1)
                    pool.wait_ge(state_done, n + 1)
                    pool.tensor_tensor(heads(sdec[:, d]), heads(state[:, d]), bcast(dec[:, t, h], 64, 2),
                                       ALU.mult).then_inc(sdec_done, 1)
            loop(pool, body)

        @block.scalar
        def _(act):
            def body(i):
                for d in range(2):
                    act.wait_ge(seg_done, i * 2 + (d + 3))
                    act.activation(sc[:, d], sc[:, d], ACT.Exp).then_inc(exp_done, 1)
            loop(act, body)

        @block.vector
        def _(dve):
            dve.sem_inc(seg_done, 2)
            dve.sem_inc(gm_done, 1)
            dve.sem_inc(yo_done, 1)
            dve.sem_inc(state_done, 2)
            dve.sem_inc(yadd_done, 1)

            def segments(i, d):
                n, t = i * 2 + d, tiles_of(i, d)
                dve.drain()
                dve.wait_ge(cumb_done, n + 1)
                dve.wait_ge(y_done, n + 1)
                for h in range(SH):
                    op = dve.tensor_scalar(sc[:, d, h * P:(h + 1) * P], cum_ps[d][:, h * P:(h + 1) * P],
                                           cum[:, t, d * SH + h:d * SH + h + 1], 0.0, ALU.subtract, ALU.min)
                op.then_inc(seg_done, 1)
                dve.wait_ge(g_done, n + 1)
                dve.tensor_tensor(gm[:, d].rearrange("p (g i) -> p g i", g=SG), g_ps[:, 0:SG * P].rearrange("p (g i) -> p g i", g=SG),
                                  bcast(mask[d][:], SG, 1), ALU.mult).then_inc(gm_done, 1)

            def carried(i, d):
                n, t = i * 2 + d, tiles_of(i, d)
                dve.drain()
                dve.wait_ge(o_done, n + 1)
                dve.tensor_tensor(heads(yo[:]), heads(o_ps[:]), bcast(ecum[:, t, d * SH:(d + 1) * SH], 64, 2),
                                  ALU.mult).then_inc(yo_done, 1)
                dve.wait_ge(s_done, n + 1)
                dve.wait_ge(sdec_done, n + 1)
                dve.tensor_tensor(state[:, d], sdec[:, d], s_ps[:], ALU.add).then_inc(state_done, 1)
                dve.drain()
                dve.tensor_tensor(y_tok[:, t], y_tok[:, t], yo[:], ALU.add)

            def scores(i, d):
                n = i * 2 + d
                dve.wait_ge(exp_done, n + 1)
                for g in range(SG):
                    v = sc[:, d, g * HG * P:(g + 1) * HG * P].rearrange("p (h i) -> p h i", h=HG)
                    op = dve.tensor_tensor(v, v, bcast(gm[:, d, g * P:(g + 1) * P], HG, 1), ALU.mult)
                op.then_inc(sc_done, 1)

            def diagonal(i, d):
                n, t = i * 2 + d, tiles_of(i, d)
                dve.drain()
                dve.wait_ge(y_done, n + 3)
                dve.tensor_tensor(y_tok[:, t], y_tok[:, t], y_ps[:], ALU.add).then_inc(yadd_done, 1)

            def body(i):
                segments(i, 0)
                carried(i, 0)
                segments(i, 1)
                scores(i, 0)
                carried(i, 1)
                scores(i, 1)
                diagonal(i, 0)
                diagonal(i, 1)
            loop(dve, body)

        @block.tensor
        def _(pe):
            pe.sem_inc(y_done, 2)

            def body(i):
                for d in range(2):
                    n, t = i * 2 + d, tiles_of(i, d)
                    pe.wait_ge(seg_done, n + 1)
                    for h in range(SH):
                        mm = pe.matmul(cum_ps[d][:, h * P:(h + 1) * P], pick[:, d * SH + h, :],
                                       cumT[:, bass.ds(t * P, P)], start=True, stop=True)
                    mm.then_inc(cumb_done, 1)
                    pe.wait_ge(bc_done, n + 1)
                    pe.wait_ge(gm_done, n + 1)
                    for g in range(SG):
                        mm = pe.matmul(g_ps[:, g * P:(g + 1) * P], bc[:, d, g, :], bc[:, d, SG + g, :], start=True, stop=True)
                    mm.then_inc(g_done, 1)
                    pe.wait_ge(yo_done, n + 1)
                    pe.wait_ge(state_done, n + 1)
                    for g in range(SG):
                        r = slice(g * HG * 64, (g + 1) * HG * 64)
                        mm = pe.matmul(o_ps[:, r], bc[:, d, SG + g, :], state[:, d, r], start=True, stop=True)
                    mm.then_inc(o_done, 1)
                    pe.wait_ge(x_done, n + 1)
                    pe.wait_ge(state_done, n + 2)
                    for g in range(SG):
                        r = slice(g * HG * 64, (g + 1) * HG * 64)
                        mm = pe.matmul(s_ps[:, r], bt[:, d, g * P:(g + 1) * P], xe[:, d, r], start=True, stop=True)
                    mm.then_inc(s_done, 1)
                for d in range(2):
                    n = i * 2 + d
                    pe.wait_ge(sc_done, n + 1)
                    pe.wait_ge(yadd_done, n + 1)
                    for h in range(SH):
                        mm = pe.matmul(y_ps[:, h * 64:(h + 1) * 64], sc[:, d, h * P:(h + 1) * P],
                                       xd[:, d, h * 64:(h + 1) * 64], start=True, stop=True)
                    mm.then_inc(y_done, 1)
            loop(pe, body)


def state_stage(nc, I, C, W):
    with ExitStack() as ctx:
        s = Scope(nc, ctx, "state")
        out, inn = s.sb("out", [P, 2, 4, P]), s.sb("in", [P, 2, 4, P])
        ps_out, ps_in = [s.ps(f"out{d}") for d in range(2)], [s.ps(f"in{d}") for d in range(2)]
        loaded, turned_out, turned_in = s.sem("loaded"), s.sem("turned_out"), s.sem("turned_in")
        out_done, stored = s.sem("out_done"), s.sem("stored")
        block = ctx.enter_context(nc.Block())
        state = W["state"]

        @block.sync
        def _(sp):
            for d, name in enumerate(("state_ssm_fwd", "state_ssm_bwd")):
                sp.dma_start(inn[:, d], I[name][0, 0].rearrange("(q a) p n -> (a p) q n", a=2)).then_inc(loaded, 16)
            for d, name in enumerate(("new_hf", "new_hb")):
                sp.wait_ge(out_done, d + 1)
                sp.dma_start(I[name][0, 0].rearrange("(q a) p n -> (a p) q n", a=2), out[:, d]).then_inc(stored, 16)
            sp.wait_ge(stored, 32)

        @block.tensor
        def _(pe):
            for d in range(2):
                for q in range(4):
                    mm = pe.transpose(ps_out[d][:, q * P:(q + 1) * P], state[:, d, q * P:(q + 1) * P], C["ident"][:])
                mm.then_inc(turned_out, 1)
            pe.wait_ge(loaded, 32)
            for d in range(2):
                for q in range(4):
                    mm = pe.transpose(ps_in[d][:, q * P:(q + 1) * P], inn[:, d, q, :], C["ident"][:])
                mm.then_inc(turned_in, 1)

        @block.vector
        def _(dve):
            for d in range(2):
                dve.wait_ge(turned_out, d + 1)
                dve.tensor_copy(out[:, d].rearrange("p q n -> p (q n)"), ps_out[d][:]).then_inc(out_done, 1)
            for d in range(2):
                dve.wait_ge(turned_in, d + 1)
                dve.tensor_copy(state[:, d], ps_in[d][:])


def scan_stages(nc, I, C, W, M):
    with ExitStack() as ctx:
        s = Scope(nc, ctx, "scan")
        W["tok"], W["xbcT"] = s.sb("tok", [P, TILES, XBC]), s.sb("xbcT", [P, 4, COUT])
        W["pick"], W["state"] = s.sb("pick", [2 * SH, 2 * SH, P]), s.sb("st", [P, 2, DSSM])
        for k in ("cum", "tot", "ecum", "dte", "dec"):
            W[k] = s.sb(k, [P, TILES, 2 * SH])
        W["cumT"] = s.sb("cumT", [2 * SH, TILES * P])
        conv_stage(nc, I, C, W, M)
        with ExitStack() as load_ctx:
            pick_in = Scope(nc, load_ctx, "pick").sem("in")
            block = load_ctx.enter_context(nc.Block())

            @block.sync
            def _(sp):
                sp.dma_start(W["pick"][:], I["pick"]).then_inc(pick_in, 16)
                sp.wait_ge(pick_in, 16)

            @block.vector
            def _(dve):
                dve.memset(W["state"][:], 0.0)
        ssd_stage(nc, I, C, W, "ssdp", 1, lambda i, d: 0, lambda i, d: 0)
        state_stage(nc, I, C, W)
        ssd_stage(nc, I, C, W, "ssds", STILES, lambda i, d: i + 1 if d == 0 else i * -1 + STILES,
                  lambda i, d: i * P + (2 + P) if d == 0 else i * -P + (2 + STILES * P))


class Item:

    def __init__(self, t, h):
        self.step, self.t, self.h, self.buf = t, t.n, h, h % 2
        self.n = t.n * HEADS + h
        self.prompt = isinstance(t.n, int) and t.n == 0

    def next(self, last_tile):
        if self.h < HEADS - 1:
            return Item(self.step, self.h + 1)
        return None if last_tile else Item(self.step.next(), 0)


def attention_stage(nc, I, C, W):
    with ExitStack() as ctx:
        s = Scope(nc, ctx, "att")
        lam_rows, lam_prod = s.sb("lam_rows", [P, 4, QKD]), s.sb("lam_prod", [P, 2, QKD])
        lam_sum, lam_neg = s.sb("lam_sum", [P, 2]), s.sb("lam_neg", [P, 1])
        q_now = s.sb("q_now", [P, 2, HEADS, P])
        e = s.sb("e", [P, 2, 2, TILES * P])
        aT = s.sb("aT", [P, TILES * P])
        top, shift = s.sb("top", [P, 2, 2]), s.sb("shift", [P, 2, 2])
        total, inv, ratio = s.sb("total", [P, 2, 2]), s.sb("inv", [P, 2, 2]), s.sb("ratio", [P, 2, 1])
        sc = s.ps("sc", 5 * 512)
        turned = [s.ps(f"turned{b}") for b in range(2)]
        o_ps = s.ps("o")
        lam_in, lam_prod_done, lam_exp_done = s.sem("lam_in"), s.sem("lam_prod_done"), s.sem("lam_exp_done")
        q_staged, sc_done, shift_done, e_done = s.sem("q_staged"), s.sem("sc_done"), s.sem("shift_done"), s.sem("e_done")
        tail_done, a_done, o_done, o_read = s.sem("tail_done"), s.sem("a_done"), s.sem("o_done"), s.sem("o_read")
        t_done = [s.sem(f"t_done{g}") for g in range(3)]
        t_read = [s.sem(f"t_read{g}") for g in range(3)]
        block = ctx.enter_context(nc.Block())
        kT, qT, v_tok, o_tok = W["kT"], W["qT"], W["v_tok"], W["o_tok"]
        ident = C["ident"]

        def tail(m):
            return sc[:, 4 * 512 + m * P:4 * 512 + (m + 1) * P]

        def score_parts(it, m):
            if it.prompt:
                return [(sc[:, 2 * m * 512:2 * m * 512 + P], e[:, it.buf, m, 0:P], 0, P)]
            return [(sc[:, 2 * m * 512:(2 * m + 2) * 512], e[:, it.buf, m, 0:1024], P, P + 1024),
                    (tail(m), e[:, it.buf, m, 1024:1152], P + 1024, P + 1152)]

        def groups(it):
            return [range(0, 1)] if it.prompt else [range(0, 4), range(4, 8), range(8, 9)]

        def full_n(it):
            return it.n - HEADS

        def tiles(eng, first, body):
            first(Item(Step(0, 0), 0))
            body(Step(0, 0), False)
            with eng.Fori(0, STILES // 2 - 1) as i:
                body(Step(i, 1), False)
                body(Step(i, 2), False)
            body(Step(0, STILES - 1), False)
            body(Step(0, STILES), True)

        @block.sync
        def _(sp):
            for k, name in enumerate(("lambda_q1", "lambda_k1", "lambda_q2", "lambda_k2")):
                sp.dma_start(lam_rows[:, k], row_bcast(I[name][0])).then_inc(lam_in, 16)

        @block.gpsimd
        def _(pool):
            def copy(t, buf):
                pool.wait_ge(sc_done, t * HEADS + HEADS)
                pool.tensor_copy(q_now[:, buf], qT[:, :, bass.ds(t * P, P)]).then_inc(q_staged, 1)
            copy(0, 0)
            with pool.Fori(0, STILES // 2) as i:
                copy(i * 2 + 1, 1)
                copy(i * 2 + 2, 0)

        @block.scalar
        def _(act):
            act.wait_ge(lam_prod_done, 1)
            act.activation(lam_sum[:], lam_sum[:], ACT.Exp).then_inc(lam_exp_done, 1)

            def exponentials(it):
                act.wait_ge(shift_done, it.n + 1)
                act.wait_ge(o_done, it.n + 1)
                for m in range(2):
                    bias = shift[:, it.buf, m:m + 1]
                    parts = score_parts(it, m)
                    if it.prompt:
                        act.activation(parts[0][1], parts[0][0], ACT.Exp, bias=bias, scale=SCALE,
                                       accum_out=total[:, it.buf, m:m + 1]).then_inc(e_done, 1)
                    else:
                        act.activation(parts[0][1], parts[0][0], ACT.Exp, bias=bias, scale=SCALE,
                                       accum_out=total[:, it.buf, m:m + 1])
                        act.activation(parts[1][1], parts[1][0], ACT.Exp, bias=bias, scale=SCALE,
                                       accum_out=inv[:, it.buf, m:m + 1]).then_inc(e_done, 1)

            def evacuate(it):
                act.wait_ge(o_done, it.n + 2)
                for g, ks in enumerate(groups(it)[:2]):
                    act.wait_ge(t_done[g], (it.n if g == 0 else full_n(it)) + 1)
                    act.copy(aT[:, ks[0] * P:(ks[-1] + 1) * P], turned[g][:, 0:len(ks) * P]).then_inc(t_read[g], 1)

            def body(t, last):
                for h in range(HEADS):
                    it = Item(t, h)
                    evacuate(it)
                    nxt = it.next(last)
                    if nxt:
                        exponentials(nxt)
            tiles(act, exponentials, body)

        @block.vector
        def _(dve):
            dve.sem_inc(o_read, 1)
            dve.sem_inc(t_read[2], 1)
            dve.wait_ge(lam_in, 64)
            for k in range(2):
                dve.tensor_tensor(lam_prod[:, k], lam_rows[:, 2 * k], lam_rows[:, 2 * k + 1], ALU.mult)
            dve.drain()
            dve.tensor_reduce(lam_sum[:], lam_prod[:], AX, ALU.add).then_inc(lam_prod_done, 1)
            dve.wait_ge(lam_exp_done, 1)
            dve.tensor_tensor(lam_neg[:], lam_sum[:, 1:2], lam_sum[:, 0:1], ALU.subtract)
            dve.drain()
            dve.tensor_scalar(lam_neg[:], lam_neg[:], -LAM0, None, ALU.add)

            def maxima(it):
                dve.drain()
                dve.wait_ge(sc_done, it.n + 2 * HEADS + 1)
                if it.prompt:
                    for m in range(2):
                        dve.tensor_reduce(top[:, it.buf, m:m + 1], score_parts(it, m)[0][0], AX, ALU.max)
                    dve.drain()
                else:
                    for m in range(2):
                        dve.tensor_reduce(top[:, it.buf, m:m + 1], score_parts(it, m)[0][0], AX, ALU.max)
                    dve.tensor_reduce(shift[:, it.buf, :], sc[:, 4 * 512:4 * 512 + 2 * P].rearrange("p (m k) -> p m k", m=2),
                                      AX, ALU.max)
                    dve.drain()
                    dve.tensor_tensor(top[:, it.buf], top[:, it.buf], shift[:, it.buf], ALU.max)
                    dve.drain()
                dve.tensor_scalar(shift[:, it.buf], top[:, it.buf], -SCALE, None, ALU.mult).then_inc(shift_done, 1)

            def combine(it):
                dve.drain()
                dve.wait_ge(e_done, it.n * 2 + 4)
                tot = total[:, it.buf]
                if not it.prompt:
                    dve.tensor_tensor(tot, tot, inv[:, it.buf], ALU.add)
                    dve.drain()
                dve.reciprocal(inv[:, it.buf], tot)
                dve.drain()
                dve.tensor_scalar(ratio[:, it.buf], inv[:, it.buf, 1:2], tot[:, 0:1], lam_neg[:, 0:1], ALU.mult, ALU.mult)
                dve.drain()
                w = P if it.prompt else TILES * P
                dve.scalar_tensor_tensor(out=e[:, it.buf, 0, 0:w], in0=e[:, it.buf, 1, 0:w], scalar=ratio[:, it.buf, 0:1],
                                         in1=e[:, it.buf, 0, 0:w], op0=ALU.mult, op1=ALU.add).then_inc(a_done, 1)

            def finish(it):
                if not it.prompt:
                    dve.wait_ge(o_done, it.n + 2)
                    dve.wait_ge(t_done[2], full_n(it) + 1)
                    dve.tensor_copy(aT[:, 8 * P:9 * P], turned[0][:, 0:P]).then_inc(t_read[2], 1)
                dve.wait_ge(o_done, it.n + 3)
                dve.tensor_scalar(o_tok[:, it.t, it.h * P:(it.h + 1) * P], o_ps[:, 0:P], inv[:, it.buf, 0:1], None,
                                  ALU.mult).then_inc(o_read, 1)

            def first(it):
                maxima(it)
                combine(it)

            def body(t, last):
                for h in range(HEADS):
                    it = Item(t, h)
                    nxt = it.next(last)
                    if nxt:
                        maxima(nxt)
                    finish(it)
                    if nxt:
                        combine(nxt)
            tiles(dve, first, body)

        @block.tensor
        def _(pe):
            pe.sem_inc(sc_done, 2 * HEADS)
            pe.sem_inc(o_done, 2)
            pe.sem_inc(e_done, 2)

            def scores(it):
                pe.wait_ge(q_staged, it.t + 1)
                qbuf = it.step.buf

                def score(m, dst, lo, hi):
                    rows = slice(m * QKD, (m + 1) * QKD)
                    return pe.matmul(dst, q_now[rows, qbuf, it.h, :], kT[rows, it.h, lo:hi], start=True, stop=True)

                pe.wait_ge(e_done, it.n * 2 + 2)
                if it.prompt:
                    for m in range(2):
                        mm = score(m, sc[:, 2 * m * 512:2 * m * 512 + P], 0, P)
                    mm.then_inc(sc_done, 1)
                    return
                for part in range(2):
                    for m in range(2):
                        score(m, sc[:, (2 * m + part) * 512:(2 * m + part + 1) * 512], P + part * 512, P + (part + 1) * 512)
                score(0, tail(0), P + 1024, P + 1152).then_inc(tail_done, 1)
                pe.wait_ge(tail_done, full_n(it) + 1)
                score(1, tail(1), P + 1024, P + 1152).then_inc(sc_done, 1)

            def turn(it, g):
                ks = groups(it)[g]
                bank = turned[g % 2]
                for j, k in enumerate(ks):
                    mm = pe.transpose(bank[:, j * P:(j + 1) * P], e[:, it.buf, 0, k * P:(k + 1) * P], ident[:])
                mm.then_inc(t_done[g], 1)

            def values(it, g):
                ks = groups(it)[g]
                n = it.n if g == 0 else full_n(it)
                pe.wait_ge(t_read[g], n + (2 if g == 2 else 1))
                last = groups(it)[-1][-1]
                for k in ks:
                    mm = pe.matmul(o_ps[:, 0:P], aT[:, k * P:(k + 1) * P],
                                   v_tok[:, k + (0 if it.prompt else 1), it.h * P:(it.h + 1) * P],
                                   start=(k == 0), stop=(k == last))
                return mm

            def weigh(it):
                pe.wait_ge(a_done, it.n + 1)
                pe.wait_ge(o_read, it.n + 1)
                if it.prompt:
                    turn(it, 0)
                    values(it, 0).then_inc(o_done, 1)
                    return
                pe.wait_ge(t_read[2], full_n(it) + 1)
                turn(it, 0)
                turn(it, 1)
                values(it, 0)
                turn(it, 2)
                values(it, 1)
                values(it, 2).then_inc(o_done, 1)

            def body(t, last):
                for h in range(HEADS):
                    it = Item(t, h)
                    nxt = it.next(last)
                    if nxt:
                        scores(nxt)
                    weigh(it)
            tiles(pe, scores, body)


def refine(dve, r, ssq, scale, tmp):
    dve.drain()
    dve.tensor_scalar(tmp, ssq, scale, EPS, ALU.mult, ALU.add)
    dve.drain()
    dve.scalar_tensor_tensor(out=tmp, in0=tmp, scalar=-0.5, in1=r, op0=ALU.mult, op1=ALU.mult)
    dve.drain()
    dve.tensor_tensor(tmp, tmp, r, ALU.mult)
    dve.drain()
    dve.scalar_tensor_tensor(out=r, in0=tmp, scalar=1.5, in1=r, op0=ALU.add, op1=ALU.mult)
    dve.drain()


def mixer_stage(nc, I, C, W, M):
    with ExitStack() as ctx:
        s = Scope(nc, ctx, "mix")
        w_out = s.sb("w_out", [P, KT, D])
        gate, amul, aadd = (s.sb(k, [P, 2, D]) for k in ("gate", "amul", "aadd"))
        gain = s.sb("gain", [P, D])
        gcol = s.sb("gcol", [P, KT])
        wr, br = s.sb("wr", [P, KT, NG + NE]), s.sb("br", [P, NG + NE])
        z, x = s.sb("z", [P, 2, DSSM]), s.sb("x", [P, 2, D])
        mix, mixT = s.sb("mix", [P, 2, D]), s.sb("mixT", [P, 2, KT * P])
        h2, h2T = s.sb("h2", [P, 2, D]), s.sb("h2T", [P, KT * P])
        junk, junk2 = s.sb("junk", [P, DSSM]), s.sb("junk2", [P, D])
        ssq, rstd, tmp = s.sb("ssq", [P, 2, 5]), s.sb("rstd", [P, 2, 5]), s.sb("tmp", [P, 5])
        ssq2, rstd2, tmp2 = s.sb("ssq2", [P, 2]), s.sb("rstd2", [P, 2]), s.sb("tmp2", [P, 1])
        epsc = s.sb("epsc", [P, 1])
        t1_ps, acc, t2_ps = s.ps("t1", D), s.ps("acc", D), s.ps("t2", D)
        lg_ps = s.ps("lg")
        w_in_sem, g_in, eps_done, gains_done = s.sem("w_out_in"), s.sem("g_in"), s.sem("eps_done"), s.sem("gains_done")
        z_in, x_in = [s.sem(f"z_in{u}") for u in range(2)], [s.sem(f"x_in{u}") for u in range(2)]
        silu_done, gated, sq_done, mix_done = s.sem("silu_done"), s.sem("gated"), s.sem("sq_done"), s.sem("mix_done")
        t1_done, mixT_done, acc_done, acc_read = s.sem("t1_done"), s.sem("mixT_done"), s.sem("acc_done"), s.sem("acc_read")
        x2_done, sq2_done, h2_scaled, h2_done = s.sem("x2_done"), s.sem("sq2_done"), s.sem("h2_scaled"), s.sem("h2_done")
        t2_done, h2T_done, lg_done, lg_read = s.sem("t2_done"), s.sem("h2T_done"), s.sem("lg_done"), s.sem("lg_read")
        h2_stored = [s.sem(f"h2_stored{u}") for u in range(2)]
        block = ctx.enter_context(nc.Block())
        y_tok, o_tok, x2, logits = W["y_tok"], W["o_tok"], W["x2"], W["logits"]

        def tiles(eng, first, body):
            first(Step(0, 0))
            body(Step(0, 0), True)
            with eng.Fori(0, STILES // 2 - 1) as i:
                body(Step(i, 1), True)
                body(Step(i, 2), True)
            body(Step(0, TILES - 2), True)
            body(Step(0, TILES - 1), False)

        def is_first(t):
            return isinstance(t.n, int) and t.n == 0

        @block.sync
        def _(sp):
            sp.dma_start(gcol[:, 0:1], I["attn_subln_g"][0].unsqueeze(1)).then_inc(g_in, 16)
            sp.dma_start(gcol[:, HEADS:KT], I["ssm_norm_g"][0].rearrange("(k p) -> p k", p=P),
                         allow_slow_non_contiguous=True).then_inc(g_in, 16)
            for cond in range(2):
                for dst, sec in ((gate, GATE1), (amul, SCALE2), (aadd, SHIFT2)):
                    sp.dma_start(dst[:, cond], row_bcast(M["mods"][cond, sec * D:(sec + 1) * D])).then_inc(g_in, 16)
            sp.dma_start(gain[:], row_bcast(I["norm_ffn_g"][0])).then_inc(g_in, 16)
            sp.dma_start(wr[:, :, 0:NG], I["w_group_router"][0].rearrange("(k p) n -> p k n", p=P)).then_inc(g_in, 16)
            sp.dma_start(wr[:, :, NG:], I["w_expert_router"][0].rearrange("(k p) n -> p k n", p=P)).then_inc(g_in, 16)
            sp.dma_start(br[:, 0:NG], row_bcast(I["b_group_router"][0])).then_inc(g_in, 16)
            sp.dma_start(br[:, NG:], row_bcast(I["b_expert_router"][0])).then_inc(g_in, 16)

            def load(t):
                xrows = I["x_prompt"][0] if is_first(t) else I["x_sample"][0, bass.ds((t.n - 1) * P, P), :]
                sp.wait_ge(gated, t.n + 1)
                sp.dma_start(z[:, t.buf], M["z"][bass.ds(t.n * P, P), :]).then_inc(z_in[t.buf], 16)
                sp.wait_ge(x2_done, t.n + 1)
                sp.dma_start(x[:, t.buf], xrows).then_inc(x_in[t.buf], 16)

            def body(t, more):
                if more:
                    load(t.next())
                sp.wait_ge(h2_done, t.n + 3)
                sp.dma_start(M["h2"][bass.ds(t.n * P, P), :], h2[:, t.buf]).then_inc(h2_stored[t.buf], 16)
            tiles(sp, load, body)
            sp.wait_ge(h2_stored[0], 16 * 6)
            sp.wait_ge(h2_stored[1], 16 * 5)

        @block.gpsimd
        def _(pool):
            for k in range(KT):
                pool.dma_start(w_out[:, k], I["w_out"][0, k * P:(k + 1) * P, :]).then_inc(w_in_sem, 16)
            pool.sem_inc(x2_done, 2)
            pool.sem_inc(h2_done, 2)

            def body(t, more):
                pool.wait_ge(x_in[t.buf], t.nth * 16 + 16)
                pool.wait_ge(acc_read, t.n + 2)
                pool.tensor_tensor(x2[:, t.n], x2[:, t.n], x[:, t.buf], ALU.add).then_inc(x2_done, 1)
                pool.wait_ge(h2_scaled, t.n + 1)
                pool.tensor_tensor(h2[:, t.buf], h2[:, t.buf], aadd[:, 0 if is_first(t) else 1], ALU.add).then_inc(h2_done, 1)
            tiles(pool, lambda t: None, body)

        @block.scalar
        def _(act):
            act.sem_inc(h2T_done, 1)
            act.wait_ge(eps_done, 1)

            def prepare(t):
                act.wait_ge(z_in[t.buf], t.nth * 16 + 16)
                act.activation(z[:, t.buf], z[:, t.buf], ACT.Silu).then_inc(silu_done, 1)
                for h in range(HEADS):
                    act.activation(junk[:, h * P:(h + 1) * P], o_tok[:, t.n, h * P:(h + 1) * P], ACT.Square,
                                   accum_out=ssq[:, t.buf, h:h + 1])
                act.drain()
                act.activation(rstd[:, t.buf, 0:HEADS], ssq[:, t.buf, 0:HEADS], ACT.Sqrt, bias=epsc[:, 0:1], scale=1.0 / P)
                act.wait_ge(gated, t.n + 3)
                act.activation(junk[:], mix[:, t.buf, DATT:], ACT.Square, accum_out=ssq[:, t.buf, HEADS:HEADS + 1])
                act.drain()
                act.activation(rstd[:, t.buf, HEADS:HEADS + 1], ssq[:, t.buf, HEADS:HEADS + 1], ACT.Sqrt, bias=epsc[:, 0:1],
                               scale=1.0 / DSSM).then_inc(sq_done, 1)

            def evacuate(t):
                act.wait_ge(lg_done, t.n + 1)
                act.wait_ge(t2_done, t.n + 3)
                act.copy(h2T[:], t2_ps[:]).then_inc(h2T_done, 1)

            def body(t, more):
                if more:
                    prepare(t.next())
                act.wait_ge(x2_done, t.n + 3)
                act.activation(junk2[:], x2[:, t.n], ACT.Square, accum_out=ssq2[:, t.buf:t.buf + 1])
                act.drain()
                act.activation(rstd2[:, t.buf:t.buf + 1], ssq2[:, t.buf:t.buf + 1], ACT.Sqrt, bias=epsc[:, 0:1],
                               scale=1.0 / D).then_inc(sq2_done, 1)
                if not is_first(t):
                    evacuate(Step(t.i, t.c - 1))
            tiles(act, prepare, body)
            evacuate(Step(0, TILES - 1))

        @block.vector
        def _(dve):
            dve.memset(epsc[:], EPS).then_inc(eps_done, 1)
            dve.sem_inc(gated, 2)
            dve.sem_inc(mixT_done, 1)
            dve.sem_inc(acc_read, 1)
            dve.sem_inc(lg_read, 1)
            for u in range(2):
                dve.sem_inc(h2_stored[u], 16)
            dve.wait_ge(g_in, 16 * 13)
            for cond in range(2):
                dve.scalar_tensor_tensor(out=amul[:, cond], in0=amul[:, cond], scalar=1.0, in1=gain[:], op0=ALU.add, op1=ALU.mult)
            dve.tensor_scalar(gcol[:, 0:1], gcol[:, 0:1], 1.0 - LAM0, None, ALU.mult)
            dve.drain()
            for h in range(1, HEADS):
                dve.tensor_copy(gcol[:, h:h + 1], gcol[:, 0:1])
            dve.drain()

            def prepare(t):
                dve.drain()
                dve.wait_ge(silu_done, t.n + 1)
                dve.wait_ge(t1_done, t.n + 1)
                dve.tensor_tensor(mix[:, t.buf, DATT:], z[:, t.buf], y_tok[:, t.n], ALU.mult).then_inc(gated, 1)
                dve.wait_ge(sq_done, t.n + 1)
                r = rstd[:, t.buf]
                dve.reciprocal(r, r)
                refine(dve, r[:, 0:HEADS], ssq[:, t.buf, 0:HEADS], 1.0 / P, tmp[:, 0:HEADS])
                refine(dve, r[:, HEADS:], ssq[:, t.buf, HEADS:], 1.0 / DSSM, tmp[:, HEADS:])
                dve.tensor_tensor(mix[:, t.buf, 0:DATT].rearrange("p (h d) -> p h d", h=HEADS),
                                  o_tok[:, t.n].rearrange("p (h d) -> p h d", h=HEADS), bcast(r[:, 0:HEADS], P, 2), ALU.mult)
                dve.tensor_scalar(mix[:, t.buf, DATT:], mix[:, t.buf, DATT:], r[:, HEADS:], None, ALU.mult).then_inc(mix_done, 1)

            def gains(t):
                dve.wait_ge(acc_done, t.n + 1)
                dve.wait_ge(t1_done, t.n + 3)
                dve.tensor_tensor(mixT[:, t.buf].rearrange("p (k t) -> p k t", k=KT), t1_ps[:].rearrange("p (k t) -> p k t", k=KT),
                                  bcast(gcol[:], P, 2), ALU.mult).then_inc(mixT_done, 1)

            def router(t):
                dve.wait_ge(lg_done, t.n + 2)
                dve.tensor_tensor(logits[:, t.n], lg_ps[:, 0:NG + NE], br[:], ALU.add).then_inc(lg_read, 1)

            def first(t):
                prepare(t)
                gains(t)

            def body(t, more):
                cond = 0 if is_first(t) else 1
                if more:
                    prepare(t.next())
                dve.wait_ge(acc_done, t.n + 3)
                dve.tensor_tensor(x2[:, t.n], acc[:], gate[:, cond], ALU.mult).then_inc(acc_read, 1)
                if more:
                    gains(t.next())
                dve.wait_ge(sq2_done, t.n + 1)
                r = rstd2[:, t.buf:t.buf + 1]
                dve.reciprocal(r, r)
                refine(dve, r, ssq2[:, t.buf:t.buf + 1], 1.0 / D, tmp2[:])
                dve.wait_ge(t2_done, t.n + 1)
                dve.wait_ge(h2_stored[t.buf], t.nth * 16 + 16)
                dve.scalar_tensor_tensor(out=h2[:, t.buf], in0=x2[:, t.n], scalar=r, in1=amul[:, cond], op0=ALU.mult,
                                         op1=ALU.mult).then_inc(h2_scaled, 1)
                if not is_first(t):
                    router(Step(t.i, t.c - 1))

            tiles(dve, first, body)
            router(Step(0, TILES - 1))

        @block.tensor
        def _(pe):
            ident = C["ident"]
            pe.sem_inc(t1_done, 2)
            pe.sem_inc(acc_done, 2)
            pe.sem_inc(lg_done, 1)
            pe.sem_inc(t2_done, 2)
            pe.wait_ge(w_in_sem, 16 * KT)

            def turn_mix(t):
                pe.wait_ge(mix_done, t.n + 1)
                pe.wait_ge(mixT_done, t.n + 1)
                for k in range(KT):
                    mm = pe.transpose(t1_ps[:, k * P:(k + 1) * P], mix[:, t.buf, k * P:(k + 1) * P], ident[:])
                mm.then_inc(t1_done, 1)

            def finish(t):
                pe.wait_ge(h2_done, t.n + 3)
                pe.wait_ge(h2T_done, t.n + 1)
                for k in range(KT):
                    mm = pe.transpose(t2_ps[:, k * P:(k + 1) * P], h2[:, t.buf, k * P:(k + 1) * P], ident[:])
                mm.then_inc(t2_done, 1)
                pe.wait_ge(h2T_done, t.n + 2)
                pe.wait_ge(lg_read, t.n + 1)
                for k in range(KT):
                    mm = pe.matmul(lg_ps[:, 0:NG + NE], h2T[:, k * P:(k + 1) * P], wr[:, k], start=(k == 0), stop=(k == KT - 1))
                mm.then_inc(lg_done, 1)

            def body(t, more):
                pe.wait_ge(mixT_done, t.n + 2)
                pe.wait_ge(acc_read, t.n + 1)
                for half in range(2):
                    for k in range(KT):
                        mm = pe.matmul(acc[:, half * 512:(half + 1) * 512], mixT[:, t.buf, k * P:(k + 1) * P],
                                       w_out[:, k, half * 512:(half + 1) * 512], start=(k == 0), stop=(k == KT - 1))
                mm.then_inc(acc_done, 1)
                if more:
                    turn_mix(t.next())
                if not is_first(t):
                    finish(Step(t.i, t.c - 1))
            tiles(pe, turn_mix, body)
            finish(Step(0, TILES - 1))


def routing_stage(nc, I, C, W, M):
    with ExitStack() as ctx:
        s = Scope(nc, ctx, "route")
        T = TILES
        steps, tokens = s.sb("steps", [P, BLOCKS]), s.sb("tokens", [P, T])
        ones, zeros = s.sb("ones", [P, P]), s.sb("zeros", [P, 2 * BLOCKS])
        gmax, gdiff, gsum, pg = s.sb("gmax", [P, T]), s.sb("gdiff", [P, T, NG]), s.sb("gsum", [P, T]), s.sb("pg", [P, T])
        ohg, oh = s.sb("ohg", [P, T, NG]), s.sb("oh", [P, 2, T, EPG])
        seen, left = s.sb("seen", [P, T]), s.sb("left", [P, T])
        prod, esel, esel2 = s.sb("prod", [P, T, NG, EPG]), s.sb("esel", [P, T, EPG]), s.sb("esel2", [P, T, EPG])
        top = s.sb("top", [P, 2, T])
        ediff, wsum = s.sb("ediff", [P, T]), s.sb("wsum", [P, T])
        pick = s.sb("pick", [P, 2, T, NE])
        both, place, weighed = s.sb("both", [P, T, NE]), s.sb("place", [P, T, NE]), s.sb("weighed", [P, T, NE])
        before, count = s.sb("before", [P, T, NE]), s.sb("count", [P, NE])
        more, nblk, bend, bones = s.sb("more", [P, NE, T]), s.sb("nblk", [P, NE]), s.sb("bend", [P, NE]), s.sb("bones", [P, NE])
        past, of_block = s.sb("past", [P, BLOCKS, NE]), s.sb("of_block", [P, BLOCKS])
        slot_f = s.sb("slot_f", [P, T])
        slot_u = [[s.sb(f"slot{c}_{t}", [P, 1], U32) for t in range(T)] for c in range(2)]
        value = s.sb("value", [P, 2, T, 2])
        table = s.sb("table", [P, BLOCKS, 2])
        rank_ps, sum_ps = s.ps("rank"), s.ps("sum")
        c_in, z_done, z_stored = s.sem("c_in"), s.sem("z_done"), s.sem("z_stored")
        g_done, gexp_done, e_done, eexp_done = s.sem("g_done"), s.sem("gexp_done"), s.sem("e_done"), s.sem("eexp_done")
        both_done, ranked, slots_done, scattered, table_in = (s.sem(k) for k in
                                                              ("both_done", "ranked", "slots_done", "scattered", "table_in"))
        block = ctx.enter_context(nc.Block())
        logits = W["logits"]
        lg = logits[:, :, 0:NG]
        le = logits[:, :, NG:].rearrange("p t (g e) -> p t g e", g=NG)

        @block.sync
        def _(sp):
            sp.dma_start(steps[:], row_bcast(I["steps"])).then_inc(c_in, 16)
            sp.dma_start(tokens[:], I["tokens"]).then_inc(c_in, 16)
            sp.wait_ge(z_done, 1)
            sp.dma_start(M["slots"].rearrange("(p b) c -> p (b c)", p=P), zeros[:]).then_inc(z_stored, 16)
            sp.wait_ge(scattered, 16 * 2 * T)
            sp.dma_start(table[:], M["slots"].rearrange("(b p) c -> p b c", p=P)).then_inc(table_in, 16)

        @block.gpsimd
        def _(pool):
            pool.memset(zeros[:], 0.0).then_inc(z_done, 1)
            pool.wait_ge(z_stored, 16)
            pool.wait_ge(slots_done, 1)
            for c in range(2):
                for t in range(T):
                    pool.indirect_dma_start(M["slots"], bass.IndirectOffsetOnAxis(ap=slot_u[c][t][:], axis=0),
                                            value[:, c, t, :], None).then_inc(scattered, 16)
            pool.wait_ge(scattered, 16 * 2 * T)

        @block.scalar
        def _(act):
            act.wait_ge(g_done, 1)
            act.activation(gdiff[:], gdiff[:], ACT.Exp).then_inc(gexp_done, 1)
            act.wait_ge(e_done, 1)
            act.activation(ediff[:], ediff[:], ACT.Exp).then_inc(eexp_done, 1)

        @block.tensor
        def _(pe):
            pe.wait_ge(both_done, 1)
            v = both[:].rearrange("p t e -> p (t e)")
            pe.matmul(rank_ps[:, 0:T * NE], C["tri_lt"][:], v, start=True, stop=True)
            pe.matmul(sum_ps[:, 0:T * NE], ones[:], v, start=True, stop=True).then_inc(ranked, 1)

        @block.vector
        def _(dve):
            def tt(out, a, b, op):
                dve.tensor_tensor(out, a, b, op)
                dve.drain()

            def keep_first(v, n):
                dve.tensor_copy(seen[:], v[:, :, 0])
                dve.drain()
                for j in range(1, n):
                    dve.tensor_scalar(left[:], seen[:], -1.0, 1.0, ALU.mult, ALU.add)
                    dve.drain()
                    tt(v[:, :, j], v[:, :, j], left[:], ALU.mult)
                    tt(seen[:], seen[:], v[:, :, j], ALU.max)

            dve.memset(ones[:], 1.0)
            dve.memset(bones[:], 1.0)
            dve.tensor_reduce(gmax[:], lg, AX, ALU.max)
            dve.drain()
            dve.tensor_tensor(gdiff[:], lg, bcast(gmax[:], NG, 2), ALU.subtract).then_inc(g_done, 1)
            tt(ohg[:], lg, bcast(gmax[:], NG, 2), ALU.is_equal)
            keep_first(ohg[:], NG)
            tt(prod[:], le, bcast(ohg[:], EPG, 3), ALU.mult)
            dve.tensor_reduce(esel[:], prod[:].rearrange("p t g e -> p t e g"), AX, ALU.add)
            dve.drain()
            dve.tensor_reduce(top[:, 0], esel[:], AX, ALU.max)
            dve.drain()
            tt(oh[:, 0], esel[:], bcast(top[:, 0], EPG, 2), ALU.is_equal)
            keep_first(oh[:, 0], EPG)
            dve.scalar_tensor_tensor(out=esel2[:].rearrange("p t e -> p (t e)"), in0=oh[:, 0].rearrange("p t e -> p (t e)"),
                                     scalar=-3.0e38, in1=esel[:].rearrange("p t e -> p (t e)"), op0=ALU.mult, op1=ALU.add)
            dve.drain()
            dve.tensor_reduce(top[:, 1], esel2[:], AX, ALU.max)
            dve.drain()
            dve.tensor_tensor(ediff[:], top[:, 1], top[:, 0], ALU.subtract).then_inc(e_done, 1)
            tt(oh[:, 1], esel2[:], bcast(top[:, 1], EPG, 2), ALU.is_equal)
            keep_first(oh[:, 1], EPG)
            dve.wait_ge(gexp_done, 1)
            dve.tensor_reduce(gsum[:], gdiff[:], AX, ALU.add)
            dve.wait_ge(eexp_done, 1)
            dve.tensor_scalar(wsum[:], ediff[:], 1.0, None, ALU.add)
            dve.drain()
            tt(pg[:], gsum[:], wsum[:], ALU.mult)
            dve.reciprocal(pg[:], pg[:])
            dve.drain()
            dve.tensor_copy(value[:, 0, :, 1], pg[:])
            dve.tensor_tensor(value[:, 1, :, 1], pg[:], ediff[:], ALU.mult)
            dve.wait_ge(c_in, 32)
            for c in range(2):
                dve.tensor_copy(value[:, c, :, 0], tokens[:])
                dve.tensor_tensor(pick[:, c].rearrange("p t (g e) -> p t g e", g=NG), bcast(ohg[:], EPG, 3),
                                  bcast(oh[:, c], NG, 2), ALU.mult)
            dve.drain()
            dve.tensor_tensor(both[:], pick[:, 0], pick[:, 1], ALU.add).then_inc(both_done, 1)
            dve.memset(before[:, 0], 0.0)
            dve.drain()
            dve.wait_ge(ranked, 1)
            for t in range(1, T):
                tt(before[:, t], before[:, t - 1], sum_ps[:, (t - 1) * NE:t * NE], ALU.add)
            tt(count[:], before[:, T - 1], sum_ps[:, (T - 1) * NE:T * NE], ALU.add)
            tt(place[:], before[:], rank_ps[:, 0:T * NE].rearrange("p (t e) -> p t e", t=T), ALU.add)
            dve.tensor_scalar(count[:], count[:], 1.0 / P, None, ALU.mult)
            dve.drain()
            tt(more[:], bcast(count[:], T, 2), bcast(steps[:, 0:T], NE, 1), ALU.is_gt)
            dve.tensor_reduce(nblk[:], more[:], AX, ALU.add)
            dve.drain()
            dve.tensor_tensor_scan(bend[:], bones[:], nblk[:], 0.0, ALU.mult, ALU.add)
            dve.drain()
            tt(past[:], bcast(steps[:], NE, 2), bcast(bend[:], BLOCKS, 1), ALU.is_ge)
            dve.tensor_reduce(of_block[:], past[:], AX, ALU.add)
            dve.drain()
            dve.tensor_scalar(of_block[:], of_block[:], float(NE - 1), None, ALU.min)
            dve.drain()
            dve.tensor_copy(W["block_expert"][:], of_block[:])
            tt(nblk[:], bend[:], nblk[:], ALU.subtract)
            dve.tensor_scalar(nblk[:], nblk[:], float(P), None, ALU.mult)
            dve.drain()
            tt(place[:], place[:], bcast(nblk[:], T, 1), ALU.add)
            for c in range(2):
                tt(weighed[:], pick[:, c], place[:], ALU.mult)
                dve.tensor_reduce(slot_f[:], weighed[:], AX, ALU.add)
                dve.drain()
                for t in range(T):
                    dve.tensor_copy(slot_u[c][t][:], slot_f[:, t:t + 1])
                op = dve.tensor_copy(W["slot_of"][:, :, c], slot_f[:])
                dve.drain()
            dve.tensor_copy(slot_f[:], slot_f[:]).then_inc(slots_done, 1)
            dve.wait_ge(table_in, 16)
            dve.tensor_copy(W["block_token"][:], table[:, :, 0])
            dve.tensor_copy(W["block_weight"][:], table[:, :, 1])


def expert_stage(nc, I, C, W, M):
    NB = 3
    with ExitStack() as ctx:
        s = Scope(nc, ctx, "moe")
        wgu, wd = s.sb("wgu", [P, NB, KT, 2 * FF]), s.sb("wd", [P, NB, 2, D])
        idx = [s.sb(f"idx{u}", [P, 1], U32) for u in range(NB)]
        xg, xT = s.sb("xg", [P, NB, D]), s.sb("xT", [P, NB, KT * P])
        act_g, hid, hidT = s.sb("act_g", [P, FF]), s.sb("hid", [P, FF]), s.sb("hidT", [P, FF])
        y = s.sb("y", [P, NB, D])
        x_ps, gu_ps, h_ps, y_ps = s.ps("x", D), s.ps("gu"), s.ps("h"), s.ps("y", D)
        w_in = [s.sem(f"w_in{u}") for u in range(NB)]
        xg_in = [s.sem(f"xg_in{u}") for u in range(NB)]
        y_out = [s.sem(f"y_out{u}") for u in range(NB)]
        idx_done, x_turned, xT_done, gu_done, silu_done, hid_done = (s.sem(k) for k in ("idx_done", "x_turned", "xT_done", "gu_done", "silu_done", "hid_done"))
        h_turned, hidT_done, y_done, y_read = (s.sem(k) for k in ("h_turned", "hidT_done", "y_done", "y_read"))
        block = ctx.enter_context(nc.Block())
        started = s.sem("started")
        expert, token, weight = W["block_expert"], W["block_token"], W["block_weight"]
        LOOPS = BLOCKS // NB
        assert LOOPS * NB == BLOCKS

        @block.sync
        def _(sp):
            with sp.Fori(0, LOOPS) as i:
                for u in range(NB):
                    n = i * NB + u
                    e = sp.value_load(expert[0:1, bass.ds(n, 1)], min_val=0, max_val=NE - 1)
                    sp.wait_ge(y_done, n + 1)
                    sp.dma_start(wgu[:, u, :, 0:FF], I["w_exp_gate"][0, e].rearrange("(k p) f -> p k f", p=P)).then_inc(w_in[u], 16)
                    sp.dma_start(wgu[:, u, :, FF:], I["w_exp_up"][0, e].rearrange("(k p) f -> p k f", p=P)).then_inc(w_in[u], 16)
                    sp.dma_start(wd[:, u], I["w_exp_down"][0, e].rearrange("(k p) d -> p k d", p=P)).then_inc(w_in[u], 16)

        @block.gpsimd
        def _(pool):
            with pool.Fori(0, LOOPS) as i:
                for u in range(NB):
                    n = i * NB + u
                    pool.wait_ge(x_turned, n + 1)
                    pool.tensor_copy(idx[u][:], token[:, bass.ds(n, 1)]).then_inc(idx_done, 1)
                    pool.wait_ge(idx_done, n + 1)
                    pool.sem_inc(started, 1)
                    pool.indirect_dma_start(xg[:, u], None, M["h2"],
                                            bass.IndirectOffsetOnAxis(ap=idx[u][:], axis=0)).then_inc(xg_in[u], 16)

        @block.tensor
        def _(pe):
            ident = C["ident"]
            pe.sem_inc(y_done, NB)
            pe.sem_inc(x_turned, NB)
            pe.sem_inc(gu_done, NB)

            def turn(n, u, nth):
                pe.wait_ge(xg_in[u], nth * 16 + 16)
                pe.wait_ge(xT_done, n + 1)
                for k in range(KT):
                    mm = pe.transpose(x_ps[:, k * P:(k + 1) * P], xg[:, u, k * P:(k + 1) * P], ident[:])
                mm.then_inc(x_turned, 1)

            def block_(n, u, i, turn_next):
                pe.wait_ge(w_in[u], i * 48 + 48)
                pe.wait_ge(xT_done, n + 2)
                pe.wait_ge(hid_done, n + 1)
                for k in range(KT):
                    mm = pe.matmul(gu_ps[:], xT[:, u, k * P:(k + 1) * P], wgu[:, u, k], start=(k == 0), stop=(k == KT - 1))
                mm.then_inc(gu_done, 1)
                if turn_next:
                    turn(n + 1, (u + 1) % NB, i + (u + 1) // NB)
                pe.wait_ge(hid_done, n + 2)
                pe.wait_ge(hidT_done, n + 1)
                for k in range(2):
                    mm = pe.transpose(h_ps[:, k * P:(k + 1) * P], hid[:, k * P:(k + 1) * P], ident[:])
                mm.then_inc(h_turned, 1)
                pe.wait_ge(hidT_done, n + 2)
                pe.wait_ge(y_read, n + 1)
                for half in range(2):
                    for k in range(2):
                        mm = pe.matmul(y_ps[:, half * 512:(half + 1) * 512], hidT[:, k * P:(k + 1) * P],
                                       wd[:, u, k, half * 512:(half + 1) * 512], start=(k == 0), stop=(k == 1))
                mm.then_inc(y_done, 1)

            turn(0, 0, 0)
            with pe.Fori(0, LOOPS - 1) as i:
                for u in range(NB):
                    block_(i * NB + u, u, i, True)
            for u in range(NB):
                block_((LOOPS - 1) * NB + u, u, LOOPS - 1, u < NB - 1)

        @block.scalar
        def _(act):
            act.sem_inc(xT_done, 1)
            act.sem_inc(y_read, 1)

            def take_x(n, u):
                act.wait_ge(x_turned, n + 1 + NB)
                act.wait_ge(gu_done, n + 1)
                act.copy(xT[:, u], x_ps[:]).then_inc(xT_done, 1)

            def block_(n, u, i, take_next):
                act.wait_ge(gu_done, n + 1 + NB)
                act.wait_ge(hid_done, n + 1)
                act.activation(act_g[:], gu_ps[:, 0:FF], ACT.Silu).then_inc(silu_done, 1)
                if take_next:
                    take_x(n + 1, (u + 1) % NB)
                act.wait_ge(y_done, n + 1 + NB)
                act.wait_ge(y_out[u], i * 16 + 16)
                act.copy(y[:, u], y_ps[:]).then_inc(y_read, 1)

            for u in range(NB):
                act.sem_inc(y_out[u], 16)
            take_x(0, 0)
            with act.Fori(0, LOOPS - 1) as i:
                for u in range(NB):
                    block_(i * NB + u, u, i, True)
                    act.wait_ge(y_read, i * NB + (u + 2))
                    act.dma_start(M["y_slots"][bass.ds((i * NB + u) * P, P), :], y[:, u]).then_inc(y_out[u], 16)
            for u in range(NB):
                n = (LOOPS - 1) * NB + u
                block_(n, u, LOOPS - 1, u < NB - 1)
                act.wait_ge(y_read, n + 2)
                act.dma_start(M["y_slots"][n * P:(n + 1) * P, :], y[:, u]).then_inc(y_out[u], 16)
            for u in range(NB):
                act.wait_ge(y_out[u], 16 * (LOOPS + 1))

        @block.vector
        def _(dve):
            dve.sem_inc(hid_done, 1)
            dve.sem_inc(hidT_done, 1)
            with dve.Fori(0, LOOPS) as i:
                for u in range(NB):
                    n = i * NB + u
                    dve.wait_ge(silu_done, n + 1)
                    dve.scalar_tensor_tensor(out=hid[:], in0=gu_ps[:, FF:2 * FF], scalar=weight[:, bass.ds(n, 1)],
                                             in1=act_g[:], op0=ALU.mult, op1=ALU.mult).then_inc(hid_done, 1)
                    dve.wait_ge(h_turned, n + 1)
                    dve.wait_ge(y_done, n + NB)
                    dve.tensor_copy(hidT[:], h_ps[:, 0:FF]).then_inc(hidT_done, 1)


def final_stage(nc, I, C, W, M):
    with ExitStack() as ctx:
        s = Scope(nc, ctx, "fin")
        gate, gain = s.sb("gate", [P, 2, D]), s.sb("gain", [P, D])
        ya, yb = s.sb("ya", [P, 2, D]), s.sb("yb", [P, 2, D])
        idx = [[s.sb(f"idx{c}{u}", [P, 1], U32) for u in range(2)] for c in range(2)]
        out, junk = s.sb("out", [P, 2, D]), s.sb("junk", [P, D])
        ssq, rstd, tmp, epsc = s.sb("ssq", [P, 2]), s.sb("rstd", [P, 2]), s.sb("tmp", [P, 1]), s.sb("epsc", [P, 1])
        g_in, idx_done = s.sem("g_in"), s.sem("idx_done")
        y_in = [s.sem(f"y_in{u}") for u in range(2)]
        x3_done, sq_done, out_done, out_stored = s.sem("x3_done"), s.sem("sq_done"), s.sem("out_done"), [s.sem(f"out_stored{u}") for u in range(2)]
        block = ctx.enter_context(nc.Block())
        started = s.sem("started")
        x2, slot_of = W["x2"], W["slot_of"]

        def tiles(eng, body):
            body(Step(0, 0))
            with eng.Fori(0, STILES // 2) as i:
                body(Step(i, 1))
                body(Step(i, 2))

        def is_first(t):
            return isinstance(t.n, int) and t.n == 0

        @block.sync
        def _(sp):
            for cond in range(2):
                sp.dma_start(gate[:, cond], row_bcast(M["mods"][cond, GATE2 * D:(GATE2 + 1) * D])).then_inc(g_in, 16)
            sp.dma_start(gain[:], row_bcast(I["final_norm_g"])).then_inc(g_in, 16)

            def body(t):
                dst = I["y_prompt"][0] if is_first(t) else I["y_sample"][0, bass.ds((t.n - 1) * P, P), :]
                sp.wait_ge(out_done, t.n + 1)
                sp.dma_start(dst, out[:, t.buf]).then_inc(out_stored[t.buf], 16)
            tiles(sp, body)
            sp.wait_ge(out_stored[0], 16 * 6)
            sp.wait_ge(out_stored[1], 16 * 5)

        @block.gpsimd
        def _(pool):
            def body(t):
                pool.wait_ge(x3_done, t.n + 1)
                for c in range(2):
                    pool.tensor_copy(idx[c][t.buf][:], slot_of[:, t.n, c:c + 1]).then_inc(idx_done, 1)
                pool.wait_ge(idx_done, t.n * 2 + 2)
                pool.sem_inc(started, 1)
                for c, dst in enumerate((ya, yb)):
                    pool.indirect_dma_start(dst[:, t.buf], None, M["y_slots"],
                                            bass.IndirectOffsetOnAxis(ap=idx[c][t.buf][:], axis=0)).then_inc(y_in[t.buf], 16)
            tiles(pool, body)

        @block.scalar
        def _(act):
            def body(t):
                act.wait_ge(x3_done, t.n + 3)
                act.activation(junk[:], x2[:, t.n], ACT.Square, accum_out=ssq[:, t.buf:t.buf + 1])
                act.drain()
                act.activation(rstd[:, t.buf:t.buf + 1], ssq[:, t.buf:t.buf + 1], ACT.Sqrt, bias=epsc[:, 0:1],
                               scale=1.0 / D).then_inc(sq_done, 1)
            tiles(act, body)

        @block.vector
        def _(dve):
            dve.memset(epsc[:], EPS)
            dve.sem_inc(x3_done, 2)
            for u in range(2):
                dve.sem_inc(out_stored[u], 16)
            dve.wait_ge(g_in, 48)

            def body(t):
                cond = 0 if is_first(t) else 1
                dve.wait_ge(y_in[t.buf], t.nth * 32 + 32)
                dve.tensor_tensor(ya[:, t.buf], ya[:, t.buf], yb[:, t.buf], ALU.add)
                dve.drain()
                dve.tensor_tensor(ya[:, t.buf], ya[:, t.buf], gate[:, cond], ALU.mult)
                dve.drain()
                dve.tensor_tensor(x2[:, t.n], x2[:, t.n], ya[:, t.buf], ALU.add).then_inc(x3_done, 1)
                r = rstd[:, t.buf:t.buf + 1]
                dve.wait_ge(sq_done, t.n + 1)
                dve.reciprocal(r, r)
                refine(dve, r, ssq[:, t.buf:t.buf + 1], 1.0 / D, tmp[:])
                dve.wait_ge(out_stored[t.buf], t.nth * 16 + 16)
                dve.scalar_tensor_tensor(out=out[:, t.buf], in0=x2[:, t.n], scalar=r, in1=gain[:], op0=ALU.mult,
                                         op1=ALU.mult).then_inc(out_done, 1)
            tiles(dve, body)


def load_stage(nc, tag, loads):
    with ExitStack() as ctx:
        loaded = Scope(nc, ctx, tag).sem("done")
        block = ctx.enter_context(nc.Block())

        @block.sync
        def _(sp):
            for dst, src in loads:
                sp.dma_start(dst, src).then_inc(loaded, 16)
            sp.wait_ge(loaded, 16 * len(loads))


def build(nc, I, M):
    with ExitStack() as ctx:
        s = Scope(nc, ctx, "all")
        C = {"ident": s.sb("ident", [P, P])}
        load_stage(nc, "load_ident", [(C["ident"][:], I["ident"])])
        W = {}
        with ExitStack() as mix_ctx:
            with ExitStack() as att_ctx:
                right = Scope(nc, att_ctx, "att_in")
                with ExitStack() as proj_ctx:
                    ps = Scope(nc, proj_ctx, "w")
                    W["w_in"], W["w_in_sem"] = ps.sb("w_in", [P, KT, IN_COLS]), ps.sem("w_in_sem")
                    ada_stage(nc, I, C, W, M)
                    W["kT"] = right.sb("kT", [P, HEADS, (TILES + 1) * P], side="right")
                    W["qT"] = right.sb("qT", [P, HEADS, TILES * P], side="right")
                    W["v_tok"] = right.sb("v_tok", [P, TILES + 1, 512], side="right")
                    W["dt_tok"] = right.sb("dt_tok", [P, TILES, 2 * SH], side="right")
                    projection_stage(nc, I, C, W, M)
                for name in ("tri_le", "tri_ge", "tri_lt"):
                    C[name] = s.sb(name, [P, P])
                load_stage(nc, "load_tri", [(C[name][:], I[name]) for name in ("tri_le", "tri_ge", "tri_lt")])
                m = Scope(nc, mix_ctx, "mix_in")
                W["y_tok"] = m.sb("y_tok", [P, TILES, DSSM])
                scan_stages(nc, I, C, W, M)
                W["o_tok"] = m.sb("o_tok", [P, TILES, DATT])
                attention_stage(nc, I, C, W)
            r = Scope(nc, ctx, "moe_in")
            W["x2"] = r.sb("x2", [P, TILES, D], side="right")
            W["logits"] = r.sb("logits", [P, TILES, NG + NE], side="right")
            mixer_stage(nc, I, C, W, M)
        W["block_expert"] = s.sb("block_expert", [P, BLOCKS], I32)
        W["block_token"] = s.sb("block_token", [P, BLOCKS], U32)
        W["block_weight"] = s.sb("block_weight", [P, BLOCKS])
        W["slot_of"] = s.sb("slot_of", [P, TILES, 2], U32)
        routing_stage(nc, I, C, W, M)
        expert_stage(nc, I, C, W, M)
        final_stage(nc, I, C, W, M)


_INS = ['x_prompt', 'x_sample', 'cache_k', 'cache_v', 'state_ssm_fwd', 'state_ssm_bwd', 'c', 'c_ctx', 'w_ada', 'b_ada',
        'norm_mix_g', 'w_in', 'w_out', 'lambda_q1', 'lambda_k1', 'lambda_q2', 'lambda_k2', 'attn_subln_g', 'conv_w',
        'conv_b', 'a_log_fwd', 'a_log_bwd', 'dt_bias_fwd', 'dt_bias_bwd', 'ssm_d', 'ssm_norm_g', 'norm_ffn_g',
        'w_group_router', 'b_group_router', 'w_expert_router', 'b_expert_router', 'w_exp_gate', 'w_exp_up',
        'w_exp_down', 'final_norm_g']
_OUTS = {'y_prompt': (1, P, D), 'y_sample': (1, STILES * P, D), 'new_k': (1, 1, P, HEADS, 2, QKD),
         'new_v': (1, 1, P, HEADS, P), 'new_hf': (1, 1, SH, 64, P), 'new_hb': (1, 1, SH, 64, P)}
_SCRATCH = {'mods': (2, 6 * D), 'z': (TILES * P, 512), 'xbc': (TILES * P, XBC),
            'h2': (TILES * P, D), 'slots': (SLOTS, 2), 'y_slots': (SLOTS, D)}
_DEBUG = []


def shape_constants():
    i = np.arange(P)
    c = {
        'ident': np.eye(P, dtype=np.float32),
        'tri_le': (i[:, None] <= i[None, :]).astype(np.float32),
        'tri_ge': (i[:, None] >= i[None, :]).astype(np.float32),
        'tri_lt': (i[:, None] < i[None, :]).astype(np.float32),
        'pick': np.repeat(np.eye(2 * SH, dtype=np.float32)[:, :, None], P, axis=2),
    }
    c['steps'] = np.arange(BLOCKS, dtype=np.float32)
    c['tokens'] = (i[:, None] + P * np.arange(TILES)[None, :]).astype(np.float32)
    pos = np.arange(STILES * P)
    freqs = np.float32(10000.0) ** (-np.arange(16, dtype=np.float32) / np.float32(16))
    rope = np.zeros((TILES, P, 2, 2, 2, 16), np.float32)
    rope[0, :, 0] = 1.0
    for axis, ids in enumerate((pos // 64, pos % 64)):
        ang = (ids.astype(np.float32)[:, None] * freqs).reshape(STILES, P, 16)
        rope[1:, :, 0, axis, 0] = rope[1:, :, 0, axis, 1] = np.cos(ang)
        rope[1:, :, 1, axis, 0] = -np.sin(ang)
        rope[1:, :, 1, axis, 1] = np.sin(ang)
    c['rope'] = rope.reshape(TILES, P, 2, QKD)
    return c


def kernel(**inputs):
    import concourse.bacc as _bacc
    from concourse.bass_utils import run_bass_kernel_spmd as _run

    nc = _bacc.Bacc("TRN2", target_bir_lowering=False, num_devices=1)
    arrays, io = {}, {}
    for name in _INS:
        arrays[f"in_{name}"] = np.ascontiguousarray(inputs[name])
    for name, a in shape_constants().items():
        arrays[f"in_{name}"] = a
    for name, a in arrays.items():
        io[name[3:]] = nc.dram_tensor(name, a.shape, F32, kind="ExternalInput").ap()
    for name, shape in _OUTS.items():
        io[name] = nc.dram_tensor(f"out_{name}", shape, F32, kind="ExternalOutput").ap()
    scratch = {name: nc.dram_tensor(f"scratch_{name}", shape, F32,
                                    kind="ExternalOutput" if name in _DEBUG else "Internal").ap()
               for name, shape in _SCRATCH.items()}
    build(nc, io, scratch)
    r = _run(nc, [arrays], core_ids=[0])
    if _DEBUG:
        return tuple(r.results[0][f"scratch_{n}"] if n in _SCRATCH else r.results[0][f"out_{n}"] for n in _DEBUG)
    return tuple(r.results[0][f"out_{name}"] for name in _OUTS)
```

```python
import math
from contextlib import ExitStack

import numpy as np

import concourse.bass as bass
from concourse import mybir

P = 128
D = 1024
KT = D // P
TILES = 9
STILES = 8
HEADS = 4
QKD = 64
DQK = 512
DATT = 512
DSSM = 512
SH = 8
SG = 2
HG = SH // SG
XBC = 1024
NXBC = XBC // P
IN_COLS = 2 * DQK + DATT + DSSM + XBC + 2 * SH
CONV = 5
NG = 4
EPG = 4
NE = NG * EPG
FF = 256
EPS = 1e-6
LAM0 = 0.8 - 0.6 * math.exp(-0.0)
SCALE = QKD ** -0.5
BLOCKS = 2 * TILES + NE - 1
SLOTS = BLOCKS * P
CIN = 2 + P + 2 + STILES * P + 2
COUT = CIN - 4
ADA_COLS, ADA_FIRST = 512, 2 * D // 512
SHIFT1, SCALE1, GATE1, SHIFT2, SCALE2, GATE2 = range(6)

ALU = mybir.AluOpType
ACT = mybir.ActivationFunctionType
F32 = mybir.dt.float32
F32R = mybir.dt.float32r
I32 = mybir.dt.int32
U32 = mybir.dt.uint32
AX = mybir.AxisListType.X


class Scope:

    def __init__(self, nc, ctx, tag):
        self.nc, self.ctx, self.tag, self.sems = nc, ctx, tag, []
        ctx.callback(self.close)

    def sb(self, name, shape, dt=F32, side=None):
        return self.ctx.enter_context(self.nc.sbuf_tensor(f"{self.tag}_{name}", shape, dt, side=side))

    def ps(self, name, cols=512):
        return self.ctx.enter_context(self.nc.psum_tensor(f"{self.tag}_{name}_ps", [P, cols], F32))

    def sem(self, name):
        self.sems.append(self.nc.alloc_semaphore(name=f"{self.tag}_{name}"))
        return self.sems[-1]

    def close(self):
        if self.sems:
            self.nc.clear_and_free_semaphores(self.sems)
            self.nc.all_engine_barrier()


def split_low(eng, low, value, high):
    return eng.tensor_tensor(low, value, high.bitcast(F32), ALU.subtract)


def split_product(pe, out, a_high, a_low, b_high, b_low, start, stop):
    pe.matmul(out, a_high, b_high, start=start, stop=False)
    pe.matmul(out, a_high, b_low, start=False, stop=False)
    return pe.matmul(out, a_low, b_high, start=False, stop=stop)


class Step:

    def __init__(self, i, c):
        self.i, self.c = i, c
        self.buf = c % 2
        self.n = i * 2 + c if not isinstance(i, int) else 2 * i + c
        self.nth = i + c // 2

    def next(self):
        return Step(self.i, self.c + 1)


def bcast(ap, n, axis):
    shape = list(ap.shape)
    shape.insert(axis, n)
    return ap.unsqueeze(axis).to_broadcast(shape)


def row_bcast(row, n=P):
    return row.unsqueeze(0).to_broadcast([n, row.shape[0]])


def ada_stage(nc, I, C, W, M):
    NB, W_COLS, CB = 4, ADA_COLS, ADA_FIRST
    w_ada = I["w_ada"][0].rearrange("(p j) n -> p j n", j=KT)
    with ExitStack() as ctx:
        s = Scope(nc, ctx, "ada")
        raw, cond = s.sb("raw", [P, 2, KT]), C["cond"]
        w = s.sb("w", [P, NB, KT, W_COLS])
        rows = s.sb("rows", [2, CB * W_COLS])
        acc = [s.ps(f"acc{u}") for u in range(NB)]
        in_sem, w_ada_in = s.sem("cond_in"), [s.sem(f"w_ada_in{u}") for u in range(NB)]
        silu_done = s.sem("silu_done")
        mm_done, row_done, stored = s.sem("mm_done"), s.sem("row_done"), s.sem("stored")
        block = ctx.enter_context(nc.Block())

        @block.sync
        def _(sp):
            sp.dma_start(raw[:, 0], I["c_ctx"].rearrange("(p j) -> p j", j=KT)).then_inc(in_sem, 16)
            sp.dma_start(raw[:, 1], I["c"][0].rearrange("(p j) -> p j", j=KT)).then_inc(in_sem, 16)
            sp.dma_start(rows[:], row_bcast(I["b_ada"][0, 0:CB * W_COLS], 2)).then_inc(in_sem, 16)
            for u in range(NB):
                sp.dma_start(w[:, u], w_ada[:, :, u * W_COLS:(u + 1) * W_COLS]).then_inc(w_ada_in[u], 16)
            load_w_in(sp, I, W, 0)

        @block.scalar
        def _(act):
            act.wait_ge(in_sem, 48)
            act.activation(cond[:].rearrange("p k c -> p c k"), raw[:], ACT.Silu).then_inc(silu_done, 1)
            act.wait_ge(row_done, CB)
            act.dma_start(M["mods"][:, 0:CB * W_COLS], rows[:]).then_inc(stored, 16)
            act.wait_ge(stored, 16)

        @block.tensor
        def _(pe):
            pe.wait_ge(silu_done, 1)
            for u in range(NB):
                pe.wait_ge(w_ada_in[u], 16)
                for k in range(KT):
                    mm = pe.matmul(acc[u][0:2, :], cond[:, k, :], w[:, u, k, :], start=(k == 0), stop=(k == KT - 1))
                mm.then_inc(mm_done, 1)

        @block.vector
        def _(dve):
            dve.wait_ge(in_sem, 48)
            for u in range(NB):
                dve.wait_ge(mm_done, u + 1)
                cols = rows[:, u * W_COLS:(u + 1) * W_COLS]
                dve.tensor_tensor(cols, acc[u][0:2, :], cols, ALU.add).then_inc(row_done, 1)


def load_w_in(sp, I, W, b):
    cols = slice(b * 512, (b + 1) * 512 if b < len(W["w_in_sems"]) - 1 else IN_COLS)
    sp.dma_start(W["w_in"][:, :, cols], I["w_in"][0].rearrange("(k p) n -> p k n", p=P)[:, :, cols]
                 ).then_inc(W["w_in_sems"][b], 16)


def projection_stage(nc, I, C, W, M):
    with ExitStack() as ctx:
        s = Scope(nc, ctx, "proj")
        amul, aadd = s.sb("amul", [P, 2, D]), s.sb("aadd", [P, 2, D])
        rope = s.sb("rope", [P, 2, 2, QKD])
        x = s.sb("x", [P, 2, D])
        h = s.sb("h", [P, 2, D])
        gain = h[:, 0]
        hT = s.sb("hT", [P, 2, KT, P])
        stage = s.sb("stage", [P, 3, 512])
        q_out, k_rot = s.sb("q_out", [P, 512]), s.sb("k_rot", [P, 512])
        swap = W["kT"][:, :, TILES * P:(TILES + 1) * P]
        ssq, std, rstd = s.sb("ssq", [P, 2]), s.sb("std", [P, 2]), s.sb("rstd", [P, 2])
        epsc = s.sb("epsc", [P, 1])
        turned = s.ps("turned", 1024)
        acc = [s.ps(f"acc{u}") for u in range(4)]
        k_turned = s.ps("k_turned")
        dt_acc = s.ps("dt_acc")
        w_in = W["w_in"]

        mods_in, x_in, rope_in = s.sem("mods_in"), [s.sem(f"x_in{u}") for u in range(2)], [s.sem(f"rope_in{u}") for u in range(2)]
        mods_done, std_done, h_done = s.sem("mods_done"), s.sem("std_done"), s.sem("h_done")
        turn_done, hT_done = s.sem("turn_done"), s.sem("hT_done")
        acc_done = [s.sem(f"acc_done{u}") for u in range(4)]
        acc_read = [s.sem(f"acc_read{u}") for u in range(4)]
        dt_done, dt_read = s.sem("dt_done"), s.sem("dt_read")
        q_rot_done, q_turn_done, qT_done = s.sem("q_rot_done"), s.sem("q_turn_done"), s.sem("qT_done")
        k_rot_done, k_turn_done, kT_done = s.sem("k_rot_done"), s.sem("k_turn_done"), s.sem("kT_done")
        staged, stored = [s.sem(f"staged{u}") for u in range(3)], [s.sem(f"stored{u}") for u in range(3)]
        ctx_in, ctx_kin, new_stored = s.sem("ctx_in"), s.sem("ctx_kin"), [s.sem(f"new_stored{u}") for u in range(2)]
        block = ctx.enter_context(nc.Block())
        qT, kT, v_tok, dt_tok = W["qT"], W["kT"], W["v_tok"], W["dt_tok"]
        Q, K, V, Z, X0, X1 = range(6)
        BANK = {Q: 0, K: 1, V: 2, Z: 3, X0: 0, X1: 1}

        @block.sync
        def _(sp):
            def load(t, src):
                sp.wait_ge(h_done, t.n + 1)
                sp.dma_start(x[:, t.buf], src).then_inc(x_in[t.buf], 16)
                sp.wait_ge(k_rot_done, t.n + 1)
                sp.dma_start(rope[:, t.buf], I["rope"][t.n]).then_inc(rope_in[t.buf], 16)

            def sample_rows(t):
                return I["x_sample"][0, bass.ds((t.n - 1) * P, P), :]

            def store(t):
                for u, dst in ((0, M["z"][bass.ds(t.n * P, P), :]), (1, M["xbc"][bass.ds(t.n * P, P), 0:512]),
                               (2, M["xbc"][bass.ds(t.n * P, P), 512:1024])):
                    sp.wait_ge(staged[u], t.n + 2)
                    sp.dma_start(dst, stage[:, u]).then_inc(stored[u], 16)

            load(Step(0, 0), I["x_prompt"][0])
            sp.wait_ge(mods_in, 80)
            for b in range(1, len(W["w_in_sems"])):
                load_w_in(sp, I, W, b)
                if b == 2:
                    load(Step(0, 1), sample_rows(Step(0, 1)))
            load(Step(0, 2), sample_rows(Step(0, 2)))
            sp.wait_ge(k_rot_done, 3)
            sp.dma_start(I["new_k"][0, 0].rearrange("t h m d -> t (h m d)"), k_rot[:]).then_inc(new_stored[0], 16)
            sp.wait_ge(staged[0], 2)
            sp.dma_start(I["new_v"][0, 0].rearrange("t h d -> t (h d)"), v_tok[:, 0, :]).then_inc(new_stored[1], 16)
            store(Step(0, 0))
            with sp.Fori(0, STILES // 2 - 1) as i:
                for c in (1, 2):
                    load(Step(i, c + 2), sample_rows(Step(i, c + 2)))
                    store(Step(i, c))
            store(Step(0, TILES - 2))
            store(Step(0, TILES - 1))
            sp.wait_ge(kT_done, TILES + 1)
            sp.dma_start(k_rot[:], I["cache_k"][0, 0].rearrange("t h m d -> t (h m d)")).then_inc(ctx_kin, 16)
            sp.dma_start(v_tok[:, TILES, :], I["cache_v"][0, 0].rearrange("t h d -> t (h d)")).then_inc(ctx_in, 16)
            sp.wait_ge(ctx_in, 16)
            for u in range(3):
                sp.wait_ge(stored[u], 16 * (TILES + 1))
            for u in range(2):
                sp.wait_ge(new_stored[u], 16)

        @block.scalar
        def _(act):
            for cond in range(2):
                act.dma_start(amul[:, cond], row_bcast(M["mods"][cond, SCALE1 * D:(SCALE1 + 1) * D])).then_inc(mods_in, 16)
                act.dma_start(aadd[:, cond], row_bcast(M["mods"][cond, SHIFT1 * D:(SHIFT1 + 1) * D])).then_inc(mods_in, 16)
            act.dma_start(gain, row_bcast(I["norm_mix_g"][0])).then_inc(mods_in, 16)
            for u in range(3):
                act.sem_inc(staged[u], 1)
                act.sem_inc(stored[u], 16)
            act.sem_inc(acc_read[2], 1)
            act.sem_inc(hT_done, 1)

            def norm(t):
                act.wait_ge(x_in[t.buf], t.nth * 16 + 16)
                act.wait_ge(turn_done, t.n + 1)
                act.activation(h[:, t.buf], x[:, t.buf], ACT.Square, accum_out=ssq[:, t.buf:t.buf + 1])
                act.drain()
                act.activation(std[:, t.buf:t.buf + 1], ssq[:, t.buf:t.buf + 1], ACT.Sqrt, bias=epsc[:, 0:1],
                               scale=1.0 / D).then_inc(std_done, 1)

            def turn_out(t):
                act.wait_ge(turn_done, t.n + 3)
                act.wait_ge(dt_done, t.n + 1)
                act.copy(hT[:, t.buf].rearrange("p k t -> p (k t)"), turned[:]).then_inc(hT_done, 1)

            def out(t):
                act.wait_ge(acc_done[2], t.n + 1)
                act.copy(v_tok[:, t.n, :], acc[2][:]).then_inc(acc_read[2], 1)
                act.wait_ge(acc_done[3], t.n + 1)
                act.wait_ge(stored[0], t.n * 16 + 16)
                act.copy(stage[:, 0], acc[3][:]).then_inc(staged[0], 1)
                act.wait_ge(acc_done[0], t.n * 2 + 2)
                act.wait_ge(stored[1], t.n * 16 + 16)
                act.copy(stage[:, 1], acc[0][:]).then_inc(staged[1], 1)
                act.wait_ge(acc_done[1], t.n * 2 + 2)
                act.wait_ge(stored[2], t.n * 16 + 16)
                act.copy(stage[:, 2], acc[1][:]).then_inc(staged[2], 1)

            act.wait_ge(mods_done, 1)
            norm(Step(0, 0))
            turn_out(Step(0, 0))
            norm(Step(0, 1))
            turn_out(Step(0, 1))
            out(Step(0, 0))
            with act.Fori(0, STILES // 2 - 1) as i:
                for c in (1, 2):
                    norm(Step(i, c + 1))
                    turn_out(Step(i, c + 1))
                    out(Step(i, c))
            norm(Step(0, TILES - 1))
            turn_out(Step(0, TILES - 1))
            out(Step(0, TILES - 2))
            out(Step(0, TILES - 1))

        @block.vector
        def _(dve):
            dve.memset(epsc[:], EPS)
            dve.wait_ge(mods_in, 80)
            for cond in range(2):
                op = dve.scalar_tensor_tensor(out=amul[:, cond], in0=amul[:, cond], scalar=1.0, in1=gain,
                                              op0=ALU.add, op1=ALU.mult)
            op.then_inc(mods_done, 1)
            dve.wait_ge(mods_done, 1)
            dve.sem_inc(h_done, 2)
            dve.sem_inc(k_rot_done, 2)
            dve.sem_inc(kT_done, 1)
            dve.sem_inc(q_rot_done, 1)
            dve.sem_inc(dt_read, 1)

            def norm(t, cond):
                dve.wait_ge(std_done, t.n + 1)
                r = rstd[:, t.buf:t.buf + 1]
                dve.reciprocal(r, std[:, t.buf:t.buf + 1])
                dve.drain()
                dve.scalar_tensor_tensor(out=h[:, t.buf], in0=x[:, t.buf], scalar=r, in1=amul[:, cond],
                                         op0=ALU.mult, op1=ALU.mult)
                dve.drain()
                dve.tensor_tensor(h[:, t.buf], h[:, t.buf], aadd[:, cond], ALU.add).then_inc(h_done, 1)

            def rotate(dst, src, t, done):
                cos = bcast(rope[:, t.buf, 0, :], 8, 1)
                sin = rope[:, t.buf, 1, :].rearrange("p (a s f) -> p a s f", a=2, s=2)
                v = src.rearrange("p (h m a s f) -> p h m a s f", h=HEADS, m=2, a=2, s=2)
                w = swap.rearrange("p h (m a s f) -> p h m a s f", m=2, a=2, s=2)
                for half in range(2):
                    for axis in range(2):
                        dve.tensor_tensor(w[:, :, :, axis, half, :], v[:, :, :, axis, 1 - half, :],
                                          bcast(bcast(sin[:, axis, half, :], 2, 1), HEADS, 1), ALU.mult)
                dve.tensor_tensor(dst.rearrange("p (g f) -> p g f", g=8), src.rearrange("p (g f) -> p g f", g=8),
                                  cos, ALU.mult)
                dve.drain()
                dve.tensor_tensor(dst.rearrange("p (h d) -> p h d", h=HEADS), dst.rearrange("p (h d) -> p h d", h=HEADS), swap,
                                  ALU.add).then_inc(done, 1)
                dve.drain()

            def out(t):
                dve.wait_ge(rope_in[t.buf], t.nth * 16 + 16)
                dve.wait_ge(acc_done[0], t.n * 2 + 1)
                dve.wait_ge(q_turn_done, t.n + 1)
                rotate(q_out[:], acc[0][:], t, q_rot_done)
                dve.wait_ge(q_turn_done, t.n + 2)
                dve.tensor_copy(qT[:, :, bass.ds(t.n * P, P)], k_turned[:].rearrange("p (h t) -> p h t", h=HEADS)).then_inc(qT_done, 1)
                dve.wait_ge(acc_done[1], t.n * 2 + 1)
                dve.wait_ge(k_turn_done, t.n + 1)
                rotate(k_rot[:], acc[1][:], t, k_rot_done)
                dve.wait_ge(k_turn_done, t.n + 2)
                dve.tensor_copy(kT[:, :, bass.ds(t.n * P, P)], k_turned[:].rearrange("p (h t) -> p h t", h=HEADS)).then_inc(kT_done, 1)
                dve.wait_ge(dt_done, t.n + 3)
                dve.tensor_copy(dt_tok[:, t.n, :], dt_acc[:, 0:2 * SH]).then_inc(dt_read, 1)

            norm(Step(0, 0), 0)
            norm(Step(0, 1), 1)
            out(Step(0, 0))
            dve.wait_ge(new_stored[0], 16)
            with dve.Fori(0, STILES // 2 - 1) as i:
                for c in (1, 2):
                    norm(Step(i, c + 1), 1)
                    out(Step(i, c))
            norm(Step(0, TILES - 1), 1)
            out(Step(0, TILES - 2))
            out(Step(0, TILES - 1))
            dve.wait_ge(k_turn_done, TILES + 2)
            dve.tensor_copy(kT[:, :, TILES * P:(TILES + 1) * P], k_turned[:].rearrange("p (h t) -> p h t", h=HEADS)).then_inc(kT_done, 1)

        @block.tensor
        def _(pe):
            ident = C["ident"]
            pe.sem_inc(turn_done, 2)
            pe.sem_inc(dt_done, 2)
            pe.sem_inc(k_turn_done, 1)
            pe.sem_inc(q_turn_done, 1)

            def turn(t):
                pe.wait_ge(h_done, t.n + 3)
                pe.wait_ge(hT_done, t.n + 1)
                for k in range(KT):
                    mm = pe.transpose(turned[:, k * P:(k + 1) * P], h[:, t.buf, k * P:(k + 1) * P], ident[:])
                mm.then_inc(turn_done, 1)

            def product(t, b):
                if isinstance(t.n, int) and t.n == 0:
                    pe.wait_ge(W["w_in_sems"][b], 16)
                for k in range(KT):
                    mm = pe.matmul(acc[BANK[b]][:], hT[:, t.buf, k, :], w_in[:, k, b * 512:(b + 1) * 512],
                                   start=(k == 0), stop=(k == KT - 1))
                mm.then_inc(acc_done[BANK[b]], 1)

            def products(t, turn_next):
                pe.wait_ge(hT_done, t.n + 2)
                pe.wait_ge(staged[1], t.n + 1)
                product(t, Q)
                pe.wait_ge(staged[2], t.n + 1)
                product(t, K)
                if turn_next:
                    turn(t.next())
                pe.wait_ge(acc_read[2], t.n + 1)
                product(t, V)
                pe.wait_ge(staged[0], t.n + 1)
                product(t, Z)
                pe.wait_ge(q_rot_done, t.n + 2)
                pe.wait_ge(kT_done, t.n + 1)
                for hd in range(HEADS):
                    mm = pe.transpose(k_turned[:, hd * P:(hd + 1) * P], q_out[:, hd * P:(hd + 1) * P], ident[:])
                mm.then_inc(q_turn_done, 1)
                product(t, X0)
                pe.wait_ge(k_rot_done, t.n + 3)
                pe.wait_ge(qT_done, t.n + 1)
                for hd in range(HEADS):
                    mm = pe.transpose(k_turned[:, hd * P:(hd + 1) * P], k_rot[:, hd * P:(hd + 1) * P], ident[:])
                mm.then_inc(k_turn_done, 1)
                product(t, X1)
                pe.wait_ge(dt_read, t.n + 1)
                for k in range(KT):
                    mm = pe.matmul(dt_acc[:, 0:2 * SH], hT[:, t.buf, k, :], w_in[:, k, 3072:IN_COLS],
                                   start=(k == 0), stop=(k == KT - 1))
                mm.then_inc(dt_done, 1)

            turn(Step(0, 0))
            products(Step(0, 0), True)
            with pe.Fori(0, STILES // 2 - 1) as i:
                for c in (1, 2):
                    products(Step(i, c), True)
            products(Step(0, TILES - 2), True)
            products(Step(0, TILES - 1), False)
            pe.wait_ge(ctx_kin, 16)
            pe.wait_ge(kT_done, TILES + 1)
            for hd in range(HEADS):
                mm = pe.transpose(k_turned[:, hd * P:(hd + 1) * P], k_rot[:, hd * P:(hd + 1) * P], ident[:])
            mm.then_inc(k_turn_done, 1)


def conv_stage(nc, I, C, W, M):
    assert NXBC == 6 * D // ADA_COLS - ADA_FIRST
    w_ada = I["w_ada"][0].rearrange("(p j) n -> p j n", j=KT)
    w = W
    with ExitStack() as ctx:
        s = Scope(nc, ctx, "conv")
        dt_bias, a_neg = s.sb("dt_bias", [P, 2 * SH]), s.sb("a_neg", [P, 2 * SH])
        d_row = s.sb("d_row", [P, SH])
        taps = s.sb("taps", [P, NXBC, CONV + 1])
        ones = s.sb("ones", [P, P])
        t1, t2, t3, t4 = (s.sb(f"t{i}", [P, TILES, 2 * SH]) for i in range(4))
        la = s.sb("la", [P, TILES, 2 * SH])
        raw = s.sb("raw", [P, 2, TILES, P])
        xin = s.sb("xin", [P, 2, CIN])
        acc = s.sb("acc", [P, 2, COUT])
        taps_row = acc[0:CONV + 1, 0, 0:XBC]
        wa, rows = s.sb("wa", [P, 2, KT, ADA_COLS]), s.sb("rows", [2, 2, ADA_COLS])
        turned_in, turned_out = s.ps("turned_in", 1536), s.ps("turned_out", 1536)
        sums, row_ps = s.ps("sums"), s.ps("row")
        wa_in, row_stored = [s.sem(f"wa_in{u}") for u in range(2)], [s.sem(f"row_stored{u}") for u in range(2)]
        row_mm, row_done = s.sem("row_mm"), s.sem("row_done")
        small_in, raw_in = s.sem("small_in"), [s.sem(f"raw_in{u}") for u in range(2)]
        exp_done, ln_done, a_done, pre_done = s.sem("exp_done"), s.sem("ln_done"), s.sem("a_done"), s.sem("pre_done")
        la_done, sums_done, cum_done, expo_done = s.sem("la_done"), s.sem("sums_done"), s.sem("cum_done"), s.sem("expo_done")
        taps_turned, taps_done = s.sem("taps_turned"), s.sem("taps_done")
        cumT_turned, cumT_done = s.sem("cumT_turned"), s.sem("cumT_done")
        zeroed, turn_done, xin_done = s.sem("zeroed"), s.sem("turn_done"), s.sem("xin_done")
        acc_done, smooth_done, back_done, tok_done = s.sem("acc_done"), s.sem("smooth_done"), s.sem("back_done"), s.sem("tok_done")
        kept, skip_done = s.sem("kept"), s.sem("skip_done")
        block = ctx.enter_context(nc.Block())
        tok, xbcT, y_tok, dt_tok = w["tok"], w["xbcT"], w["y_tok"], w["dt_tok"]
        cum, tot, ecum, dte, dec, cumT = (w[k] for k in ("cum", "tot", "ecum", "dte", "dec", "cumT"))
        xbc_dram = M["xbc"].rearrange("(t p) c -> p t c", p=P)

        def slices(eng, first, body):
            first(Step(0, 0))
            with eng.Fori(0, NXBC // 2 - 1) as i:
                body(Step(i, 0), True)
                body(Step(i, 1), True)
            body(Step(NXBC // 2 - 1, 0), True)
            body(Step(NXBC // 2 - 1, 1), False)

        @block.sync
        def _(sp):
            for half, (bias, alog) in enumerate((("dt_bias_fwd", "a_log_fwd"), ("dt_bias_bwd", "a_log_bwd"))):
                sp.dma_start(dt_bias[:, half * SH:(half + 1) * SH], row_bcast(I[bias][0])).then_inc(small_in, 16)
                sp.dma_start(a_neg[:, half * SH:(half + 1) * SH], row_bcast(I[alog][0])).then_inc(small_in, 16)
            sp.dma_start(d_row[:], row_bcast(I["ssm_d"][0])).then_inc(small_in, 16)
            sp.dma_start(taps_row[0:CONV, :], I["conv_w"][0]).then_inc(small_in, 16)
            sp.dma_start(taps_row[CONV:CONV + 1, :], I["conv_b"]).then_inc(small_in, 16)

            def load_raw(t):
                sp.dma_start(raw[:, t.buf], xbc_dram[:, :, bass.ds(t.n * P, P)]).then_inc(raw_in[t.buf], 16)

            def load_ada(t):
                sp.dma_start(wa[:, t.buf], w_ada[:, :, bass.ds((t.n + ADA_FIRST) * ADA_COLS, ADA_COLS)]).then_inc(wa_in[t.buf], 16)

            def load_bias(t):
                sp.dma_start(rows[:, t.buf], row_bcast(I["b_ada"][0, bass.ds((t.n + ADA_FIRST) * ADA_COLS, ADA_COLS)], 2)
                             ).then_inc(wa_in[t.buf], 16)

            def store_row(t):
                sp.wait_ge(row_done, t.n + 2)
                sp.dma_start(M["mods"][:, bass.ds((t.n + ADA_FIRST) * ADA_COLS, ADA_COLS)], rows[:, t.buf]
                             ).then_inc(row_stored[t.buf], 16)

            for c in range(2):
                load_raw(Step(0, c))
                load_ada(Step(0, c))
                load_bias(Step(0, c))
            with sp.Fori(0, NXBC // 2 - 1) as i:
                for c in range(2):
                    t, later = Step(i, c), Step(i, c + 2)
                    sp.wait_ge(turn_done, t.n + 1)
                    load_raw(later)
                    sp.wait_ge(row_mm, t.n + 1)
                    load_ada(later)
                    store_row(t)
                    sp.wait_ge(row_stored[t.buf], t.nth * 16 + 16)
                    load_bias(later)
            for c in range(2):
                store_row(Step(NXBC // 2 - 1, c))
            for c in range(2):
                sp.wait_ge(row_stored[c], 16 * NXBC // 2)

        @block.gpsimd
        def _(pool):
            pool.memset(ones[:], 1.0).then_inc(zeroed, 1)
            pool.memset(xin[:], 0.0).then_inc(zeroed, 1)
            pool.sem_inc(kept, 2 + 4)
            with pool.Fori(0, 2) as i:
                for u in range(2):
                    pool.wait_ge(smooth_done, i * 2 + (u + 7))
                    pool.tensor_copy(xbcT[:, i * 2 + u, :], acc[:, u]).then_inc(kept, 1)
            pool.wait_ge(tok_done, NXBC + 1)
            xs = tok[:, :, 0:DSSM].rearrange("p t (h d) -> p t h d", h=SH)
            for t in range(3):
                r = slice(3 * t, 3 * t + 3)
                pool.tensor_tensor(y_tok[:, r].rearrange("p t (h d) -> p t h d", h=SH), xs[:, r],
                                   bcast(bcast(d_row[:], 64, 2), 3, 1), ALU.mult).then_inc(skip_done, 1)
            pool.wait_ge(skip_done, 3)

        @block.scalar
        def _(act):
            act.wait_ge(small_in, 16 * 7)
            act.activation(a_neg[:], a_neg[:], ACT.Exp).then_inc(a_done, 1)
            act.wait_ge(pre_done, 1)
            act.activation(t2[:], t2[:], ACT.Exp).then_inc(exp_done, 1)
            act.wait_ge(pre_done, 2)
            act.activation(t4[:], t3[:], ACT.Ln).then_inc(ln_done, 1)
            act.wait_ge(cum_done, 1)
            act.activation(ecum[:], cum[:], ACT.Exp)
            act.activation(dec[:], tot[:], ACT.Exp)
            act.activation(t1[:], t1[:], ACT.Exp).then_inc(expo_done, 1)
            act.wait_ge(cumT_turned, 1)
            act.copy(cumT[:], turned_out[0:2 * SH, 0:TILES * P]).then_inc(cumT_done, 1)
            act.sem_inc(xin_done, 1)
            act.sem_inc(smooth_done, 2)
            act.sem_inc(tok_done, 1)
            act.wait_ge(zeroed, 2)

            def take_in(t):
                act.wait_ge(turn_done, t.n + 1)
                act.wait_ge(acc_done, t.n + 1)
                act.copy(xin[:, t.buf, 2:2 + P], turned_in[:, 0:P])
                act.copy(xin[:, t.buf, 4 + P:4 + TILES * P], turned_in[:, P:TILES * P]).then_inc(xin_done, 1)

            def body(t, more):
                if more:
                    take_in(t.next())
                act.wait_ge(acc_done, t.n + 3)
                act.activation(acc[:, t.buf], acc[:, t.buf], ACT.Silu).then_inc(smooth_done, 1)
                act.wait_ge(back_done, t.n + 3)
                act.copy(tok[:, :, bass.ds(t.n * P, P)],
                         turned_out[:, 0:TILES * P].rearrange("p (t c) -> p t c", t=TILES)).then_inc(tok_done, 1)
            slices(act, take_in, body)

        @block.vector
        def _(dve):
            dve.sem_inc(acc_done, 2)
            dve.sem_inc(row_done, 1)
            dve.wait_ge(small_in, 16 * 7)
            dve.tensor_tensor(t1[:], dt_tok[:], bcast(dt_bias[:], TILES, 1), ALU.add)
            dve.drain()
            dve.tensor_scalar(t3[:], t1[:], -1.0, None, ALU.mult)
            dve.drain()
            dve.tensor_tensor(t2[:], t1[:], t3[:], ALU.min).then_inc(pre_done, 1)
            dve.wait_ge(exp_done, 1)
            dve.tensor_scalar(t3[:], t2[:], 1.0, None, ALU.add).then_inc(pre_done, 1)
            dve.tensor_scalar(t1[:], t1[:], 0.0, None, ALU.max)
            dve.wait_ge(ln_done, 1)
            dve.tensor_scalar(la[:], t3[:], 1.0, None, ALU.is_equal)
            dve.drain()
            dve.scalar_tensor_tensor(out=t3[:], in0=t3[:], scalar=-1.0, in1=la[:], op0=ALU.add, op1=ALU.add)
            dve.tensor_tensor(t4[:], t4[:], la[:], ALU.add)
            dve.drain()
            dve.reciprocal(t3[:], t3[:])
            dve.tensor_tensor(t4[:], t4[:], t2[:], ALU.mult)
            dve.drain()
            dve.tensor_tensor(t4[:], t4[:], t3[:], ALU.mult)
            dve.drain()
            dve.tensor_tensor(dt_tok[:], t1[:], t4[:], ALU.add)
            dve.drain()
            dve.wait_ge(a_done, 1)
            dve.scalar_tensor_tensor(out=la[:], in0=dt_tok[:], scalar=-1.0, in1=bcast(a_neg[:], TILES, 1),
                                     op0=ALU.mult, op1=ALU.mult).then_inc(la_done, 1)
            dve.wait_ge(sums_done, 1)
            n = TILES * SH
            for half in range(2):
                dve.tensor_copy(cum[:, :, half * SH:(half + 1) * SH],
                                sums[:, half * n:(half + 1) * n].rearrange("p (t h) -> p t h", t=TILES))
            dve.tensor_copy(tot[:], sums[:, 2 * n:4 * n].rearrange("p (t h) -> p t h", t=TILES))
            dve.drain()
            dve.tensor_tensor(t1[:], tot[:], cum[:], ALU.subtract).then_inc(cum_done, 1)
            dve.wait_ge(expo_done, 1)
            dve.tensor_tensor(dte[:], dt_tok[:], t1[:], ALU.mult)
            dve.wait_ge(taps_turned, 1)
            dve.tensor_copy(taps[:], turned_in[:, 0:NXBC * (CONV + 1)].rearrange("p (c k) -> p c k", c=NXBC)).then_inc(taps_done, 1)
            dve.wait_ge(taps_done, 1)

            def body(t, more):
                dve.wait_ge(xin_done, t.n + 2)
                dve.wait_ge(back_done, t.n + 1)
                dve.wait_ge(kept, t.n + 1)
                out, ct = acc[:, t.buf], t.n
                dve.tensor_scalar(out, xin[:, t.buf, 0:COUT], taps[:, ct, 0:1], taps[:, ct, CONV:CONV + 1], ALU.mult, ALU.add)
                for k in range(1, CONV):
                    dve.drain()
                    op = dve.scalar_tensor_tensor(out=out, in0=xin[:, t.buf, k:k + COUT], scalar=taps[:, ct, k:k + 1],
                                                  in1=out, op0=ALU.mult, op1=ALU.add)
                op.then_inc(acc_done, 1)
                dve.wait_ge(row_mm, t.n + 1)
                dve.wait_ge(wa_in[t.buf], t.nth * 32 + 32)
                dve.tensor_tensor(rows[:, t.buf], row_ps[0:2, :], rows[:, t.buf], ALU.add).then_inc(row_done, 1)
            slices(dve, lambda t: None, body)

        @block.tensor
        def _(pe):
            ident = C["ident"]
            pe.wait_ge(small_in, 16 * 7)
            for c in range(NXBC):
                mm = pe.transpose(turned_in[:, c * (CONV + 1):(c + 1) * (CONV + 1)], taps_row[:, c * P:(c + 1) * P],
                                  ident[0:CONV + 1, 0:CONV + 1])
            mm.then_inc(taps_turned, 1)
            pe.wait_ge(la_done, 1)
            pe.wait_ge(zeroed, 1)
            n = TILES * SH
            pe.matmul(sums[:, 0:n], C["tri_le"][:], la[:, :, 0:SH], start=True, stop=True)
            pe.matmul(sums[:, n:2 * n], C["tri_ge"][:], la[:, :, SH:2 * SH], start=True, stop=True)
            pe.matmul(sums[:, 2 * n:4 * n], ones[:], la[:], start=True, stop=True).then_inc(sums_done, 1)
            pe.wait_ge(cum_done, 1)
            for t in range(TILES):
                mm = pe.transpose(turned_out[0:2 * SH, t * P:(t + 1) * P], cum[:, t, :], ident[:])
            mm.then_inc(cumT_turned, 1)
            pe.wait_ge(cumT_done, 1)
            pe.wait_ge(taps_done, 1)
            pe.sem_inc(back_done, 2)

            def turn_in(t):
                pe.wait_ge(raw_in[t.buf], t.nth * 16 + 16)
                pe.wait_ge(xin_done, t.n + 1)
                for k in range(TILES):
                    mm = pe.transpose(turned_in[:, k * P:(k + 1) * P], raw[:, t.buf, k, :], ident[:])
                mm.then_inc(turn_done, 1)

            def body(t, more):
                if more:
                    turn_in(t.next())
                pe.wait_ge(wa_in[t.buf], t.nth * 32 + 32)
                pe.wait_ge(row_done, t.n + 1)
                for k in range(KT):
                    mm = pe.matmul(row_ps[0:2, :], C["cond"][:, k, :], wa[:, t.buf, k, :], start=(k == 0), stop=(k == KT - 1))
                mm.then_inc(row_mm, 1)
                pe.wait_ge(smooth_done, t.n + 3)
                pe.wait_ge(tok_done, t.n + 1)
                for k in range(TILES):
                    col = 0 if k == 0 else 2 + k * P
                    mm = pe.transpose(turned_out[:, k * P:(k + 1) * P], acc[:, t.buf, col:col + P], ident[:])
                mm.then_inc(back_done, 1)
            slices(pe, turn_in, body)


class ScanStep:

    def __init__(self, i, c):
        self.i, self.c = i, c
        self.n = i * 4 + c
        self.d, self.buf = c % 2, c % 4
        self.pair = i * 2 + c // 2

    def next(self):
        return ScanStep(self.i, self.c + 1)

    def last(self):
        return ScanStep(self.i, self.c - 1)


def ssd_stage(nc, I, C, W, tag, pairs, tiles_of, col_of):
    STEPS = 2 * pairs
    w = W
    with ExitStack() as ctx:
        s = Scope(nc, ctx, tag)
        bc, bt = s.sb("bc", [P, 4, 4, P]), s.sb("bt", [P, 4, SG * P])
        xd, xe = s.sb("xd", [P, 4, DSSM]), s.sb("xe", [P, 4, DSSM])
        sdec = s.sb("sdec", [P, 2, DSSM])
        sc, gm = s.sb("sc", [P, 2, SH * P]), s.sb("gm", [P, 2, SG * P])
        yo = s.sb("yo", [P, DSSM])
        cum_ps = [s.ps(f"cum{d}", SH * P) for d in range(2)]
        g_ps, o_ps, y_ps, s_ps = s.ps("g"), s.ps("o"), s.ps("y"), s.ps("s")
        bc_done, x_done, sdec_done = s.sem("bc_done"), s.sem("x_done"), s.sem("sdec_done")
        cumb_done, g_done, o_done, s_done, y_done = (s.sem(k) for k in ("cumb_done", "g_done", "o_done", "s_done", "y_done"))
        seg_done, exp_done, gm_done, sc_done = (s.sem(k) for k in ("seg_done", "exp_done", "gm_done", "sc_done"))
        yo_done, state_done, yadd_done = s.sem("yo_done"), s.sem("state_done"), s.sem("yadd_done")
        block = ctx.enter_context(nc.Block())
        tok, xbcT, y_tok, dt_tok, state, pick = (w[k] for k in ("tok", "xbcT", "y_tok", "dt_tok", "state", "pick"))
        cum, ecum, dte, dec, cumT = (w[k] for k in ("cum", "ecum", "dte", "dec", "cumT"))
        mask = (C["tri_le"], C["tri_ge"])

        def heads(ap):
            return ap.rearrange("p (h d) -> p h d", h=SH)

        def place(k):
            return k.n, k.d, k.buf, tiles_of(k.pair, k.d), slice(k.d * SH, (k.d + 1) * SH)

        def steps(eng, first, body):
            first(ScanStep(0, 0))
            body(ScanStep(0, 0), False, True)
            if STEPS > 4:
                assert STEPS % 4 == 0
                with eng.Fori(0, STEPS // 4 - 1) as i:
                    for c in range(1, 5):
                        body(ScanStep(i, c), True, True)
            for n in range((STEPS - 1) // 4 * 4 + 1, STEPS):
                body(ScanStep(0, n), True, n < STEPS - 1)

        @block.gpsimd
        def _(pool):
            def body(k, before, after):
                n, d, b, t, h = place(k)
                pool.wait_ge(y_done, n + 1)
                xs = heads(tok[:, t, 0:DSSM])
                pool.tensor_tensor(heads(xd[:, b]), xs, bcast(dt_tok[:, t, h], 64, 2), ALU.mult)
                pool.tensor_tensor(heads(xe[:, b]), xs, bcast(dte[:, t, h], 64, 2), ALU.mult).then_inc(x_done, 1)
                pool.wait_ge(state_done, n + 1)
                pool.tensor_tensor(heads(sdec[:, d]), heads(state[:, d]), bcast(dec[:, t, h], 64, 2),
                                   ALU.mult).then_inc(sdec_done, 1)
            steps(pool, lambda k: None, body)

        @block.scalar
        def _(act):
            def bring(k):
                n, d, b, t, h = place(k)
                act.wait_ge(s_done, n + 1)
                act.copy(bc[:, b], xbcT[:, :, bass.ds(col_of(k.pair, d), P)])
                act.copy(bt[:, b], tok[:, t, DSSM:DSSM + SG * P]).then_inc(bc_done, 1)

            def body(k, before, after):
                if after:
                    bring(k.next())
                act.wait_ge(seg_done, k.n + 3)
                act.activation(sc[:, k.d], sc[:, k.d], ACT.Exp).then_inc(exp_done, 1)
            steps(act, bring, body)

        @block.vector
        def _(dve):
            dve.sem_inc(seg_done, 2)
            dve.sem_inc(gm_done, 1)
            dve.sem_inc(yo_done, 1)
            dve.sem_inc(state_done, 2)
            dve.sem_inc(yadd_done, 1)

            def segments(k):
                n, d, b, t, _ = place(k)
                dve.drain()
                dve.wait_ge(cumb_done, n + 1)
                dve.wait_ge(y_done, n + 3)
                for h in range(SH):
                    op = dve.tensor_scalar(sc[:, d, h * P:(h + 1) * P], cum_ps[d][:, h * P:(h + 1) * P],
                                           cum[:, t, d * SH + h:d * SH + h + 1], 0.0, ALU.subtract, ALU.min)
                op.then_inc(seg_done, 1)
                dve.wait_ge(g_done, n + 1)
                dve.tensor_tensor(gm[:, d].rearrange("p (g i) -> p g i", g=SG), g_ps[:, 0:SG * P].rearrange("p (g i) -> p g i", g=SG),
                                  bcast(mask[d][:], SG, 1), ALU.mult).then_inc(gm_done, 1)

            def carried(k):
                n, d, b, t, h = place(k)
                dve.drain()
                dve.wait_ge(o_done, n + 1)
                dve.tensor_tensor(heads(yo[:]), heads(o_ps[:]), bcast(ecum[:, t, h], 64, 2), ALU.mult).then_inc(yo_done, 1)
                dve.wait_ge(s_done, n + 5)
                dve.wait_ge(sdec_done, n + 1)
                dve.tensor_tensor(state[:, d], sdec[:, d], s_ps[:], ALU.add).then_inc(state_done, 1)
                dve.drain()
                dve.tensor_tensor(y_tok[:, t], y_tok[:, t], yo[:], ALU.add)

            def scores(k):
                dve.wait_ge(exp_done, k.n + 1)
                for g in range(SG):
                    v = sc[:, k.d, g * HG * P:(g + 1) * HG * P].rearrange("p (h i) -> p h i", h=HG)
                    op = dve.tensor_tensor(v, v, bcast(gm[:, k.d, g * P:(g + 1) * P], HG, 1), ALU.mult)
                op.then_inc(sc_done, 1)

            def diagonal(k):
                t = tiles_of(k.pair, k.d)
                dve.drain()
                dve.wait_ge(y_done, k.n + 5)
                dve.tensor_tensor(y_tok[:, t], y_tok[:, t], y_ps[:], ALU.add).then_inc(yadd_done, 1)

            def first(k):
                segments(k)
                carried(k)

            def body(k, before, after):
                scores(k)
                if before:
                    diagonal(k.last())
                if after:
                    first(k.next())
            steps(dve, first, body)
            diagonal(ScanStep(0, STEPS - 1))

        @block.tensor
        def _(pe):
            pe.sem_inc(y_done, 4)
            pe.sem_inc(s_done, 4)

            def first(k):
                n, d, b, t, _ = place(k)
                pe.wait_ge(seg_done, n + 1)
                for h in range(SH):
                    mm = pe.matmul(cum_ps[d][:, h * P:(h + 1) * P], pick[:, d * SH + h, :],
                                   cumT[:, bass.ds(t * P, P)], start=True, stop=True)
                mm.then_inc(cumb_done, 1)
                pe.wait_ge(bc_done, n + 1)
                pe.wait_ge(gm_done, n + 1)
                for g in range(SG):
                    mm = pe.matmul(g_ps[:, g * P:(g + 1) * P], bc[:, b, g, :], bc[:, b, SG + g, :], start=True, stop=True)
                mm.then_inc(g_done, 1)
                pe.wait_ge(yo_done, n + 1)
                pe.wait_ge(state_done, n + 1)
                for g in range(SG):
                    r = slice(g * HG * 64, (g + 1) * HG * 64)
                    mm = pe.matmul(o_ps[:, r], bc[:, b, SG + g, :], state[:, d, r], start=True, stop=True)
                mm.then_inc(o_done, 1)
                pe.wait_ge(x_done, n + 1)
                pe.wait_ge(state_done, n + 2)
                for g in range(SG):
                    r = slice(g * HG * 64, (g + 1) * HG * 64)
                    mm = pe.matmul(s_ps[:, r], bt[:, b, g * P:(g + 1) * P], xe[:, b, r], start=True, stop=True)
                mm.then_inc(s_done, 1)

            def body(k, before, after):
                if after:
                    first(k.next())
                pe.wait_ge(sc_done, k.n + 1)
                pe.wait_ge(yadd_done, k.n + 1)
                for h in range(SH):
                    mm = pe.matmul(y_ps[:, h * 64:(h + 1) * 64], sc[:, k.d, h * P:(h + 1) * P],
                                   xd[:, k.buf, h * 64:(h + 1) * 64], start=True, stop=True)
                mm.then_inc(y_done, 1)
            steps(pe, first, body)


def state_stage(nc, I, C, W):
    with ExitStack() as ctx:
        s = Scope(nc, ctx, "state")
        out, inn = s.sb("out", [P, 2, 4, P]), s.sb("in", [P, 2, 4, P])
        ps_out, ps_in = [s.ps(f"out{d}") for d in range(2)], [s.ps(f"in{d}") for d in range(2)]
        loaded, turned_out, turned_in = s.sem("loaded"), s.sem("turned_out"), s.sem("turned_in")
        out_done, stored = s.sem("out_done"), s.sem("stored")
        block = ctx.enter_context(nc.Block())
        state = W["state"]

        @block.sync
        def _(sp):
            for d, name in enumerate(("state_ssm_fwd", "state_ssm_bwd")):
                sp.dma_start(inn[:, d], I[name][0, 0].rearrange("(q a) p n -> (a p) q n", a=2)).then_inc(loaded, 16)
            for d, name in enumerate(("new_hf", "new_hb")):
                sp.wait_ge(out_done, d + 1)
                sp.dma_start(I[name][0, 0].rearrange("(q a) p n -> (a p) q n", a=2), out[:, d]).then_inc(stored, 16)
            sp.wait_ge(stored, 32)

        @block.tensor
        def _(pe):
            for d in range(2):
                for q in range(4):
                    mm = pe.transpose(ps_out[d][:, q * P:(q + 1) * P], state[:, d, q * P:(q + 1) * P], C["ident"][:])
                mm.then_inc(turned_out, 1)
            pe.wait_ge(loaded, 32)
            for d in range(2):
                for q in range(4):
                    mm = pe.transpose(ps_in[d][:, q * P:(q + 1) * P], inn[:, d, q, :], C["ident"][:])
                mm.then_inc(turned_in, 1)

        @block.vector
        def _(dve):
            for d in range(2):
                dve.wait_ge(turned_out, d + 1)
                dve.tensor_copy(out[:, d].rearrange("p q n -> p (q n)"), ps_out[d][:]).then_inc(out_done, 1)
            for d in range(2):
                dve.wait_ge(turned_in, d + 1)
                dve.tensor_copy(state[:, d], ps_in[d][:])


def scan_stages(nc, I, C, W, M):
    with ExitStack() as ctx:
        s = Scope(nc, ctx, "scan")
        W["tok"], W["xbcT"] = s.sb("tok", [P, TILES, XBC]), s.sb("xbcT", [P, 4, COUT])
        for k in ("cum", "tot", "ecum", "dte", "dec"):
            W[k] = s.sb(k, [P, TILES, 2 * SH])
        W["cumT"] = s.sb("cumT", [2 * SH, TILES * P])
        conv_stage(nc, I, C, W, M)
        W["pick"], W["state"] = s.sb("pick", [2 * SH, 2 * SH, P]), s.sb("st", [P, 2, DSSM])
        with ExitStack() as load_ctx:
            pick_in = Scope(nc, load_ctx, "pick").sem("in")
            block = load_ctx.enter_context(nc.Block())

            @block.sync
            def _(sp):
                sp.dma_start(W["pick"][:], I["pick"]).then_inc(pick_in, 16)
                sp.wait_ge(pick_in, 16)

            @block.vector
            def _(dve):
                dve.memset(W["state"][:], 0.0)
        ssd_stage(nc, I, C, W, "ssdp", 1, lambda i, d: 0, lambda i, d: 0)
        state_stage(nc, I, C, W)
        ssd_stage(nc, I, C, W, "ssds", STILES, lambda i, d: i + 1 if d == 0 else i * -1 + STILES,
                  lambda i, d: i * P + (2 + P) if d == 0 else i * -P + (2 + STILES * P))


class Item:

    def __init__(self, t, h):
        self.step, self.t, self.h, self.buf = t, t.n, h, h % 2
        self.n = t.n * HEADS + h
        self.prompt = isinstance(t.n, int) and t.n == 0

    def next(self, last_tile):
        if self.h < HEADS - 1:
            return Item(self.step, self.h + 1)
        return None if last_tile else Item(self.step.next(), 0)


def attention_stage(nc, I, C, W, M):
    with ExitStack() as ctx:
        s = Scope(nc, ctx, "att")
        lam_rows, lam_prod = s.sb("lam_rows", [P, 4, QKD]), s.sb("lam_prod", [P, 2, QKD])
        lam_sum, lam_neg = s.sb("lam_sum", [P, 2]), s.sb("lam_neg", [P, 1])
        q_now = s.sb("q_now", [P, 2, HEADS, P])
        e = s.sb("e", [P, 2, 2, TILES * P])
        aT = s.sb("aT", [P, TILES * P])
        top, top2, shift = s.sb("top", [P, 2, 2]), s.sb("top2", [P, 2]), s.sb("shift", [P, 2, 2])
        total, inv, ratio = s.sb("total", [P, 2, 2]), s.sb("inv", [P, 2, 2]), s.sb("ratio", [P, 2, 1])
        sc = s.ps("sc", 5 * 512)
        turned = [s.ps(f"turned{b}") for b in range(2)]
        o_ps = s.ps("o")
        lam_in, lam_prod_done, lam_exp_done = s.sem("lam_in"), s.sem("lam_prod_done"), s.sem("lam_exp_done")
        q_staged, e_tail = s.sem("q_staged"), s.sem("e_tail")
        sc_done, shift_done, e_main = ([s.sem(f"{k}{m}") for m in range(2)] for k in ("sc_done", "shift_done", "e_main"))
        tail_done, a_done, o_done, o_read = s.sem("tail_done"), s.sem("a_done"), s.sem("o_done"), s.sem("o_read")
        t_done = [s.sem(f"t_done{g}") for g in range(3)]
        t_read = [s.sem(f"t_read{g}") for g in range(3)]
        block = ctx.enter_context(nc.Block())
        kT, qT, v_tok, o_tok = W["kT"], W["qT"], W["v_tok"], W["o_tok"]
        ident = C["ident"]

        def tail(m):
            return sc[:, 4 * 512 + m * P:4 * 512 + (m + 1) * P]

        def score_parts(it, m):
            if it.prompt:
                return [(sc[:, 2 * m * 512:2 * m * 512 + P], e[:, it.buf, m, 0:P], 0, P)]
            return [(sc[:, 2 * m * 512:(2 * m + 2) * 512], e[:, it.buf, m, 0:1024], P, P + 1024),
                    (tail(m), e[:, it.buf, m, 1024:1152], P + 1024, P + 1152)]

        def groups(it):
            return [range(0, 1)] if it.prompt else [range(0, 4), range(4, 8), range(8, 9)]

        def full_n(it):
            return it.n - HEADS

        def tiles(eng, first, body):
            first(Item(Step(0, 0), 0))
            body(Step(0, 0), False)
            with eng.Fori(0, STILES // 2 - 1) as i:
                body(Step(i, 1), False)
                body(Step(i, 2), False)
            body(Step(0, STILES - 1), False)
            body(Step(0, STILES), True)

        @block.sync
        def _(sp):
            for k, name in enumerate(("lambda_q1", "lambda_k1", "lambda_q2", "lambda_k2")):
                sp.dma_start(lam_rows[:, k], row_bcast(I[name][0])).then_inc(lam_in, 16)
            load_mixer(sp, I, W, M)

        @block.gpsimd
        def _(pool):
            def copy(t, buf):
                pool.wait_ge(sc_done[1], t * HEADS + HEADS)
                pool.tensor_copy(q_now[:, buf], qT[:, :, bass.ds(t * P, P)]).then_inc(q_staged, 1)
            copy(0, 0)
            with pool.Fori(0, STILES // 2) as i:
                copy(i * 2 + 1, 1)
                copy(i * 2 + 2, 0)

        @block.scalar
        def _(act):
            act.sem_inc(t_read[2], 1)
            act.wait_ge(lam_prod_done, 1)
            act.activation(lam_sum[:], lam_sum[:], ACT.Exp).then_inc(lam_exp_done, 1)

            def exponentials(it, m):
                if m == 0:
                    act.wait_ge(o_done, it.n + 1)
                act.wait_ge(shift_done[m], it.n + 1)
                bias = shift[:, it.buf, m:m + 1]
                for p, (scores, exps, _, _) in enumerate(score_parts(it, m)):
                    sums, done = (total, e_main[m]) if p == 0 else (inv, e_tail)
                    act.activation(exps, scores, ACT.Exp, bias=bias, scale=SCALE,
                                   accum_out=sums[:, it.buf, m:m + 1]).then_inc(done, 1)

            def evacuate(it, gs):
                for g, ks in enumerate(groups(it)):
                    if g in gs:
                        act.wait_ge(t_done[g], (it.n if g == 0 else full_n(it)) + 1)
                        act.copy(aT[:, ks[0] * P:(ks[-1] + 1) * P], turned[g % 2][:, 0:len(ks) * P]).then_inc(t_read[g], 1)

            def first(it):
                exponentials(it, 0)
                exponentials(it, 1)

            def body(t, last):
                for h in range(HEADS):
                    it = Item(t, h)
                    nxt = it.next(last)
                    act.wait_ge(o_done, it.n + 2)
                    evacuate(it, (0, 1))
                    if nxt:
                        exponentials(nxt, 0)
                    evacuate(it, (2,))
                    if nxt:
                        exponentials(nxt, 1)
            tiles(act, first, body)

        @block.vector
        def _(dve):
            dve.sem_inc(o_read, 1)
            dve.wait_ge(lam_in, 64)
            for k in range(2):
                dve.tensor_tensor(lam_prod[:, k], lam_rows[:, 2 * k], lam_rows[:, 2 * k + 1], ALU.mult)
            dve.drain()
            dve.tensor_reduce(lam_sum[:], lam_prod[:], AX, ALU.add).then_inc(lam_prod_done, 1)
            dve.wait_ge(lam_exp_done, 1)
            dve.tensor_tensor(lam_neg[:], lam_sum[:, 1:2], lam_sum[:, 0:1], ALU.subtract)
            dve.drain()
            dve.tensor_scalar(lam_neg[:], lam_neg[:], -LAM0, None, ALU.add)

            def maxima(it, m):
                dve.drain()
                dve.wait_ge(sc_done[m], it.n + (1 if m == 0 else 2 * HEADS + 1))
                top_m, other = top[:, it.buf, m:m + 1], top2[:, m:m + 1]
                dve.tensor_reduce(top_m, score_parts(it, m)[0][0], AX, ALU.max)
                if it.prompt:
                    other = top_m
                elif m == 0:
                    dve.tensor_reduce(top2[:], sc[:, 4 * 512:4 * 512 + 2 * P].rearrange("p (m k) -> p m k", m=2), AX, ALU.max)
                dve.drain()
                dve.tensor_scalar(shift[:, it.buf, m:m + 1], top_m, other, -SCALE, ALU.max, ALU.mult).then_inc(shift_done[m], 1)

            def combine(it):
                dve.drain()
                for m in range(2):
                    dve.wait_ge(e_main[m], it.n + 2)
                if not it.prompt:
                    dve.wait_ge(e_tail, full_n(it) * 2 + 4)
                tot = total[:, it.buf]
                if not it.prompt:
                    dve.tensor_tensor(tot, tot, inv[:, it.buf], ALU.add)
                    dve.drain()
                dve.reciprocal(inv[:, it.buf], tot)
                dve.drain()
                dve.tensor_scalar(ratio[:, it.buf], inv[:, it.buf, 1:2], tot[:, 0:1], lam_neg[:, 0:1], ALU.mult, ALU.mult)
                dve.drain()
                w = P if it.prompt else TILES * P
                dve.scalar_tensor_tensor(out=e[:, it.buf, 0, 0:w], in0=e[:, it.buf, 1, 0:w], scalar=ratio[:, it.buf, 0:1],
                                         in1=e[:, it.buf, 0, 0:w], op0=ALU.mult, op1=ALU.add).then_inc(a_done, 1)

            def finish(it):
                dve.wait_ge(o_done, it.n + 3)
                dve.tensor_scalar(o_tok[:, it.t, it.h * P:(it.h + 1) * P], o_ps[:, 0:P], inv[:, it.buf, 0:1], None,
                                  ALU.mult).then_inc(o_read, 1)

            def first(it):
                maxima(it, 0)
                maxima(it, 1)
                combine(it)

            def body(t, last):
                for h in range(HEADS):
                    it = Item(t, h)
                    nxt = it.next(last)
                    if nxt:
                        maxima(nxt, 0)
                        maxima(nxt, 1)
                    finish(it)
                    if nxt:
                        combine(nxt)
            tiles(dve, first, body)

        @block.tensor
        def _(pe):
            pe.sem_inc(sc_done[1], 2 * HEADS)
            pe.sem_inc(o_done, 2)
            for done, credit in ((e_main[0], 1), (e_main[1], 1), (e_tail, 2)):
                pe.sem_inc(done, credit)

            def score(it, m, dst, lo, hi):
                rows = slice(m * QKD, (m + 1) * QKD)
                return pe.matmul(dst, q_now[rows, it.step.buf, it.h, :], kT[rows, it.h, lo:hi], start=True, stop=True)

            def score_half(it, m, half):
                lo = P + half * 512
                return score(it, m, sc[:, (2 * m + half) * 512:(2 * m + half + 1) * 512], lo, lo + 512)

            def scores_first(it):
                pe.wait_ge(q_staged, it.t + 1)
                pe.wait_ge(e_main[0], it.n + 1)
                if it.prompt:
                    score(it, 0, sc[:, 0:P], 0, P).then_inc(sc_done[0], 1)
                    return
                score_half(it, 0, 0)
                pe.wait_ge(e_tail, full_n(it) * 2 + 2)
                score(it, 0, tail(0), P + 1024, P + 1152).then_inc(tail_done, 1)
                score_half(it, 0, 1)
                pe.wait_ge(tail_done, full_n(it) + 1)
                score(it, 1, tail(1), P + 1024, P + 1152).then_inc(sc_done[0], 1)

            def scores_second(it, half):
                if half == 0:
                    pe.wait_ge(e_main[1], it.n + 1)
                    if it.prompt:
                        score(it, 1, sc[:, 2 * 512:2 * 512 + P], 0, P).then_inc(sc_done[1], 1)
                    else:
                        score_half(it, 1, 0)
                elif not it.prompt:
                    score_half(it, 1, 1).then_inc(sc_done[1], 1)

            def turn(it, g):
                ks = groups(it)[g]
                bank = turned[g % 2]
                for j, k in enumerate(ks):
                    mm = pe.transpose(bank[:, j * P:(j + 1) * P], e[:, it.buf, 0, k * P:(k + 1) * P], ident[:])
                mm.then_inc(t_done[g], 1)

            def values(it, g):
                ks = groups(it)[g]
                n = it.n if g == 0 else full_n(it)
                pe.wait_ge(t_read[g], n + (2 if g == 2 else 1))
                last = groups(it)[-1][-1]
                for k in ks:
                    mm = pe.matmul(o_ps[:, 0:P], aT[:, k * P:(k + 1) * P],
                                   v_tok[:, k + (0 if it.prompt else 1), it.h * P:(it.h + 1) * P],
                                   start=(k == 0), stop=(k == last))
                return mm

            def first(it):
                scores_first(it)
                scores_second(it, 0)

            def item(it, nxt):
                if nxt:
                    scores_first(nxt)
                    scores_second(nxt, 0)
                pe.wait_ge(a_done, it.n + 1)
                if not it.prompt:
                    pe.wait_ge(t_read[2], full_n(it) + 1)
                turn(it, 0)
                if not it.prompt:
                    turn(it, 1)
                if nxt:
                    scores_second(nxt, 1)
                pe.wait_ge(o_read, it.n + 1)
                if it.prompt:
                    values(it, 0).then_inc(o_done, 1)
                    return
                values(it, 0)
                turn(it, 2)
                values(it, 1)
                values(it, 2).then_inc(o_done, 1)

            def body(t, last):
                for h in range(HEADS):
                    it = Item(t, h)
                    item(it, it.next(last))
            tiles(pe, first, body)


def refine(dve, r, ssq, scale, tmp):
    dve.drain()
    dve.tensor_scalar(tmp, ssq, scale, EPS, ALU.mult, ALU.add)
    dve.drain()
    dve.scalar_tensor_tensor(out=tmp, in0=tmp, scalar=-0.5, in1=r, op0=ALU.mult, op1=ALU.mult)
    dve.drain()
    dve.tensor_tensor(tmp, tmp, r, ALU.mult)
    dve.drain()
    dve.scalar_tensor_tensor(out=r, in0=tmp, scalar=1.5, in1=r, op0=ALU.add, op1=ALU.mult)
    dve.drain()


def load_mixer(sp, I, W, M):
    sp.dma_start(W["w_out"][:], I["w_out"][0].rearrange("(k p) n -> p k n", p=P)).then_inc(W["w_out_in"], 16)
    for cond in range(2):
        for dst, sec in (("gate", GATE1), ("amul", SCALE2), ("aadd", SHIFT2)):
            sp.dma_start(W[dst][:, cond], row_bcast(M["mods"][cond, sec * D:(sec + 1) * D])).then_inc(W["gains_in"], 16)
    sp.dma_start(W["gain"][:], row_bcast(I["norm_ffn_g"][0])).then_inc(W["gains_in"], 16)


def mixer_stage(nc, I, C, W, M):
    with ExitStack() as ctx:
        s = Scope(nc, ctx, "mix")
        w_out, gate, amul, aadd, gain = (W[k] for k in ("w_out", "gate", "amul", "aadd", "gain"))
        gcol = s.sb("gcol", [P, KT])
        wr, br = s.sb("wr", [P, KT, NG + NE]), s.sb("br", [P, NG + NE])
        z, x = s.sb("z", [P, 2, DSSM]), s.sb("x", [P, 2, D])
        mix, mixT = s.sb("mix", [P, 2, D]), s.sb("mixT", [P, 2, KT * P])
        h2, h2T = s.sb("h2", [P, 2, D]), s.sb("h2T", [P, KT * P])
        junk, junk2 = s.sb("junk", [P, DSSM]), s.sb("junk2", [P, D])
        ssq, rstd, tmp = s.sb("ssq", [P, 2, 5]), s.sb("rstd", [P, 2, 5]), s.sb("tmp", [P, 5])
        ssq2, rstd2, tmp2 = s.sb("ssq2", [P, 2]), s.sb("rstd2", [P, 2]), s.sb("tmp2", [P, 1])
        epsc = s.sb("epsc", [P, 1])
        t1_ps, acc, t2_ps = s.ps("t1", D), s.ps("acc", D), s.ps("t2", D)
        lg_ps = s.ps("lg")
        g_in, eps_done = s.sem("g_in"), s.sem("eps_done")
        z_in, x_in = [s.sem(f"z_in{u}") for u in range(2)], [s.sem(f"x_in{u}") for u in range(2)]
        silu_done, gated, sq_done, mix_done = s.sem("silu_done"), s.sem("gated"), s.sem("sq_done"), s.sem("mix_done")
        t1_done, mixT_done, acc_done, acc_read = s.sem("t1_done"), s.sem("mixT_done"), s.sem("acc_done"), s.sem("acc_read")
        x2_done, sq2_done, h2_scaled, h2_done = s.sem("x2_done"), s.sem("sq2_done"), s.sem("h2_scaled"), s.sem("h2_done")
        t2_done, h2T_done, lg_done, lg_read = s.sem("t2_done"), s.sem("h2T_done"), s.sem("lg_done"), s.sem("lg_read")
        h2_stored = [s.sem(f"h2_stored{u}") for u in range(2)]
        block = ctx.enter_context(nc.Block())
        y_tok, o_tok, x2, logits = W["y_tok"], W["o_tok"], W["x2"], W["logits"]

        def tiles(eng, first, body):
            first(Step(0, 0))
            body(Step(0, 0), True)
            with eng.Fori(0, STILES // 2 - 1) as i:
                body(Step(i, 1), True)
                body(Step(i, 2), True)
            body(Step(0, TILES - 2), True)
            body(Step(0, TILES - 1), False)

        def is_first(t):
            return isinstance(t.n, int) and t.n == 0

        @block.sync
        def _(sp):
            sp.dma_start(gcol[:, 0:1], I["attn_subln_g"][0].unsqueeze(1)).then_inc(g_in, 16)
            sp.dma_start(gcol[:, HEADS:KT], I["ssm_norm_g"][0].rearrange("(k p) -> p k", p=P),
                         allow_slow_non_contiguous=True).then_inc(g_in, 16)
            sp.dma_start(wr[:, :, 0:NG], I["w_group_router"][0].rearrange("(k p) n -> p k n", p=P)).then_inc(g_in, 16)
            sp.dma_start(wr[:, :, NG:], I["w_expert_router"][0].rearrange("(k p) n -> p k n", p=P)).then_inc(g_in, 16)
            sp.dma_start(br[:, 0:NG], row_bcast(I["b_group_router"][0])).then_inc(g_in, 16)
            sp.dma_start(br[:, NG:], row_bcast(I["b_expert_router"][0])).then_inc(g_in, 16)

            def load(t):
                xrows = I["x_prompt"][0] if is_first(t) else I["x_sample"][0, bass.ds((t.n - 1) * P, P), :]
                sp.wait_ge(gated, t.n + 1)
                sp.dma_start(z[:, t.buf], M["z"][bass.ds(t.n * P, P), :]).then_inc(z_in[t.buf], 16)
                sp.wait_ge(x2_done, t.n + 1)
                sp.dma_start(x[:, t.buf], xrows).then_inc(x_in[t.buf], 16)

            def body(t, more):
                if more:
                    load(t.next())
                sp.wait_ge(h2_done, t.n + 3)
                sp.dma_start(M["h2"][bass.ds(t.n * P, P), :], h2[:, t.buf]).then_inc(h2_stored[t.buf], 16)
            tiles(sp, load, body)
            sp.wait_ge(h2_stored[0], 16 * 6)
            sp.wait_ge(h2_stored[1], 16 * 5)

        @block.gpsimd
        def _(pool):
            pool.sem_inc(x2_done, 2)
            pool.sem_inc(h2_done, 2)

            def body(t, more):
                pool.wait_ge(x_in[t.buf], t.nth * 16 + 16)
                pool.wait_ge(acc_read, t.n + 2)
                pool.tensor_tensor(x2[:, t.n], x2[:, t.n], x[:, t.buf], ALU.add).then_inc(x2_done, 1)
                pool.wait_ge(h2_scaled, t.n + 1)
                pool.tensor_tensor(h2[:, t.buf], h2[:, t.buf], aadd[:, 0 if is_first(t) else 1], ALU.add).then_inc(h2_done, 1)
            tiles(pool, lambda t: None, body)

        @block.scalar
        def _(act):
            act.sem_inc(h2T_done, 1)
            act.wait_ge(eps_done, 1)

            def prepare(t):
                act.wait_ge(z_in[t.buf], t.nth * 16 + 16)
                act.activation(z[:, t.buf], z[:, t.buf], ACT.Silu).then_inc(silu_done, 1)
                for h in range(HEADS):
                    act.activation(junk[:, h * P:(h + 1) * P], o_tok[:, t.n, h * P:(h + 1) * P], ACT.Square,
                                   accum_out=ssq[:, t.buf, h:h + 1])
                act.drain()
                act.activation(rstd[:, t.buf, 0:HEADS], ssq[:, t.buf, 0:HEADS], ACT.Sqrt, bias=epsc[:, 0:1], scale=1.0 / P)
                act.wait_ge(gated, t.n + 3)
                act.activation(junk[:], mix[:, t.buf, DATT:], ACT.Square, accum_out=ssq[:, t.buf, HEADS:HEADS + 1])
                act.drain()
                act.activation(rstd[:, t.buf, HEADS:HEADS + 1], ssq[:, t.buf, HEADS:HEADS + 1], ACT.Sqrt, bias=epsc[:, 0:1],
                               scale=1.0 / DSSM).then_inc(sq_done, 1)

            def evacuate(t):
                act.wait_ge(lg_done, t.n + 1)
                act.wait_ge(t2_done, t.n + 3)
                act.copy(h2T[:], t2_ps[:]).then_inc(h2T_done, 1)

            def body(t, more):
                if more:
                    prepare(t.next())
                if not is_first(t):
                    evacuate(Step(t.i, t.c - 1))
                act.wait_ge(x2_done, t.n + 3)
                act.activation(junk2[:], x2[:, t.n], ACT.Square, accum_out=ssq2[:, t.buf:t.buf + 1])
                act.drain()
                act.activation(rstd2[:, t.buf:t.buf + 1], ssq2[:, t.buf:t.buf + 1], ACT.Sqrt, bias=epsc[:, 0:1],
                               scale=1.0 / D).then_inc(sq2_done, 1)
            tiles(act, prepare, body)
            evacuate(Step(0, TILES - 1))

        @block.vector
        def _(dve):
            dve.memset(epsc[:], EPS).then_inc(eps_done, 1)
            dve.sem_inc(gated, 2)
            dve.sem_inc(mixT_done, 1)
            dve.sem_inc(acc_read, 1)
            dve.sem_inc(lg_read, 1)
            for u in range(2):
                dve.sem_inc(h2_stored[u], 16)
            dve.wait_ge(g_in, 16 * 6)
            dve.wait_ge(W["gains_in"], 16 * 7)
            for cond in range(2):
                dve.scalar_tensor_tensor(out=amul[:, cond], in0=amul[:, cond], scalar=1.0, in1=gain[:], op0=ALU.add, op1=ALU.mult)
            dve.tensor_scalar(gcol[:, 0:1], gcol[:, 0:1], 1.0 - LAM0, None, ALU.mult)
            dve.drain()
            for h in range(1, HEADS):
                dve.tensor_copy(gcol[:, h:h + 1], gcol[:, 0:1])
            dve.drain()

            def prepare(t):
                dve.drain()
                dve.wait_ge(silu_done, t.n + 1)
                dve.wait_ge(t1_done, t.n + 1)
                dve.tensor_tensor(mix[:, t.buf, DATT:], z[:, t.buf], y_tok[:, t.n], ALU.mult).then_inc(gated, 1)
                dve.wait_ge(sq_done, t.n + 1)
                r = rstd[:, t.buf]
                dve.reciprocal(r, r)
                refine(dve, r[:, 0:HEADS], ssq[:, t.buf, 0:HEADS], 1.0 / P, tmp[:, 0:HEADS])
                refine(dve, r[:, HEADS:], ssq[:, t.buf, HEADS:], 1.0 / DSSM, tmp[:, HEADS:])
                dve.tensor_tensor(mix[:, t.buf, 0:DATT].rearrange("p (h d) -> p h d", h=HEADS),
                                  o_tok[:, t.n].rearrange("p (h d) -> p h d", h=HEADS), bcast(r[:, 0:HEADS], P, 2), ALU.mult)
                dve.tensor_scalar(mix[:, t.buf, DATT:], mix[:, t.buf, DATT:], r[:, HEADS:], None, ALU.mult).then_inc(mix_done, 1)

            def gains(t):
                dve.wait_ge(acc_done, t.n + 1)
                dve.wait_ge(t1_done, t.n + 3)
                dve.tensor_tensor(mixT[:, t.buf].rearrange("p (k t) -> p k t", k=KT), t1_ps[:].rearrange("p (k t) -> p k t", k=KT),
                                  bcast(gcol[:], P, 2), ALU.mult).then_inc(mixT_done, 1)

            def router(t):
                dve.wait_ge(lg_done, t.n + 2)
                dve.tensor_tensor(logits[:, t.n], lg_ps[:, 0:NG + NE], br[:], ALU.add).then_inc(lg_read, 1)

            def first(t):
                prepare(t)
                gains(t)

            def body(t, more):
                cond = 0 if is_first(t) else 1
                if more:
                    prepare(t.next())
                dve.wait_ge(acc_done, t.n + 3)
                dve.tensor_tensor(x2[:, t.n], acc[:], gate[:, cond], ALU.mult).then_inc(acc_read, 1)
                if more:
                    gains(t.next())
                dve.wait_ge(sq2_done, t.n + 1)
                r = rstd2[:, t.buf:t.buf + 1]
                dve.reciprocal(r, r)
                refine(dve, r, ssq2[:, t.buf:t.buf + 1], 1.0 / D, tmp2[:])
                dve.wait_ge(t2_done, t.n + 1)
                dve.wait_ge(h2_stored[t.buf], t.nth * 16 + 16)
                dve.scalar_tensor_tensor(out=h2[:, t.buf], in0=x2[:, t.n], scalar=r, in1=amul[:, cond], op0=ALU.mult,
                                         op1=ALU.mult).then_inc(h2_scaled, 1)
                if not is_first(t):
                    router(Step(t.i, t.c - 1))

            tiles(dve, first, body)
            router(Step(0, TILES - 1))

        @block.tensor
        def _(pe):
            ident = C["ident"]
            pe.sem_inc(t1_done, 2)
            pe.sem_inc(acc_done, 2)
            pe.sem_inc(lg_done, 1)
            pe.sem_inc(t2_done, 2)
            pe.wait_ge(W["w_out_in"], 16)

            def turn_mix(t):
                pe.wait_ge(mix_done, t.n + 1)
                pe.wait_ge(mixT_done, t.n + 1)
                for k in range(KT):
                    mm = pe.transpose(t1_ps[:, k * P:(k + 1) * P], mix[:, t.buf, k * P:(k + 1) * P], ident[:])
                mm.then_inc(t1_done, 1)

            def turn_h2(t):
                pe.wait_ge(h2_done, t.n + 3)
                pe.wait_ge(h2T_done, t.n + 1)
                for k in range(KT):
                    mm = pe.transpose(t2_ps[:, k * P:(k + 1) * P], h2[:, t.buf, k * P:(k + 1) * P], ident[:])
                mm.then_inc(t2_done, 1)

            def route(t):
                pe.wait_ge(h2T_done, t.n + 2)
                pe.wait_ge(lg_read, t.n + 1)
                for k in range(KT):
                    mm = pe.matmul(lg_ps[:, 0:NG + NE], h2T[:, k * P:(k + 1) * P], wr[:, k], start=(k == 0), stop=(k == KT - 1))
                mm.then_inc(lg_done, 1)

            def body(t, more):
                pe.wait_ge(mixT_done, t.n + 2)
                pe.wait_ge(acc_read, t.n + 1)
                for half in range(2):
                    for k in range(KT):
                        mm = pe.matmul(acc[:, half * 512:(half + 1) * 512], mixT[:, t.buf, k * P:(k + 1) * P],
                                       w_out[:, k, half * 512:(half + 1) * 512], start=(k == 0), stop=(k == KT - 1))
                    if half == 0 and not is_first(t):
                        turn_h2(Step(t.i, t.c - 1))
                mm.then_inc(acc_done, 1)
                if more:
                    turn_mix(t.next())
                if not is_first(t):
                    route(Step(t.i, t.c - 1))
            tiles(pe, turn_mix, body)
            turn_h2(Step(0, TILES - 1))
            route(Step(0, TILES - 1))


def routing_stage(nc, I, C, W, M):
    with ExitStack() as ctx:
        s = Scope(nc, ctx, "route")
        T = TILES
        steps, tokens = s.sb("steps", [P, BLOCKS]), s.sb("tokens", [P, T])
        ones, zeros = s.sb("ones", [P, P]), s.sb("zeros", [P, 2 * BLOCKS])
        gmax, gdiff, gsum, pg = s.sb("gmax", [P, T]), s.sb("gdiff", [P, T, NG]), s.sb("gsum", [P, T]), s.sb("pg", [P, T])
        ohg, oh = s.sb("ohg", [P, T, NG]), s.sb("oh", [P, 2, T, EPG])
        seen, left = s.sb("seen", [P, T]), s.sb("left", [P, T])
        prod, esel, esel2 = s.sb("prod", [P, T, NG, EPG]), s.sb("esel", [P, T, EPG]), s.sb("esel2", [P, T, EPG])
        top = s.sb("top", [P, 2, T])
        ediff, wsum = s.sb("ediff", [P, T]), s.sb("wsum", [P, T])
        pick = s.sb("pick", [P, 2, T, NE])
        both, place, weighed = s.sb("both", [P, T, NE]), s.sb("place", [P, T, NE]), s.sb("weighed", [P, T, NE])
        before, count = s.sb("before", [P, T, NE]), s.sb("count", [P, NE])
        more, nblk, bend, bones = s.sb("more", [P, NE, T]), s.sb("nblk", [P, NE]), s.sb("bend", [P, NE]), s.sb("bones", [P, NE])
        fresh, sign, buffer = (s.sb(k, [P, BLOCKS]) for k in ("fresh", "sign", "buffer"))
        past, of_block = s.sb("past", [P, BLOCKS, NE]), s.sb("of_block", [P, BLOCKS])
        slot_f = s.sb("slot_f", [P, T])
        slot_u = [[s.sb(f"slot{c}_{t}", [P, 1], U32) for t in range(T)] for c in range(2)]
        value = s.sb("value", [P, 2, T, 2])
        table = s.sb("table", [P, BLOCKS, 2])
        rank_ps, sum_ps = s.ps("rank"), s.ps("sum")
        c_in, z_done, z_stored = s.sem("c_in"), s.sem("z_done"), s.sem("z_stored")
        g_done, gexp_done, e_done, eexp_done = s.sem("g_done"), s.sem("gexp_done"), s.sem("e_done"), s.sem("eexp_done")
        both_done, ranked, slots_done, scattered, table_in = (s.sem(k) for k in
                                                              ("both_done", "ranked", "slots_done", "scattered", "table_in"))
        block = ctx.enter_context(nc.Block())
        logits = W["logits"]
        lg = logits[:, :, 0:NG]
        le = logits[:, :, NG:].rearrange("p t (g e) -> p t g e", g=NG)

        @block.sync
        def _(sp):
            sp.dma_start(steps[:], row_bcast(I["steps"])).then_inc(c_in, 16)
            sp.dma_start(tokens[:], I["tokens"]).then_inc(c_in, 16)
            sp.wait_ge(z_done, 1)
            sp.dma_start(M["slots"].rearrange("(p b) c -> p (b c)", p=P), zeros[:]).then_inc(z_stored, 16)
            sp.wait_ge(scattered, 16 * 2 * T)
            sp.dma_start(table[:], M["slots"].rearrange("(b p) c -> p b c", p=P)).then_inc(table_in, 16)

        @block.gpsimd
        def _(pool):
            pool.memset(zeros[:], 0.0).then_inc(z_done, 1)
            pool.wait_ge(z_stored, 16)
            pool.wait_ge(slots_done, 1)
            for c in range(2):
                for t in range(T):
                    pool.indirect_dma_start(M["slots"], bass.IndirectOffsetOnAxis(ap=slot_u[c][t][:], axis=0),
                                            value[:, c, t, :], None).then_inc(scattered, 16)
            pool.wait_ge(scattered, 16 * 2 * T)

        @block.scalar
        def _(act):
            act.wait_ge(g_done, 1)
            act.activation(gdiff[:], gdiff[:], ACT.Exp).then_inc(gexp_done, 1)
            act.wait_ge(e_done, 1)
            act.activation(ediff[:], ediff[:], ACT.Exp).then_inc(eexp_done, 1)

        @block.tensor
        def _(pe):
            pe.wait_ge(both_done, 1)
            v = both[:].rearrange("p t e -> p (t e)")
            pe.matmul(rank_ps[:, 0:T * NE], C["tri_lt"][:], v, start=True, stop=True)
            pe.matmul(sum_ps[:, 0:T * NE], ones[:], v, start=True, stop=True).then_inc(ranked, 1)

        @block.vector
        def _(dve):
            def tt(out, a, b, op):
                dve.tensor_tensor(out, a, b, op)
                dve.drain()

            def keep_first(v, n):
                dve.tensor_copy(seen[:], v[:, :, 0])
                dve.drain()
                for j in range(1, n):
                    dve.tensor_scalar(left[:], seen[:], -1.0, 1.0, ALU.mult, ALU.add)
                    dve.drain()
                    tt(v[:, :, j], v[:, :, j], left[:], ALU.mult)
                    tt(seen[:], seen[:], v[:, :, j], ALU.max)

            dve.memset(ones[:], 1.0)
            dve.memset(bones[:], 1.0)
            dve.tensor_reduce(gmax[:], lg, AX, ALU.max)
            dve.drain()
            dve.tensor_tensor(gdiff[:], lg, bcast(gmax[:], NG, 2), ALU.subtract).then_inc(g_done, 1)
            tt(ohg[:], lg, bcast(gmax[:], NG, 2), ALU.is_equal)
            keep_first(ohg[:], NG)
            tt(prod[:], le, bcast(ohg[:], EPG, 3), ALU.mult)
            dve.tensor_reduce(esel[:], prod[:].rearrange("p t g e -> p t e g"), AX, ALU.add)
            dve.drain()
            dve.tensor_reduce(top[:, 0], esel[:], AX, ALU.max)
            dve.drain()
            tt(oh[:, 0], esel[:], bcast(top[:, 0], EPG, 2), ALU.is_equal)
            keep_first(oh[:, 0], EPG)
            dve.scalar_tensor_tensor(out=esel2[:].rearrange("p t e -> p (t e)"), in0=oh[:, 0].rearrange("p t e -> p (t e)"),
                                     scalar=-3.0e38, in1=esel[:].rearrange("p t e -> p (t e)"), op0=ALU.mult, op1=ALU.add)
            dve.drain()
            dve.tensor_reduce(top[:, 1], esel2[:], AX, ALU.max)
            dve.drain()
            dve.tensor_tensor(ediff[:], top[:, 1], top[:, 0], ALU.subtract).then_inc(e_done, 1)
            tt(oh[:, 1], esel2[:], bcast(top[:, 1], EPG, 2), ALU.is_equal)
            keep_first(oh[:, 1], EPG)
            dve.wait_ge(gexp_done, 1)
            dve.tensor_reduce(gsum[:], gdiff[:], AX, ALU.add)
            dve.wait_ge(eexp_done, 1)
            dve.tensor_scalar(wsum[:], ediff[:], 1.0, None, ALU.add)
            dve.drain()
            tt(pg[:], gsum[:], wsum[:], ALU.mult)
            dve.reciprocal(pg[:], pg[:])
            dve.drain()
            dve.tensor_copy(value[:, 0, :, 1], pg[:])
            dve.tensor_tensor(value[:, 1, :, 1], pg[:], ediff[:], ALU.mult)
            dve.wait_ge(c_in, 32)
            for c in range(2):
                dve.tensor_copy(value[:, c, :, 0], tokens[:])
                dve.tensor_tensor(pick[:, c].rearrange("p t (g e) -> p t g e", g=NG), bcast(ohg[:], EPG, 3),
                                  bcast(oh[:, c], NG, 2), ALU.mult)
            dve.drain()
            dve.tensor_tensor(both[:], pick[:, 0], pick[:, 1], ALU.add).then_inc(both_done, 1)
            dve.memset(before[:, 0], 0.0)
            dve.drain()
            dve.wait_ge(ranked, 1)
            for t in range(1, T):
                tt(before[:, t], before[:, t - 1], sum_ps[:, (t - 1) * NE:t * NE], ALU.add)
            tt(count[:], before[:, T - 1], sum_ps[:, (T - 1) * NE:T * NE], ALU.add)
            tt(place[:], before[:], rank_ps[:, 0:T * NE].rearrange("p (t e) -> p t e", t=T), ALU.add)
            dve.tensor_scalar(count[:], count[:], 1.0 / P, None, ALU.mult)
            dve.drain()
            tt(more[:], bcast(count[:], T, 2), bcast(steps[:, 0:T], NE, 1), ALU.is_gt)
            dve.tensor_reduce(nblk[:], more[:], AX, ALU.add)
            dve.drain()
            dve.tensor_tensor_scan(bend[:], bones[:], nblk[:], 0.0, ALU.mult, ALU.add)
            dve.drain()
            tt(past[:], bcast(steps[:], NE, 2), bcast(bend[:], BLOCKS, 1), ALU.is_ge)
            dve.tensor_reduce(of_block[:], past[:], AX, ALU.add)
            dve.drain()
            dve.tensor_scalar(of_block[:], of_block[:], float(NE - 1), None, ALU.min)
            dve.drain()
            dve.tensor_copy(W["block_expert"][:], of_block[:])
            dve.memset(fresh[:, 0:1], 1.0)
            dve.tensor_tensor(fresh[:, 1:], of_block[:, 1:], of_block[:, 0:BLOCKS - 1], ALU.not_equal)
            dve.drain()
            dve.tensor_copy(W["block_new"][:], fresh[:])
            dve.tensor_scalar(sign[:], fresh[:], 2.0, -1.0, ALU.mult, ALU.add)
            dve.drain()
            dve.tensor_tensor_scan(buffer[:], fresh[:], sign[:], 0.0, ALU.subtract, ALU.mult)
            dve.drain()
            dve.tensor_copy(W["block_buf"][:], buffer[:])
            tt(nblk[:], bend[:], nblk[:], ALU.subtract)
            dve.tensor_scalar(nblk[:], nblk[:], float(P), None, ALU.mult)
            dve.drain()
            tt(place[:], place[:], bcast(nblk[:], T, 1), ALU.add)
            for c in range(2):
                tt(weighed[:], pick[:, c], place[:], ALU.mult)
                dve.tensor_reduce(slot_f[:], weighed[:], AX, ALU.add)
                dve.drain()
                for t in range(T):
                    dve.tensor_copy(slot_u[c][t][:], slot_f[:, t:t + 1])
                op = dve.tensor_copy(W["slot_of"][:, :, c], slot_f[:])
                dve.drain()
            dve.tensor_copy(slot_f[:], slot_f[:]).then_inc(slots_done, 1)
            dve.wait_ge(table_in, 16)
            dve.tensor_copy(W["block_token"][:], table[:, :, 0])
            dve.tensor_copy(W["block_weight"][:], table[:, :, 1])


def expert_stage(nc, I, C, W, M):
    with ExitStack() as ctx:
        s = Scope(nc, ctx, "moe")
        wgu, wd = s.sb("wgu", [P, 2, KT, 2 * FF]), s.sb("wd", [P, 2, 2, D])
        wgu_hi, wgu_lo = (s.sb(k, [P, 2, KT, 2 * FF], F32R) for k in ("wgu_hi", "wgu_lo"))
        wd_hi, wd_lo = (s.sb(k, [P, 2, 2, D], F32R) for k in ("wd_hi", "wd_lo"))
        idx = [s.sb(f"idx{u}", [P, 1], U32) for u in range(2)]
        xg = s.sb("xg", [P, 2, D])
        xT_hi, xT_lo = (s.sb(k, [P, KT * P], F32R) for k in ("xT_hi", "xT_lo"))
        act_g, hid = s.sb("act_g", [P, FF]), s.sb("hid", [P, FF])
        hidT_hi, hidT_lo = (s.sb(k, [P, FF], F32R) for k in ("hidT_hi", "hidT_lo"))
        y = s.sb("y", [P, D])
        x_ps, gu_ps, h_ps, y_ps = s.ps("x", D), [s.ps(f"gu{u}") for u in range(2)], s.ps("h"), s.ps("y", D)
        gu_in, d_in, xg_in = ([s.sem(f"{k}{u}") for u in range(2)] for k in ("gu_in", "d_in", "xg_in"))
        y_out = s.sem("y_out")
        gu_hi_done, gu_lo_done, d_hi_done, d_lo_done = (s.sem(k) for k in ("gu_hi_done", "gu_lo_done", "d_hi_done", "d_lo_done"))
        idx_done, started, x_turned, x_hi_done, x_lo_done = (s.sem(k) for k in ("idx_done", "started", "x_turned", "x_hi_done", "x_lo_done"))
        gu_done, silu_done, hid_done, h_turned = (s.sem(k) for k in ("gu_done", "silu_done", "hid_done", "h_turned"))
        hidT_done, y_done, y_read = (s.sem(k) for k in ("hidT_done", "y_done", "y_read"))
        block = ctx.enter_context(nc.Block())
        expert, token, weight = W["block_expert"], W["block_token"], W["block_weight"]

        def blocks(eng, body):
            assert BLOCKS % 2 == 1
            body(Step(0, 0), 3)
            with eng.Fori(0, (BLOCKS - 5) // 2) as i:
                body(Step(i, 1), 3)
                body(Step(i, 2), 3)
            for n in range(BLOCKS - 4, BLOCKS):
                body(Step(0, n), BLOCKS - 1 - n)

        def weight_buffer(eng, k):
            return eng.value_load(W["block_buf"][0:1, bass.ds(k.n, 1)], min_val=0, max_val=1)

        def block_values(eng, k):
            return (eng.value_load(expert[0:1, bass.ds(k.n, 1)], min_val=0, max_val=NE - 1), weight_buffer(eng, k),
                    eng.value_load(W["block_new"][0:1, bass.ds(k.n, 1)], min_val=0, max_val=1))

        @block.sync
        def _(sp):
            def load_gu(k):
                e, buf, new = block_values(sp, k)
                sp.wait_ge(gu_lo_done, k.n + 1)
                sp.dma_start(wgu[:, buf, :, 0:FF], I["w_exp_gate"][0, e].rearrange("(k p) f -> p k f", p=P), cond=new).then_inc(gu_in[k.buf], 16)
                sp.dma_start(wgu[:, buf, :, FF:], I["w_exp_up"][0, e].rearrange("(k p) f -> p k f", p=P), cond=new).then_inc(gu_in[k.buf], 16)

            def load_d(k):
                e, buf, new = block_values(sp, k)
                sp.wait_ge(d_lo_done, k.n + 1)
                sp.dma_start(wd[:, buf], I["w_exp_down"][0, e].rearrange("(k p) d -> p k d", p=P), cond=new).then_inc(d_in[k.buf], 16)

            def body(t, left):
                if left >= 3:
                    load_gu(t.next().next().next())
                if not (isinstance(t.n, int) and t.n == 0):
                    store(Step(t.i, t.c - 1))
                if left >= 2:
                    load_d(t.next().next())

            def store(t):
                sp.wait_ge(y_read, t.n + 2)
                sp.dma_start(M["y_slots"][bass.ds(t.n * P, P), :], y[:]).then_inc(y_out, 16)

            load_gu(Step(0, 0))
            load_d(Step(0, 0))
            load_gu(Step(0, 1))
            load_d(Step(0, 1))
            load_gu(Step(0, 2))
            blocks(sp, body)
            store(Step(0, BLOCKS - 1))
            sp.wait_ge(y_out, 16 * (BLOCKS + 1))

        @block.gpsimd
        def _(pool):
            pool.sem_inc(d_lo_done, 2)

            def gather(k):
                pool.wait_ge(x_turned, k.n + 1)
                pool.tensor_copy(idx[k.buf][:], token[:, bass.ds(k.n, 1)]).then_inc(idx_done, 1)
                pool.wait_ge(idx_done, k.n + 1)
                pool.sem_inc(started, 1)
                pool.indirect_dma_start(xg[:, k.buf], None, M["h2"],
                                        bass.IndirectOffsetOnAxis(ap=idx[k.buf][:], axis=0)).then_inc(xg_in[k.buf], 16)

            def body(t, left):
                if left >= 2:
                    gather(t.next().next())
                buf = weight_buffer(pool, t)
                pool.wait_ge(d_hi_done, t.n + 1)
                for half in range(2):
                    op = split_low(pool, wd_lo[:, t.buf, half], wd[:, buf, half], wd_hi[:, t.buf, half])
                op.then_inc(d_lo_done, 1)
            gather(Step(0, 0))
            gather(Step(0, 1))
            blocks(pool, body)

        @block.tensor
        def _(pe):
            ident = C["ident"]
            pe.sem_inc(y_done, 2)
            pe.sem_inc(x_turned, 2)
            pe.sem_inc(gu_done, 2)
            pe.sem_inc(h_turned, 2)

            def turn_x(k):
                pe.wait_ge(xg_in[k.buf], k.nth * 16 + 16)
                pe.wait_ge(x_lo_done, k.n + 1)
                for j in range(KT):
                    mm = pe.transpose(x_ps[:, j * P:(j + 1) * P], xg[:, k.buf, j * P:(j + 1) * P], ident[:])
                mm.then_inc(x_turned, 1)

            def gate_up(k):
                pe.wait_ge(x_lo_done, k.n + 2)
                pe.wait_ge(gu_lo_done, k.n + 3)
                pe.wait_ge(hid_done, k.n + 1)
                for j in range(KT):
                    cols = slice(j * P, (j + 1) * P)
                    mm = split_product(pe, gu_ps[k.buf][:], xT_hi[:, cols], xT_lo[:, cols],
                                       wgu_hi[:, k.buf, j], wgu_lo[:, k.buf, j], j == 0, j == KT - 1)
                mm.then_inc(gu_done, 1)

            def body(t, left):
                if left >= 1:
                    gate_up(t.next())
                pe.wait_ge(hid_done, t.n + 3)
                pe.wait_ge(hidT_done, t.n + 1)
                for j in range(2):
                    mm = pe.transpose(h_ps[:, j * P:(j + 1) * P], hid[:, j * P:(j + 1) * P], ident[:])
                mm.then_inc(h_turned, 1)
                if left >= 2:
                    turn_x(t.next().next())
                pe.wait_ge(hidT_done, t.n + 2)
                pe.wait_ge(d_lo_done, t.n + 3)
                pe.wait_ge(y_read, t.n + 1)
                for half in range(2):
                    cols = slice(half * 512, (half + 1) * 512)
                    for j in range(2):
                        mm = split_product(pe, y_ps[:, cols], hidT_hi[:, j * P:(j + 1) * P], hidT_lo[:, j * P:(j + 1) * P],
                                           wd_hi[:, t.buf, j, cols], wd_lo[:, t.buf, j, cols], j == 0, j == 1)
                mm.then_inc(y_done, 1)

            turn_x(Step(0, 0))
            gate_up(Step(0, 0))
            turn_x(Step(0, 1))
            blocks(pe, body)

        @block.scalar
        def _(act):
            act.sem_inc(y_read, 1)
            act.sem_inc(y_out, 16)

            def gu_high(k):
                buf = weight_buffer(act, k)
                act.wait_ge(gu_in[k.buf], k.nth * 32 + 32)
                act.wait_ge(gu_done, k.n + 1)
                for j in range(0, KT, 2):
                    act.copy(wgu_hi[:, k.buf, j:j + 2], wgu[:, buf, j:j + 2]).then_inc(gu_hi_done, 1)

            def d_high(k):
                buf = weight_buffer(act, k)
                act.wait_ge(d_in[k.buf], k.nth * 16 + 16)
                act.wait_ge(y_done, k.n + 1)
                act.copy(wd_hi[:, k.buf], wd[:, buf]).then_inc(d_hi_done, 1)

            def x_high(k):
                act.wait_ge(x_turned, k.n + 3)
                act.wait_ge(gu_done, k.n + 2)
                act.copy(xT_hi[:], x_ps[:]).then_inc(x_hi_done, 1)

            def silu(k):
                act.wait_ge(gu_done, k.n + 3)
                act.wait_ge(hid_done, k.n + 2)
                act.activation(act_g[:], gu_ps[k.buf][:, 0:FF], ACT.Silu).then_inc(silu_done, 1)

            def evacuate(t):
                act.wait_ge(y_done, t.n + 3)
                act.wait_ge(y_out, t.n * 16 + 16)
                act.copy(y[:], y_ps[:]).then_inc(y_read, 1)

            def body(t, left):
                if left >= 2:
                    gu_high(t.next().next())
                if not (isinstance(t.n, int) and t.n == 0):
                    evacuate(Step(t.i, t.c - 1))
                if left >= 1:
                    d_high(t.next())
                    silu(t.next())
                if left >= 2:
                    x_high(t.next().next())

            gu_high(Step(0, 0))
            x_high(Step(0, 0))
            gu_high(Step(0, 1))
            d_high(Step(0, 0))
            silu(Step(0, 0))
            x_high(Step(0, 1))
            blocks(act, body)
            evacuate(Step(0, BLOCKS - 1))

        @block.vector
        def _(dve):
            dve.sem_inc(gu_lo_done, 2)
            dve.sem_inc(x_lo_done, 1)
            dve.sem_inc(hid_done, 2)
            dve.sem_inc(hidT_done, 1)

            def gu_low(k):
                buf = weight_buffer(dve, k)
                for j in range(0, KT, 2):
                    dve.wait_ge(gu_hi_done, k.n * (KT // 2) + (j // 2 + 1))
                    op = split_low(dve, wgu_lo[:, k.buf, j:j + 2], wgu[:, buf, j:j + 2], wgu_hi[:, k.buf, j:j + 2])
                op.then_inc(gu_lo_done, 1)

            def x_low(k):
                dve.wait_ge(x_hi_done, k.n + 1)
                split_low(dve, xT_lo[:], x_ps[:], xT_hi[:]).then_inc(x_lo_done, 1)

            def hidden(k):
                dve.wait_ge(silu_done, k.n + 1)
                dve.wait_ge(h_turned, k.n + 2)
                dve.scalar_tensor_tensor(out=hid[:], in0=gu_ps[k.buf][:, FF:2 * FF], scalar=weight[:, bass.ds(k.n, 1)],
                                         in1=act_g[:], op0=ALU.mult, op1=ALU.mult).then_inc(hid_done, 1)

            def body(t, left):
                hidden(t)
                if left >= 2:
                    gu_low(t.next().next())
                dve.wait_ge(h_turned, t.n + 3)
                dve.wait_ge(y_done, t.n + 2)
                dve.tensor_copy(hidT_hi[:], h_ps[:, 0:FF])
                dve.drain()
                split_low(dve, hidT_lo[:], h_ps[:, 0:FF], hidT_hi[:]).then_inc(hidT_done, 1)
                if left >= 2:
                    x_low(t.next().next())

            gu_low(Step(0, 0))
            x_low(Step(0, 0))
            gu_low(Step(0, 1))
            x_low(Step(0, 1))
            blocks(dve, body)


def final_stage(nc, I, C, W, M):
    with ExitStack() as ctx:
        s = Scope(nc, ctx, "fin")
        gate, gain = s.sb("gate", [P, 2, D]), s.sb("gain", [P, D])
        ya, yb = s.sb("ya", [P, 2, D]), s.sb("yb", [P, 2, D])
        idx = [[s.sb(f"idx{c}{u}", [P, 1], U32) for u in range(2)] for c in range(2)]
        out, junk = s.sb("out", [P, 2, D]), s.sb("junk", [P, D])
        ssq, rstd, tmp, epsc = s.sb("ssq", [P, 2]), s.sb("rstd", [P, 2]), s.sb("tmp", [P, 1]), s.sb("epsc", [P, 1])
        g_in, idx_done = s.sem("g_in"), s.sem("idx_done")
        y_in = [s.sem(f"y_in{u}") for u in range(2)]
        x3_done, sq_done, out_done, out_stored = s.sem("x3_done"), s.sem("sq_done"), s.sem("out_done"), [s.sem(f"out_stored{u}") for u in range(2)]
        block = ctx.enter_context(nc.Block())
        started = s.sem("started")
        x2, slot_of = W["x2"], W["slot_of"]

        def tiles(eng, body, first=lambda t: None):
            first(Step(0, 0))
            body(Step(0, 0), True)
            with eng.Fori(0, STILES // 2 - 1) as i:
                body(Step(i, 1), True)
                body(Step(i, 2), True)
            body(Step(0, TILES - 2), True)
            body(Step(0, TILES - 1), False)

        def is_first(t):
            return isinstance(t.n, int) and t.n == 0

        @block.sync
        def _(sp):
            for cond in range(2):
                sp.dma_start(gate[:, cond], row_bcast(M["mods"][cond, GATE2 * D:(GATE2 + 1) * D])).then_inc(g_in, 16)
            sp.dma_start(gain[:], row_bcast(I["final_norm_g"])).then_inc(g_in, 16)

            def body(t, more):
                dst = I["y_prompt"][0] if is_first(t) else I["y_sample"][0, bass.ds((t.n - 1) * P, P), :]
                sp.wait_ge(out_done, t.n + 1)
                sp.dma_start(dst, out[:, t.buf]).then_inc(out_stored[t.buf], 16)
            tiles(sp, body)
            sp.wait_ge(out_stored[0], 16 * 6)
            sp.wait_ge(out_stored[1], 16 * 5)

        @block.gpsimd
        def _(pool):
            def body(t, more):
                pool.wait_ge(x3_done, t.n + 1)
                for c in range(2):
                    pool.tensor_copy(idx[c][t.buf][:], slot_of[:, t.n, c:c + 1]).then_inc(idx_done, 1)
                pool.wait_ge(idx_done, t.n * 2 + 2)
                pool.sem_inc(started, 1)
                for c, dst in enumerate((ya, yb)):
                    pool.indirect_dma_start(dst[:, t.buf], None, M["y_slots"],
                                            bass.IndirectOffsetOnAxis(ap=idx[c][t.buf][:], axis=0)).then_inc(y_in[t.buf], 16)
            tiles(pool, body)

        @block.scalar
        def _(act):
            def body(t, more):
                act.wait_ge(x3_done, t.n + 3)
                act.activation(junk[:], x2[:, t.n], ACT.Square, accum_out=ssq[:, t.buf:t.buf + 1])
                act.drain()
                act.activation(rstd[:, t.buf:t.buf + 1], ssq[:, t.buf:t.buf + 1], ACT.Sqrt, bias=epsc[:, 0:1],
                               scale=1.0 / D).then_inc(sq_done, 1)
            tiles(act, body)

        @block.vector
        def _(dve):
            dve.memset(epsc[:], EPS)
            dve.sem_inc(x3_done, 2)
            for u in range(2):
                dve.sem_inc(out_stored[u], 16)
            dve.wait_ge(g_in, 48)

            def residual(t):
                cond = 0 if is_first(t) else 1
                dve.wait_ge(y_in[t.buf], t.nth * 32 + 32)
                dve.tensor_tensor(ya[:, t.buf], ya[:, t.buf], yb[:, t.buf], ALU.add)
                dve.drain()
                dve.tensor_tensor(ya[:, t.buf], ya[:, t.buf], gate[:, cond], ALU.mult)
                dve.drain()
                dve.tensor_tensor(x2[:, t.n], x2[:, t.n], ya[:, t.buf], ALU.add).then_inc(x3_done, 1)

            def body(t, more):
                if more:
                    residual(t.next())
                r = rstd[:, t.buf:t.buf + 1]
                dve.wait_ge(sq_done, t.n + 1)
                dve.reciprocal(r, r)
                refine(dve, r, ssq[:, t.buf:t.buf + 1], 1.0 / D, tmp[:])
                dve.wait_ge(out_stored[t.buf], t.nth * 16 + 16)
                dve.scalar_tensor_tensor(out=out[:, t.buf], in0=x2[:, t.n], scalar=r, in1=gain[:], op0=ALU.mult,
                                         op1=ALU.mult).then_inc(out_done, 1)
            tiles(dve, body, residual)


def load_stage(nc, tag, loads):
    with ExitStack() as ctx:
        loaded = Scope(nc, ctx, tag).sem("done")
        block = ctx.enter_context(nc.Block())

        @block.sync
        def _(sp):
            for dst, src in loads:
                sp.dma_start(dst, src).then_inc(loaded, 16)
            sp.wait_ge(loaded, 16 * len(loads))


def build(nc, I, M):
    with ExitStack() as ctx:
        s = Scope(nc, ctx, "all")
        C = {"ident": s.sb("ident", [P, P]), "cond": s.sb("cond", [P, KT, 2])}
        load_stage(nc, "load_ident", [(C["ident"][:], I["ident"])])
        W = {}
        with ExitStack() as mix_ctx:
            with ExitStack() as att_ctx:
                right = Scope(nc, att_ctx, "att_in")
                with ExitStack() as proj_ctx:
                    ps = Scope(nc, proj_ctx, "w")
                    W["w_in"], W["w_in_sems"] = ps.sb("w_in", [P, KT, IN_COLS]), [ps.sem(f"w_in_sem{b}") for b in range(6)]
                    ada_stage(nc, I, C, W, M)
                    W["kT"] = right.sb("kT", [P, HEADS, (TILES + 1) * P], side="right")
                    W["qT"] = right.sb("qT", [P, HEADS, TILES * P], side="right")
                    W["v_tok"] = right.sb("v_tok", [P, TILES + 1, 512], side="right")
                    W["dt_tok"] = right.sb("dt_tok", [P, TILES, 2 * SH], side="right")
                    projection_stage(nc, I, C, W, M)
                for name in ("tri_le", "tri_ge", "tri_lt"):
                    C[name] = s.sb(name, [P, P])
                load_stage(nc, "load_tri", [(C[name][:], I[name]) for name in ("tri_le", "tri_ge", "tri_lt")])
                m = Scope(nc, mix_ctx, "mix_in")
                W["y_tok"] = m.sb("y_tok", [P, TILES, DSSM])
                scan_stages(nc, I, C, W, M)
                W["o_tok"] = m.sb("o_tok", [P, TILES, DATT])
                W["w_out"], W["gain"] = m.sb("w_out", [P, KT, D]), m.sb("gain", [P, D])
                for name in ("gate", "amul", "aadd"):
                    W[name] = m.sb(name, [P, 2, D])
                W["w_out_in"], W["gains_in"] = m.sem("w_out_in"), m.sem("gains_in")
                attention_stage(nc, I, C, W, M)
            r = Scope(nc, ctx, "moe_in")
            W["x2"] = r.sb("x2", [P, TILES, D], side="right")
            W["logits"] = r.sb("logits", [P, TILES, NG + NE], side="right")
            mixer_stage(nc, I, C, W, M)
        W["block_expert"] = s.sb("block_expert", [P, BLOCKS], I32)
        W["block_new"], W["block_buf"] = s.sb("block_new", [P, BLOCKS], I32), s.sb("block_buf", [P, BLOCKS], I32)
        W["block_token"] = s.sb("block_token", [P, BLOCKS], U32)
        W["block_weight"] = s.sb("block_weight", [P, BLOCKS])
        W["slot_of"] = s.sb("slot_of", [P, TILES, 2], U32)
        routing_stage(nc, I, C, W, M)
        expert_stage(nc, I, C, W, M)
        final_stage(nc, I, C, W, M)


_INS = ['x_prompt', 'x_sample', 'cache_k', 'cache_v', 'state_ssm_fwd', 'state_ssm_bwd', 'c', 'c_ctx', 'w_ada', 'b_ada',
        'norm_mix_g', 'w_in', 'w_out', 'lambda_q1', 'lambda_k1', 'lambda_q2', 'lambda_k2', 'attn_subln_g', 'conv_w',
        'conv_b', 'a_log_fwd', 'a_log_bwd', 'dt_bias_fwd', 'dt_bias_bwd', 'ssm_d', 'ssm_norm_g', 'norm_ffn_g',
        'w_group_router', 'b_group_router', 'w_expert_router', 'b_expert_router', 'w_exp_gate', 'w_exp_up',
        'w_exp_down', 'final_norm_g']
_OUTS = {'y_prompt': (1, P, D), 'y_sample': (1, STILES * P, D), 'new_k': (1, 1, P, HEADS, 2, QKD),
         'new_v': (1, 1, P, HEADS, P), 'new_hf': (1, 1, SH, 64, P), 'new_hb': (1, 1, SH, 64, P)}
_SCRATCH = {'mods': (2, 6 * D), 'z': (TILES * P, 512), 'xbc': (TILES * P, XBC),
            'h2': (TILES * P, D), 'slots': (SLOTS, 2), 'y_slots': (SLOTS, D)}
_DEBUG = []


def shape_constants():
    i = np.arange(P)
    c = {
        'ident': np.eye(P, dtype=np.float32),
        'tri_le': (i[:, None] <= i[None, :]).astype(np.float32),
        'tri_ge': (i[:, None] >= i[None, :]).astype(np.float32),
        'tri_lt': (i[:, None] < i[None, :]).astype(np.float32),
        'pick': np.repeat(np.eye(2 * SH, dtype=np.float32)[:, :, None], P, axis=2),
    }
    c['steps'] = np.arange(BLOCKS, dtype=np.float32)
    c['tokens'] = (i[:, None] + P * np.arange(TILES)[None, :]).astype(np.float32)
    pos = np.arange(STILES * P)
    freqs = np.float32(10000.0) ** (-np.arange(16, dtype=np.float32) / np.float32(16))
    rope = np.zeros((TILES, P, 2, 2, 2, 16), np.float32)
    rope[0, :, 0] = 1.0
    for axis, ids in enumerate((pos // 64, pos % 64)):
        ang = (ids.astype(np.float32)[:, None] * freqs).reshape(STILES, P, 16)
        rope[1:, :, 0, axis, 0] = rope[1:, :, 0, axis, 1] = np.cos(ang)
        rope[1:, :, 1, axis, 0] = -np.sin(ang)
        rope[1:, :, 1, axis, 1] = np.sin(ang)
    c['rope'] = rope.reshape(TILES, P, 2, QKD)
    return c


def kernel(**inputs):
    import concourse.bacc as _bacc
    from concourse.bass_utils import run_bass_kernel_spmd as _run

    nc = _bacc.Bacc("TRN2", target_bir_lowering=False, num_devices=1)
    arrays, io = {}, {}
    for name in _INS:
        arrays[f"in_{name}"] = np.ascontiguousarray(inputs[name])
    for name, a in shape_constants().items():
        arrays[f"in_{name}"] = a
    for name, a in arrays.items():
        io[name[3:]] = nc.dram_tensor(name, a.shape, F32, kind="ExternalInput").ap()
    for name, shape in _OUTS.items():
        io[name] = nc.dram_tensor(f"out_{name}", shape, F32, kind="ExternalOutput").ap()
    scratch = {name: nc.dram_tensor(f"scratch_{name}", shape, F32,
                                    kind="ExternalOutput" if name in _DEBUG else "Internal").ap()
               for name, shape in _SCRATCH.items()}
    build(nc, io, scratch)
    r = _run(nc, [arrays], core_ids=[0])
    if _DEBUG:
        return tuple(r.results[0][f"scratch_{n}"] if n in _SCRATCH else r.results[0][f"out_{n}"] for n in _DEBUG)
    return tuple(r.results[0][f"out_{name}"] for name in _OUTS)
```

```python
import math
from contextlib import ExitStack

import numpy as np

import concourse.bass as bass
from concourse import mybir

P = 128
D = 1024
KT = D // P
TILES = 9
STILES = 8
HEADS = 4
QKD = 64
DQK = 512
DATT = 512
DSSM = 512
SH = 8
SG = 2
HG = SH // SG
XBC = 1024
NXBC = XBC // P
IN_COLS = 2 * DQK + DATT + DSSM + XBC + 2 * SH
CONV = 5
NG = 4
EPG = 4
NE = NG * EPG
FF = 256
EPS = 1e-6
LAM0 = 0.8 - 0.6 * math.exp(-0.0)
SCALE = QKD ** -0.5
BLOCKS = 2 * TILES + NE - 1
SLOTS = BLOCKS * P
CIN = 2 + P + 2 + STILES * P + 2
COUT = CIN - 4
ADA_COLS, ADA_FIRST = 512, 2 * D // 512
SHIFT1, SCALE1, GATE1, SHIFT2, SCALE2, GATE2 = range(6)

ALU = mybir.AluOpType
ACT = mybir.ActivationFunctionType
F32 = mybir.dt.float32
F32R = mybir.dt.float32r
I32 = mybir.dt.int32
U32 = mybir.dt.uint32
AX = mybir.AxisListType.X


class Scope:

    def __init__(self, nc, ctx, tag):
        self.nc, self.ctx, self.tag, self.sems = nc, ctx, tag, []
        ctx.callback(self.close)

    def sb(self, name, shape, dt=F32, side=None):
        return self.ctx.enter_context(self.nc.sbuf_tensor(f"{self.tag}_{name}", shape, dt, side=side))

    def ps(self, name, cols=512):
        return self.ctx.enter_context(self.nc.psum_tensor(f"{self.tag}_{name}_ps", [P, cols], F32))

    def sem(self, name):
        self.sems.append(self.nc.alloc_semaphore(name=f"{self.tag}_{name}"))
        return self.sems[-1]

    def close(self):
        if self.sems:
            self.nc.clear_and_free_semaphores(self.sems)
            self.nc.all_engine_barrier()


def split_low(eng, low, value, high):
    return eng.tensor_tensor(low, value, high.bitcast(F32), ALU.subtract)


def split_product(pe, out, a_high, a_low, b_high, b_low, start, stop):
    pe.matmul(out, a_high, b_high, start=start, stop=False)
    pe.matmul(out, a_high, b_low, start=False, stop=False)
    return pe.matmul(out, a_low, b_high, start=False, stop=stop)


class Step:

    def __init__(self, i, c, bufs=2):
        self.i, self.c, self.bufs = i, c, bufs
        self.buf = c % bufs
        self.n = i * bufs + c
        self.nth = i + c // bufs

    def next(self):
        return Step(self.i, self.c + 1, self.bufs)


def bcast(ap, n, axis):
    shape = list(ap.shape)
    shape.insert(axis, n)
    return ap.unsqueeze(axis).to_broadcast(shape)


def row_bcast(row, n=P):
    return row.unsqueeze(0).to_broadcast([n, row.shape[0]])


def ada_stage(nc, I, C, W, M):
    NB, W_COLS, CB = 4, ADA_COLS, ADA_FIRST
    w_ada = I["w_ada"][0].rearrange("(p j) n -> p j n", j=KT)
    with ExitStack() as ctx:
        s = Scope(nc, ctx, "ada")
        raw, cond = s.sb("raw", [P, 2, KT]), C["cond"]
        w = s.sb("w", [P, NB, KT, W_COLS])
        rows = s.sb("rows", [2, CB * W_COLS])
        acc = [s.ps(f"acc{u}") for u in range(NB)]
        in_sem, w_ada_in = s.sem("cond_in"), [s.sem(f"w_ada_in{u}") for u in range(NB)]
        silu_done = s.sem("silu_done")
        mm_done, row_done, stored = s.sem("mm_done"), s.sem("row_done"), s.sem("stored")
        block = ctx.enter_context(nc.Block())

        @block.sync
        def _(sp):
            sp.dma_start(raw[:, 0], I["c_ctx"].rearrange("(p j) -> p j", j=KT)).then_inc(in_sem, 16)
            sp.dma_start(raw[:, 1], I["c"][0].rearrange("(p j) -> p j", j=KT)).then_inc(in_sem, 16)
            sp.dma_start(rows[:], row_bcast(I["b_ada"][0, 0:CB * W_COLS], 2)).then_inc(in_sem, 16)
            for u in range(NB):
                sp.dma_start(w[:, u], w_ada[:, :, u * W_COLS:(u + 1) * W_COLS]).then_inc(w_ada_in[u], 16)

        @block.scalar
        def _(act):
            act.wait_ge(in_sem, 48)
            act.activation(cond[:].rearrange("p k c -> p c k"), raw[:], ACT.Silu).then_inc(silu_done, 1)
            act.wait_ge(row_done, CB)
            act.dma_start(M["mods"][:, 0:CB * W_COLS], rows[:]).then_inc(stored, 16)
            act.wait_ge(stored, 16)

        @block.tensor
        def _(pe):
            pe.wait_ge(silu_done, 1)
            for u in range(NB):
                pe.wait_ge(w_ada_in[u], 16)
                for k in range(KT):
                    mm = pe.matmul(acc[u][0:2, :], cond[:, k, :], w[:, u, k, :], start=(k == 0), stop=(k == KT - 1))
                mm.then_inc(mm_done, 1)

        @block.vector
        def _(dve):
            dve.wait_ge(in_sem, 48)
            for u in range(NB):
                dve.wait_ge(mm_done, u + 1)
                cols = rows[:, u * W_COLS:(u + 1) * W_COLS]
                dve.tensor_tensor(cols, acc[u][0:2, :], cols, ALU.add).then_inc(row_done, 1)


def projection_stage(nc, I, C, W, M, part):
    qkv = part == "qkv"
    base = 0 if qkv else 2 * DQK + DATT
    NCOL = 3 * 512 + (0 if qkv else 2 * SH)
    PIECES, RAW = 12, 5
    with ExitStack() as ctx:
        s = Scope(nc, ctx, part)
        amul, aadd = W["amul1"], W["aadd1"]
        x, h = s.sb("x", [P, 2, D]), s.sb("h", [P, D])
        gain = h
        hT_hi, hT_lo = (s.sb(k, [P, 2, KT, P], F32R) for k in ("hT_hi", "hT_lo"))
        w_hi, w_lo = (s.sb(k, [P, KT, NCOL], F32R) for k in ("w_hi", "w_lo"))
        raw = (W["v_tok"][:, TILES + 1 - 2 * RAW:, :].rearrange("p (r k) n -> p r k n", k=2) if qkv
               else s.sb("raw", [P, RAW, 2, 512 + 2 * SH]))
        ssq, std, rstd = s.sb("ssq", [P, 2]), s.sb("std", [P, 2]), s.sb("rstd", [P, 2])
        epsc = s.sb("epsc", [P, 1])
        turned = s.ps("turned", 1024)
        acc = [s.ps(f"acc{u}") for u in range(3)]
        mods_in, x_in = s.sem("mods_in"), [s.sem(f"x_in{u}") for u in range(2)]
        raw_in = [s.sem(f"raw_in{u}") for u in range(RAW)]
        piece_high, piece_low = s.sem("piece_high"), s.sem("piece_low")
        mods_done, std_done, h_done = s.sem("mods_done"), s.sem("std_done"), s.sem("h_done")
        turn_done, high_done, low_done = s.sem("turn_done"), s.sem("high_done"), s.sem("low_done")
        acc_done = [s.sem(f"acc_done{u}") for u in range(3)]
        dt_tok = W["dt_tok"]
        if qkv:
            qT, kT, v_tok = W["qT"], W["kT"], W["v_tok"]
            rope = s.sb("rope", [P, 2, 2, QKD])
            q_out, k_rot = s.sb("q_out", [P, 512]), s.sb("k_rot", [P, 512])
            swap = W["kT"][:, :, TILES * P:(TILES + 1) * P]
            q_turned, k_turned = s.ps("q_turned"), s.ps("k_turned")
            rope_in = [s.sem(f"rope_in{u}") for u in range(2)]
            q_rot_done, q_turn_done, qT_done = s.sem("q_rot_done"), s.sem("q_turn_done"), s.sem("qT_done")
            k_rot_done, k_turn_done, kT_done = s.sem("k_rot_done"), s.sem("k_turn_done"), s.sem("kT_done")
            v_read = s.sem("v_read")
            ctx_in, ctx_kin, new_stored = s.sem("ctx_in"), s.sem("ctx_kin"), [s.sem(f"new_stored{u}") for u in range(2)]
            products_done = acc_done[2]
        else:
            stage = s.sb("stage", [P, 3, 512])
            dt_acc = s.ps("dt_acc")
            dt_done, dt_read = s.sem("dt_done"), s.sem("dt_read")
            staged, stored = [s.sem(f"staged{u}") for u in range(3)], [s.sem(f"stored{u}") for u in range(3)]
            products_done = dt_done
        block = ctx.enter_context(nc.Block())

        def piece(m):
            b, q = m // 4, m % 4
            return slice(2 * q, 2 * q + 2), slice(b * 512, (b + 1) * 512 if b < 2 else NCOL)

        def piece_raw(m):
            cols = piece(m)[1]
            return raw[:, m % RAW, :, 0:cols.stop - cols.start]

        def tiles(eng, body):
            body(Step(0, 0), True)
            with eng.Fori(0, STILES // 2 - 1) as i:
                body(Step(i, 1), True)
                body(Step(i, 2), True)
            body(Step(0, TILES - 2), True)
            body(Step(0, TILES - 1), False)

        def is_first(t):
            return isinstance(t.n, int) and t.n == 0

        @block.sync
        def _(sp):
            def load(t):
                sp.wait_ge(h_done, t.n + 1)
                sp.dma_start(x[:, t.buf], I["x_prompt"][0] if is_first(t) else I["x_sample"][0, bass.ds((t.n - 1) * P, P), :]
                             ).then_inc(x_in[t.buf], 16)
                if qkv:
                    sp.wait_ge(k_rot_done, t.n + 1)
                    sp.dma_start(rope[:, t.buf], I["rope"][t.n]).then_inc(rope_in[t.buf], 16)

            def store(t):
                for u, dst in ((0, M["z"][bass.ds(t.n * P, P), :]), (1, M["xbc"][bass.ds(t.n * P, P), 0:512]),
                               (2, M["xbc"][bass.ds(t.n * P, P), 512:1024])):
                    sp.wait_ge(staged[u], t.n + 2)
                    sp.dma_start(dst, stage[:, u]).then_inc(stored[u], 16)

            w_src = I["w_in"][0, :, base:base + NCOL].rearrange("(k p) n -> p k n", p=P)
            load(Step(0, 0))
            for m in range(PIECES):
                ks, cols = piece(m)
                sp.wait_ge(piece_low, m + 1)
                sp.dma_start(piece_raw(m), w_src[:, ks, cols]).then_inc(raw_in[m % RAW], 16)
                if m == 3:
                    load(Step(0, 1))
            load(Step(0, 2))
            if qkv:
                sp.wait_ge(k_rot_done, 3)
                sp.dma_start(I["new_k"][0, 0].rearrange("t h m d -> t (h m d)"), k_rot[:]).then_inc(new_stored[0], 16)
                sp.wait_ge(v_read, 2)
                sp.dma_start(I["new_v"][0, 0].rearrange("t h d -> t (h d)"), v_tok[:, 0, :]).then_inc(new_stored[1], 16)
            else:
                store(Step(0, 0))
            with sp.Fori(0, STILES // 2 - 1) as i:
                for c in (1, 2):
                    load(Step(i, c + 2))
                    if not qkv:
                        store(Step(i, c))
            if not qkv:
                store(Step(0, TILES - 2))
                store(Step(0, TILES - 1))
                for u in range(3):
                    sp.wait_ge(stored[u], 16 * (TILES + 1))
                return
            sp.wait_ge(kT_done, TILES + 1)
            sp.dma_start(k_rot[:], I["cache_k"][0, 0].rearrange("t h m d -> t (h m d)")).then_inc(ctx_kin, 16)
            sp.dma_start(v_tok[:, TILES, :], I["cache_v"][0, 0].rearrange("t h d -> t (h d)")).then_inc(ctx_in, 16)
            sp.wait_ge(ctx_in, 16)
            for u in range(2):
                sp.wait_ge(new_stored[u], 16)

        @block.scalar
        def _(act):
            if not qkv:
                act.dma_start(gain[:], row_bcast(I["norm_mix_g"][0])).then_inc(mods_in, 16)
                for cond in range(2):
                    act.dma_start(amul[:, cond], row_bcast(M["mods"][cond, SCALE1 * D:(SCALE1 + 1) * D])).then_inc(mods_in, 16)
                    act.dma_start(aadd[:, cond], row_bcast(M["mods"][cond, SHIFT1 * D:(SHIFT1 + 1) * D])).then_inc(mods_in, 16)
            if qkv:
                act.sem_inc(v_read, 1)
            else:
                for u in range(3):
                    act.sem_inc(staged[u], 1)
                    act.sem_inc(stored[u], 16)

            def norm(t):
                act.wait_ge(x_in[t.buf], t.nth * 16 + 16)
                act.wait_ge(turn_done, t.n + 1)
                act.activation(h[:], x[:, t.buf], ACT.Square, accum_out=ssq[:, t.buf:t.buf + 1])
                act.drain()
                act.activation(std[:, t.buf:t.buf + 1], ssq[:, t.buf:t.buf + 1], ACT.Sqrt, bias=epsc[:, 0:1],
                               scale=1.0 / D).then_inc(std_done, 1)

            def high(t):
                act.wait_ge(turn_done, t.n + 2)
                act.wait_ge(products_done, t.n + 1)
                act.copy(hT_hi[:, t.buf].rearrange("p k t -> p (k t)"), turned[:]).then_inc(high_done, 1)

            def column_out(t, u):
                act.wait_ge(acc_done[u], t.n + 1)
                act.wait_ge(stored[u], t.n * 16 + 16)
                act.copy(stage[:, u], acc[u][:]).then_inc(staged[u], 1)

            def body(t, more):
                if more and not is_first(t):
                    norm(t.next())
                if not qkv:
                    column_out(t, 0)
                    column_out(t, 1)
                if more:
                    high(t.next())
                if qkv:
                    act.wait_ge(acc_done[2], t.n + 3)
                    act.copy(v_tok[:, t.n, :], acc[2][:]).then_inc(v_read, 1)
                else:
                    column_out(t, 2)

            act.wait_ge(mods_done, 1)
            for m in range(PIECES):
                if m == 0:
                    norm(Step(0, 0))
                elif m == 3:
                    high(Step(0, 0))
                elif m == 8:
                    norm(Step(0, 1))
                ks, cols = piece(m)
                act.wait_ge(raw_in[m % RAW], 16 * (m // RAW + 1))
                act.copy(w_hi[:, ks, cols], piece_raw(m)).then_inc(piece_high, 1)
            tiles(act, body)

        @block.vector
        def _(dve):
            dve.sem_inc(h_done, 2)
            dve.sem_inc(low_done, 1)
            dve.sem_inc(piece_low, RAW)
            if qkv:
                dve.sem_inc(k_rot_done, 2)
                dve.sem_inc(q_rot_done, 1)
                dve.sem_inc(qT_done, 1)
                dve.sem_inc(kT_done, 1)
            else:
                dve.sem_inc(dt_read, 1)
            op = dve.memset(epsc[:], EPS)
            if not qkv:
                dve.wait_ge(mods_in, 80)
                for cond in range(2):
                    op = dve.scalar_tensor_tensor(out=amul[:, cond], in0=amul[:, cond], scalar=1.0, in1=gain[:],
                                                  op0=ALU.add, op1=ALU.mult)
            op.then_inc(mods_done, 1)
            dve.wait_ge(mods_done, 1)

            def norm(t):
                cond = 0 if is_first(t) else 1
                dve.wait_ge(std_done, t.n + 1)
                r = rstd[:, t.buf:t.buf + 1]
                dve.reciprocal(r, std[:, t.buf:t.buf + 1])
                dve.drain()
                dve.scalar_tensor_tensor(out=h[:], in0=x[:, t.buf], scalar=r, in1=amul[:, cond], op0=ALU.mult, op1=ALU.mult)
                dve.drain()
                dve.tensor_tensor(h[:], h[:], aadd[:, cond], ALU.add).then_inc(h_done, 1)

            def low(t):
                dve.wait_ge(high_done, t.n + 1)
                split_low(dve, hT_lo[:, t.buf].rearrange("p k t -> p (k t)"), turned[:],
                          hT_hi[:, t.buf].rearrange("p k t -> p (k t)")).then_inc(low_done, 1)

            def rotate(dst, src, t, done):
                cos = bcast(rope[:, t.buf, 0, :], 8, 1)
                sin = rope[:, t.buf, 1, :].rearrange("p (a s f) -> p a s f", a=2, s=2)
                v = src.rearrange("p (h m a s f) -> p h m a s f", h=HEADS, m=2, a=2, s=2)
                w = swap.rearrange("p h (m a s f) -> p h m a s f", m=2, a=2, s=2)
                for half in range(2):
                    for axis in range(2):
                        dve.tensor_tensor(w[:, :, :, axis, half, :], v[:, :, :, axis, 1 - half, :],
                                          bcast(bcast(sin[:, axis, half, :], 2, 1), HEADS, 1), ALU.mult)
                dve.tensor_tensor(dst.rearrange("p (g f) -> p g f", g=8), src.rearrange("p (g f) -> p g f", g=8),
                                  cos, ALU.mult)
                dve.drain()
                dve.tensor_tensor(dst.rearrange("p (h d) -> p h d", h=HEADS), dst.rearrange("p (h d) -> p h d", h=HEADS), swap,
                                  ALU.add).then_inc(done, 1)
                dve.drain()

            def take(dst, src, t):
                return dve.tensor_copy(dst[:, :, bass.ds(t.n * P, P)], src[:].rearrange("p (h t) -> p h t", h=HEADS))

            def body(t, more):
                if more and not is_first(t):
                    norm(t.next())
                if qkv:
                    dve.wait_ge(rope_in[t.buf], t.nth * 16 + 16)
                    dve.wait_ge(acc_done[0], t.n + 1)
                    dve.wait_ge(q_turn_done, t.n + 1)
                    rotate(q_out[:], acc[0][:], t, q_rot_done)
                    dve.wait_ge(acc_done[1], t.n + 1)
                    dve.wait_ge(k_turn_done, t.n + 1)
                    rotate(k_rot[:], acc[1][:], t, k_rot_done)
                if more:
                    low(t.next())
                if qkv:
                    dve.wait_ge(q_turn_done, t.n + 2)
                    take(qT, q_turned, t).then_inc(qT_done, 1)
                    dve.wait_ge(k_turn_done, t.n + 2)
                    take(kT, k_turned, t).then_inc(kT_done, 1)
                    if is_first(t):
                        dve.wait_ge(new_stored[0], 16)
                else:
                    dve.wait_ge(dt_done, t.n + 3)
                    dve.tensor_copy(dt_tok[:, t.n, :], dt_acc[:, 0:2 * SH]).then_inc(dt_read, 1)

            for m in range(PIECES):
                if m == 0:
                    norm(Step(0, 0))
                elif m == 3:
                    low(Step(0, 0))
                elif m == 8:
                    norm(Step(0, 1))
                ks, cols = piece(m)
                dve.wait_ge(piece_high, m + 1)
                split_low(dve, w_lo[:, ks, cols], piece_raw(m), w_hi[:, ks, cols]).then_inc(piece_low, 1)
            tiles(dve, body)
            if qkv:
                dve.wait_ge(k_turn_done, TILES + 2)
                dve.tensor_copy(kT[:, :, TILES * P:(TILES + 1) * P], k_turned[:].rearrange("p (h t) -> p h t", h=HEADS)).then_inc(kT_done, 1)

        @block.tensor
        def _(pe):
            ident = C["ident"]
            pe.sem_inc(turn_done, 1)
            pe.sem_inc(products_done, 2)
            if qkv:
                pe.sem_inc(k_turn_done, 1)
                pe.sem_inc(q_turn_done, 1)

            def turn(t):
                pe.wait_ge(h_done, t.n + 3)
                pe.wait_ge(low_done, t.n + 1)
                for k in range(KT):
                    mm = pe.transpose(turned[:, k * P:(k + 1) * P], h[:, k * P:(k + 1) * P], ident[:])
                mm.then_inc(turn_done, 1)

            def product(t, out, cols):
                for k in range(KT):
                    mm = split_product(pe, out, hT_hi[:, t.buf, k, :], hT_lo[:, t.buf, k, :], w_hi[:, k, cols], w_lo[:, k, cols],
                                       k == 0, k == KT - 1)
                return mm

            def block_product(t, b):
                if is_first(t):
                    pe.wait_ge(piece_low, RAW + 4 * (b + 1))
                product(t, acc[b][:], slice(b * 512, (b + 1) * 512)).then_inc(acc_done[b], 1)

            def turn_heads(dst, src, done):
                for hd in range(HEADS):
                    mm = pe.transpose(dst[:, hd * P:(hd + 1) * P], src[:, hd * P:(hd + 1) * P], ident[:])
                mm.then_inc(done, 1)

            def body(t, more):
                pe.wait_ge(low_done, t.n + 2)
                for b in range(3):
                    if not qkv:
                        pe.wait_ge(staged[b], t.n + 1)
                    elif b == 0:
                        pe.wait_ge(q_rot_done, t.n + 1)
                    elif b == 1:
                        pe.wait_ge(k_rot_done, t.n + 2)
                    else:
                        pe.wait_ge(v_read, t.n + 1)
                    block_product(t, b)
                    if b == 1 and more:
                        turn(t.next())
                    if b == 1 and qkv:
                        pe.wait_ge(q_rot_done, t.n + 2)
                        pe.wait_ge(qT_done, t.n + 1)
                        turn_heads(q_turned, q_out, q_turn_done)
                if qkv:
                    pe.wait_ge(k_rot_done, t.n + 3)
                    pe.wait_ge(kT_done, t.n + 1)
                    turn_heads(k_turned, k_rot, k_turn_done)
                else:
                    pe.wait_ge(dt_read, t.n + 1)
                    product(t, dt_acc[:, 0:2 * SH], slice(3 * 512, NCOL)).then_inc(dt_done, 1)

            turn(Step(0, 0))
            tiles(pe, body)
            if qkv:
                pe.wait_ge(ctx_kin, 16)
                pe.wait_ge(kT_done, TILES + 1)
                turn_heads(k_turned, k_rot, k_turn_done)


def conv_stage(nc, I, C, W, M):
    assert NXBC == 6 * D // ADA_COLS - ADA_FIRST
    w_ada = I["w_ada"][0].rearrange("(p j) n -> p j n", j=KT)
    w = W
    with ExitStack() as ctx:
        s = Scope(nc, ctx, "conv")
        dt_bias, a_neg = s.sb("dt_bias", [P, 2 * SH]), s.sb("a_neg", [P, 2 * SH])
        d_row = s.sb("d_row", [P, SH])
        taps = s.sb("taps", [P, NXBC, CONV + 1])
        ones = s.sb("ones", [P, P])
        t1, t2, t3, t4 = (s.sb(f"t{i}", [P, TILES, 2 * SH]) for i in range(4))
        la = s.sb("la", [P, TILES, 2 * SH])
        raw = s.sb("raw", [P, 2, TILES, P])
        xin = s.sb("xin", [P, 2, CIN])
        acc = s.sb("acc", [P, 2, COUT])
        taps_row = acc[0:CONV + 1, 0, 0:XBC]
        wa, rows = s.sb("wa", [P, 2, KT, ADA_COLS]), s.sb("rows", [2, 2, ADA_COLS])
        turned_in, turned_out = s.ps("turned_in", 1536), s.ps("turned_out", 1536)
        sums, row_ps = s.ps("sums"), s.ps("row")
        wa_in, row_stored = [s.sem(f"wa_in{u}") for u in range(2)], [s.sem(f"row_stored{u}") for u in range(2)]
        row_mm, row_done = s.sem("row_mm"), s.sem("row_done")
        small_in, raw_in = s.sem("small_in"), [s.sem(f"raw_in{u}") for u in range(2)]
        exp_done, ln_done, a_done, pre_done = s.sem("exp_done"), s.sem("ln_done"), s.sem("a_done"), s.sem("pre_done")
        la_done, sums_done, cum_done, expo_done = s.sem("la_done"), s.sem("sums_done"), s.sem("cum_done"), s.sem("expo_done")
        taps_turned, taps_done = s.sem("taps_turned"), s.sem("taps_done")
        cumT_turned, cumT_done = s.sem("cumT_turned"), s.sem("cumT_done")
        zeroed, turn_done, xin_done = s.sem("zeroed"), s.sem("turn_done"), s.sem("xin_done")
        acc_done, smooth_done, back_done, tok_done = s.sem("acc_done"), s.sem("smooth_done"), s.sem("back_done"), s.sem("tok_done")
        kept, skip_done = s.sem("kept"), s.sem("skip_done")
        block = ctx.enter_context(nc.Block())
        tok, xbcT, y_tok, dt_tok = w["tok"], w["xbcT"], w["y_tok"], w["dt_tok"]
        cum, tot, ecum, dte, dec, cumT = (w[k] for k in ("cum", "tot", "ecum", "dte", "dec", "cumT"))
        xbc_dram = M["xbc"].rearrange("(t p) c -> p t c", p=P)

        def slices(eng, first, body):
            first(Step(0, 0))
            with eng.Fori(0, NXBC // 2 - 1) as i:
                body(Step(i, 0), True)
                body(Step(i, 1), True)
            body(Step(NXBC // 2 - 1, 0), True)
            body(Step(NXBC // 2 - 1, 1), False)

        @block.sync
        def _(sp):
            for half, (bias, alog) in enumerate((("dt_bias_fwd", "a_log_fwd"), ("dt_bias_bwd", "a_log_bwd"))):
                sp.dma_start(dt_bias[:, half * SH:(half + 1) * SH], row_bcast(I[bias][0])).then_inc(small_in, 16)
                sp.dma_start(a_neg[:, half * SH:(half + 1) * SH], row_bcast(I[alog][0])).then_inc(small_in, 16)
            sp.dma_start(d_row[:], row_bcast(I["ssm_d"][0])).then_inc(small_in, 16)
            sp.dma_start(taps_row[0:CONV, :], I["conv_w"][0]).then_inc(small_in, 16)
            sp.dma_start(taps_row[CONV:CONV + 1, :], I["conv_b"]).then_inc(small_in, 16)

            def load_raw(t):
                sp.dma_start(raw[:, t.buf], xbc_dram[:, :, bass.ds(t.n * P, P)]).then_inc(raw_in[t.buf], 16)

            def load_ada(t):
                sp.dma_start(wa[:, t.buf], w_ada[:, :, bass.ds((t.n + ADA_FIRST) * ADA_COLS, ADA_COLS)]).then_inc(wa_in[t.buf], 16)

            def load_bias(t):
                sp.dma_start(rows[:, t.buf], row_bcast(I["b_ada"][0, bass.ds((t.n + ADA_FIRST) * ADA_COLS, ADA_COLS)], 2)
                             ).then_inc(wa_in[t.buf], 16)

            def store_row(t):
                sp.wait_ge(row_done, t.n + 2)
                sp.dma_start(M["mods"][:, bass.ds((t.n + ADA_FIRST) * ADA_COLS, ADA_COLS)], rows[:, t.buf]
                             ).then_inc(row_stored[t.buf], 16)

            for c in range(2):
                load_raw(Step(0, c))
                load_ada(Step(0, c))
                load_bias(Step(0, c))
            with sp.Fori(0, NXBC // 2 - 1) as i:
                for c in range(2):
                    t, later = Step(i, c), Step(i, c + 2)
                    sp.wait_ge(turn_done, t.n + 1)
                    load_raw(later)
                    sp.wait_ge(row_mm, t.n + 1)
                    load_ada(later)
                    store_row(t)
                    sp.wait_ge(row_stored[t.buf], t.nth * 16 + 16)
                    load_bias(later)
            for c in range(2):
                store_row(Step(NXBC // 2 - 1, c))
            for c in range(2):
                sp.wait_ge(row_stored[c], 16 * NXBC // 2)

        @block.gpsimd
        def _(pool):
            pool.memset(ones[:], 1.0).then_inc(zeroed, 1)
            pool.memset(xin[:], 0.0).then_inc(zeroed, 1)
            pool.sem_inc(kept, 2 + 4)
            with pool.Fori(0, 2) as i:
                for u in range(2):
                    pool.wait_ge(smooth_done, i * 2 + (u + 7))
                    pool.tensor_copy(xbcT[:, i * 2 + u, :], acc[:, u]).then_inc(kept, 1)
            pool.wait_ge(tok_done, NXBC + 1)
            xs = tok[:, :, 0:DSSM].rearrange("p t (h d) -> p t h d", h=SH)
            for t in range(3):
                r = slice(3 * t, 3 * t + 3)
                pool.tensor_tensor(y_tok[:, r].rearrange("p t (h d) -> p t h d", h=SH), xs[:, r],
                                   bcast(bcast(d_row[:], 64, 2), 3, 1), ALU.mult).then_inc(skip_done, 1)
            pool.wait_ge(skip_done, 3)

        @block.scalar
        def _(act):
            act.wait_ge(small_in, 16 * 7)
            act.activation(a_neg[:], a_neg[:], ACT.Exp).then_inc(a_done, 1)
            act.wait_ge(pre_done, 1)
            act.activation(t2[:], t2[:], ACT.Exp).then_inc(exp_done, 1)
            act.wait_ge(pre_done, 2)
            act.activation(t4[:], t3[:], ACT.Ln).then_inc(ln_done, 1)
            act.wait_ge(cum_done, 1)
            act.activation(ecum[:], cum[:], ACT.Exp)
            act.activation(dec[:], tot[:], ACT.Exp)
            act.activation(t1[:], t1[:], ACT.Exp).then_inc(expo_done, 1)
            act.wait_ge(cumT_turned, 1)
            act.copy(cumT[:], turned_out[0:2 * SH, 0:TILES * P]).then_inc(cumT_done, 1)
            act.sem_inc(xin_done, 1)
            act.sem_inc(smooth_done, 2)
            act.sem_inc(tok_done, 1)
            act.wait_ge(zeroed, 2)

            def take_in(t):
                act.wait_ge(turn_done, t.n + 1)
                act.wait_ge(acc_done, t.n + 1)
                act.copy(xin[:, t.buf, 2:2 + P], turned_in[:, 0:P])
                act.copy(xin[:, t.buf, 4 + P:4 + TILES * P], turned_in[:, P:TILES * P]).then_inc(xin_done, 1)

            def body(t, more):
                if more:
                    take_in(t.next())
                act.wait_ge(acc_done, t.n + 3)
                act.activation(acc[:, t.buf], acc[:, t.buf], ACT.Silu).then_inc(smooth_done, 1)
                act.wait_ge(back_done, t.n + 3)
                act.copy(tok[:, :, bass.ds(t.n * P, P)],
                         turned_out[:, 0:TILES * P].rearrange("p (t c) -> p t c", t=TILES)).then_inc(tok_done, 1)
            slices(act, take_in, body)

        @block.vector
        def _(dve):
            dve.sem_inc(acc_done, 2)
            dve.sem_inc(row_done, 1)
            dve.wait_ge(small_in, 16 * 7)
            dve.tensor_tensor(t1[:], dt_tok[:], bcast(dt_bias[:], TILES, 1), ALU.add)
            dve.drain()
            dve.tensor_scalar(t3[:], t1[:], -1.0, None, ALU.mult)
            dve.drain()
            dve.tensor_tensor(t2[:], t1[:], t3[:], ALU.min).then_inc(pre_done, 1)
            dve.wait_ge(exp_done, 1)
            dve.tensor_scalar(t3[:], t2[:], 1.0, None, ALU.add).then_inc(pre_done, 1)
            dve.tensor_scalar(t1[:], t1[:], 0.0, None, ALU.max)
            dve.wait_ge(ln_done, 1)
            dve.tensor_scalar(la[:], t3[:], 1.0, None, ALU.is_equal)
            dve.drain()
            dve.scalar_tensor_tensor(out=t3[:], in0=t3[:], scalar=-1.0, in1=la[:], op0=ALU.add, op1=ALU.add)
            dve.tensor_tensor(t4[:], t4[:], la[:], ALU.add)
            dve.drain()
            dve.reciprocal(t3[:], t3[:])
            dve.tensor_tensor(t4[:], t4[:], t2[:], ALU.mult)
            dve.drain()
            dve.tensor_tensor(t4[:], t4[:], t3[:], ALU.mult)
            dve.drain()
            dve.tensor_tensor(dt_tok[:], t1[:], t4[:], ALU.add)
            dve.drain()
            dve.wait_ge(a_done, 1)
            dve.scalar_tensor_tensor(out=la[:], in0=dt_tok[:], scalar=-1.0, in1=bcast(a_neg[:], TILES, 1),
                                     op0=ALU.mult, op1=ALU.mult).then_inc(la_done, 1)
            dve.wait_ge(sums_done, 1)
            n = TILES * SH
            for half in range(2):
                dve.tensor_copy(cum[:, :, half * SH:(half + 1) * SH],
                                sums[:, half * n:(half + 1) * n].rearrange("p (t h) -> p t h", t=TILES))
            dve.tensor_copy(tot[:], sums[:, 2 * n:4 * n].rearrange("p (t h) -> p t h", t=TILES))
            dve.drain()
            dve.tensor_tensor(t1[:], tot[:], cum[:], ALU.subtract).then_inc(cum_done, 1)
            dve.wait_ge(expo_done, 1)
            dve.tensor_tensor(dte[:], dt_tok[:], t1[:], ALU.mult)
            dve.wait_ge(taps_turned, 1)
            dve.tensor_copy(taps[:], turned_in[:, 0:NXBC * (CONV + 1)].rearrange("p (c k) -> p c k", c=NXBC)).then_inc(taps_done, 1)
            dve.wait_ge(taps_done, 1)

            def body(t, more):
                dve.wait_ge(xin_done, t.n + 2)
                dve.wait_ge(back_done, t.n + 1)
                dve.wait_ge(kept, t.n + 1)
                out, ct = acc[:, t.buf], t.n
                dve.tensor_scalar(out, xin[:, t.buf, 0:COUT], taps[:, ct, 0:1], taps[:, ct, CONV:CONV + 1], ALU.mult, ALU.add)
                for k in range(1, CONV):
                    dve.drain()
                    op = dve.scalar_tensor_tensor(out=out, in0=xin[:, t.buf, k:k + COUT], scalar=taps[:, ct, k:k + 1],
                                                  in1=out, op0=ALU.mult, op1=ALU.add)
                op.then_inc(acc_done, 1)
                dve.wait_ge(row_mm, t.n + 1)
                dve.wait_ge(wa_in[t.buf], t.nth * 32 + 32)
                dve.tensor_tensor(rows[:, t.buf], row_ps[0:2, :], rows[:, t.buf], ALU.add).then_inc(row_done, 1)
            slices(dve, lambda t: None, body)

        @block.tensor
        def _(pe):
            ident = C["ident"]
            pe.wait_ge(small_in, 16 * 7)
            for c in range(NXBC):
                mm = pe.transpose(turned_in[:, c * (CONV + 1):(c + 1) * (CONV + 1)], taps_row[:, c * P:(c + 1) * P],
                                  ident[0:CONV + 1, 0:CONV + 1])
            mm.then_inc(taps_turned, 1)
            pe.wait_ge(la_done, 1)
            pe.wait_ge(zeroed, 1)
            n = TILES * SH
            pe.matmul(sums[:, 0:n], C["tri_le"][:], la[:, :, 0:SH], start=True, stop=True)
            pe.matmul(sums[:, n:2 * n], C["tri_ge"][:], la[:, :, SH:2 * SH], start=True, stop=True)
            pe.matmul(sums[:, 2 * n:4 * n], ones[:], la[:], start=True, stop=True).then_inc(sums_done, 1)
            pe.wait_ge(cum_done, 1)
            for t in range(TILES):
                mm = pe.transpose(turned_out[0:2 * SH, t * P:(t + 1) * P], cum[:, t, :], ident[:])
            mm.then_inc(cumT_turned, 1)
            pe.wait_ge(cumT_done, 1)
            pe.wait_ge(taps_done, 1)
            pe.sem_inc(back_done, 2)

            def turn_in(t):
                pe.wait_ge(raw_in[t.buf], t.nth * 16 + 16)
                pe.wait_ge(xin_done, t.n + 1)
                for k in range(TILES):
                    mm = pe.transpose(turned_in[:, k * P:(k + 1) * P], raw[:, t.buf, k, :], ident[:])
                mm.then_inc(turn_done, 1)

            def body(t, more):
                if more:
                    turn_in(t.next())
                pe.wait_ge(wa_in[t.buf], t.nth * 32 + 32)
                pe.wait_ge(row_done, t.n + 1)
                for k in range(KT):
                    mm = pe.matmul(row_ps[0:2, :], C["cond"][:, k, :], wa[:, t.buf, k, :], start=(k == 0), stop=(k == KT - 1))
                mm.then_inc(row_mm, 1)
                pe.wait_ge(smooth_done, t.n + 3)
                pe.wait_ge(tok_done, t.n + 1)
                for k in range(TILES):
                    col = 0 if k == 0 else 2 + k * P
                    mm = pe.transpose(turned_out[:, k * P:(k + 1) * P], acc[:, t.buf, col:col + P], ident[:])
                mm.then_inc(back_done, 1)
            slices(pe, turn_in, body)


class ScanStep:

    def __init__(self, i, c):
        self.i, self.c = i, c
        self.n = i * 4 + c
        self.d, self.buf = c % 2, c % 4
        self.pair = i * 2 + c // 2

    def next(self):
        return ScanStep(self.i, self.c + 1)

    def last(self):
        return ScanStep(self.i, self.c - 1)


def ssd_stage(nc, I, C, W, tag, pairs, tiles_of, col_of):
    STEPS = 2 * pairs
    w = W
    with ExitStack() as ctx:
        s = Scope(nc, ctx, tag)
        bc, bt = s.sb("bc", [P, 4, 4, P]), s.sb("bt", [P, 4, SG * P])
        xd, xe = s.sb("xd", [P, 4, DSSM]), s.sb("xe", [P, 4, DSSM])
        sdec = s.sb("sdec", [P, 2, DSSM])
        sc, gm = s.sb("sc", [P, 2, SH * P]), s.sb("gm", [P, 2, SG * P])
        yo = s.sb("yo", [P, DSSM])
        cum_ps = [s.ps(f"cum{d}", SH * P) for d in range(2)]
        g_ps, o_ps, y_ps, s_ps = s.ps("g"), s.ps("o"), s.ps("y"), s.ps("s")
        bc_done, x_done, sdec_done = s.sem("bc_done"), s.sem("x_done"), s.sem("sdec_done")
        cumb_done, g_done, o_done, s_done, y_done = (s.sem(k) for k in ("cumb_done", "g_done", "o_done", "s_done", "y_done"))
        seg_done, exp_done, gm_done, sc_done = (s.sem(k) for k in ("seg_done", "exp_done", "gm_done", "sc_done"))
        yo_done, state_done, yadd_done = s.sem("yo_done"), s.sem("state_done"), s.sem("yadd_done")
        block = ctx.enter_context(nc.Block())
        tok, xbcT, y_tok, dt_tok, state, pick = (w[k] for k in ("tok", "xbcT", "y_tok", "dt_tok", "state", "pick"))
        cum, ecum, dte, dec, cumT = (w[k] for k in ("cum", "ecum", "dte", "dec", "cumT"))
        mask = (C["tri_le"], C["tri_ge"])

        def heads(ap):
            return ap.rearrange("p (h d) -> p h d", h=SH)

        def place(k):
            return k.n, k.d, k.buf, tiles_of(k.pair, k.d), slice(k.d * SH, (k.d + 1) * SH)

        def steps(eng, first, body):
            first(ScanStep(0, 0))
            body(ScanStep(0, 0), False, True)
            if STEPS > 4:
                assert STEPS % 4 == 0
                with eng.Fori(0, STEPS // 4 - 1) as i:
                    for c in range(1, 5):
                        body(ScanStep(i, c), True, True)
            for n in range((STEPS - 1) // 4 * 4 + 1, STEPS):
                body(ScanStep(0, n), True, n < STEPS - 1)

        @block.gpsimd
        def _(pool):
            def body(k, before, after):
                n, d, b, t, h = place(k)
                pool.wait_ge(y_done, n + 1)
                xs = heads(tok[:, t, 0:DSSM])
                pool.tensor_tensor(heads(xd[:, b]), xs, bcast(dt_tok[:, t, h], 64, 2), ALU.mult)
                pool.tensor_tensor(heads(xe[:, b]), xs, bcast(dte[:, t, h], 64, 2), ALU.mult).then_inc(x_done, 1)
                pool.wait_ge(state_done, n + 1)
                pool.tensor_tensor(heads(sdec[:, d]), heads(state[:, d]), bcast(dec[:, t, h], 64, 2),
                                   ALU.mult).then_inc(sdec_done, 1)
            steps(pool, lambda k: None, body)

        @block.scalar
        def _(act):
            def bring(k):
                n, d, b, t, h = place(k)
                act.wait_ge(s_done, n + 1)
                act.copy(bc[:, b], xbcT[:, :, bass.ds(col_of(k.pair, d), P)])
                act.copy(bt[:, b], tok[:, t, DSSM:DSSM + SG * P]).then_inc(bc_done, 1)

            def body(k, before, after):
                if after:
                    bring(k.next())
                act.wait_ge(seg_done, k.n + 3)
                act.activation(sc[:, k.d], sc[:, k.d], ACT.Exp).then_inc(exp_done, 1)
            steps(act, bring, body)

        @block.vector
        def _(dve):
            dve.sem_inc(seg_done, 2)
            dve.sem_inc(gm_done, 1)
            dve.sem_inc(yo_done, 1)
            dve.sem_inc(state_done, 2)
            dve.sem_inc(yadd_done, 1)

            def segments(k):
                n, d, b, t, _ = place(k)
                dve.drain()
                dve.wait_ge(cumb_done, n + 1)
                dve.wait_ge(y_done, n + 3)
                for h in range(SH):
                    op = dve.tensor_scalar(sc[:, d, h * P:(h + 1) * P], cum_ps[d][:, h * P:(h + 1) * P],
                                           cum[:, t, d * SH + h:d * SH + h + 1], 0.0, ALU.subtract, ALU.min)
                op.then_inc(seg_done, 1)
                dve.wait_ge(g_done, n + 1)
                dve.tensor_tensor(gm[:, d].rearrange("p (g i) -> p g i", g=SG), g_ps[:, 0:SG * P].rearrange("p (g i) -> p g i", g=SG),
                                  bcast(mask[d][:], SG, 1), ALU.mult).then_inc(gm_done, 1)

            def carried(k):
                n, d, b, t, h = place(k)
                dve.drain()
                dve.wait_ge(o_done, n + 1)
                dve.tensor_tensor(heads(yo[:]), heads(o_ps[:]), bcast(ecum[:, t, h], 64, 2), ALU.mult).then_inc(yo_done, 1)
                dve.wait_ge(s_done, n + 5)
                dve.wait_ge(sdec_done, n + 1)
                dve.tensor_tensor(state[:, d], sdec[:, d], s_ps[:], ALU.add).then_inc(state_done, 1)
                dve.drain()
                dve.tensor_tensor(y_tok[:, t], y_tok[:, t], yo[:], ALU.add)

            def scores(k):
                dve.wait_ge(exp_done, k.n + 1)
                for g in range(SG):
                    v = sc[:, k.d, g * HG * P:(g + 1) * HG * P].rearrange("p (h i) -> p h i", h=HG)
                    op = dve.tensor_tensor(v, v, bcast(gm[:, k.d, g * P:(g + 1) * P], HG, 1), ALU.mult)
                op.then_inc(sc_done, 1)

            def diagonal(k):
                t = tiles_of(k.pair, k.d)
                dve.drain()
                dve.wait_ge(y_done, k.n + 5)
                dve.tensor_tensor(y_tok[:, t], y_tok[:, t], y_ps[:], ALU.add).then_inc(yadd_done, 1)

            def first(k):
                segments(k)
                carried(k)

            def body(k, before, after):
                scores(k)
                if before:
                    diagonal(k.last())
                if after:
                    first(k.next())
            steps(dve, first, body)
            diagonal(ScanStep(0, STEPS - 1))

        @block.tensor
        def _(pe):
            pe.sem_inc(y_done, 4)
            pe.sem_inc(s_done, 4)

            def first(k):
                n, d, b, t, _ = place(k)
                pe.wait_ge(seg_done, n + 1)
                for h in range(SH):
                    mm = pe.matmul(cum_ps[d][:, h * P:(h + 1) * P], pick[:, d * SH + h, :],
                                   cumT[:, bass.ds(t * P, P)], start=True, stop=True)
                mm.then_inc(cumb_done, 1)
                pe.wait_ge(bc_done, n + 1)
                pe.wait_ge(gm_done, n + 1)
                for g in range(SG):
                    mm = pe.matmul(g_ps[:, g * P:(g + 1) * P], bc[:, b, g, :], bc[:, b, SG + g, :], start=True, stop=True)
                mm.then_inc(g_done, 1)
                pe.wait_ge(yo_done, n + 1)
                pe.wait_ge(state_done, n + 1)
                for g in range(SG):
                    r = slice(g * HG * 64, (g + 1) * HG * 64)
                    mm = pe.matmul(o_ps[:, r], bc[:, b, SG + g, :], state[:, d, r], start=True, stop=True)
                mm.then_inc(o_done, 1)
                pe.wait_ge(x_done, n + 1)
                pe.wait_ge(state_done, n + 2)
                for g in range(SG):
                    r = slice(g * HG * 64, (g + 1) * HG * 64)
                    mm = pe.matmul(s_ps[:, r], bt[:, b, g * P:(g + 1) * P], xe[:, b, r], start=True, stop=True)
                mm.then_inc(s_done, 1)

            def body(k, before, after):
                if after:
                    first(k.next())
                pe.wait_ge(sc_done, k.n + 1)
                pe.wait_ge(yadd_done, k.n + 1)
                for h in range(SH):
                    mm = pe.matmul(y_ps[:, h * 64:(h + 1) * 64], sc[:, k.d, h * P:(h + 1) * P],
                                   xd[:, k.buf, h * 64:(h + 1) * 64], start=True, stop=True)
                mm.then_inc(y_done, 1)
            steps(pe, first, body)


def state_stage(nc, I, C, W):
    with ExitStack() as ctx:
        s = Scope(nc, ctx, "state")
        out, inn = s.sb("out", [P, 2, 4, P]), s.sb("in", [P, 2, 4, P])
        ps_out, ps_in = [s.ps(f"out{d}") for d in range(2)], [s.ps(f"in{d}") for d in range(2)]
        loaded, turned_out, turned_in = s.sem("loaded"), s.sem("turned_out"), s.sem("turned_in")
        out_done, stored = s.sem("out_done"), s.sem("stored")
        block = ctx.enter_context(nc.Block())
        state = W["state"]

        @block.sync
        def _(sp):
            for d, name in enumerate(("state_ssm_fwd", "state_ssm_bwd")):
                sp.dma_start(inn[:, d], I[name][0, 0].rearrange("(q a) p n -> (a p) q n", a=2)).then_inc(loaded, 16)
            for d, name in enumerate(("new_hf", "new_hb")):
                sp.wait_ge(out_done, d + 1)
                sp.dma_start(I[name][0, 0].rearrange("(q a) p n -> (a p) q n", a=2), out[:, d]).then_inc(stored, 16)
            sp.wait_ge(stored, 32)

        @block.tensor
        def _(pe):
            for d in range(2):
                for q in range(4):
                    mm = pe.transpose(ps_out[d][:, q * P:(q + 1) * P], state[:, d, q * P:(q + 1) * P], C["ident"][:])
                mm.then_inc(turned_out, 1)
            pe.wait_ge(loaded, 32)
            for d in range(2):
                for q in range(4):
                    mm = pe.transpose(ps_in[d][:, q * P:(q + 1) * P], inn[:, d, q, :], C["ident"][:])
                mm.then_inc(turned_in, 1)

        @block.vector
        def _(dve):
            for d in range(2):
                dve.wait_ge(turned_out, d + 1)
                dve.tensor_copy(out[:, d].rearrange("p q n -> p (q n)"), ps_out[d][:]).then_inc(out_done, 1)
            for d in range(2):
                dve.wait_ge(turned_in, d + 1)
                dve.tensor_copy(state[:, d], ps_in[d][:])


def scan_stages(nc, I, C, W, M):
    with ExitStack() as ctx:
        s = Scope(nc, ctx, "scan")
        W["tok"], W["xbcT"] = s.sb("tok", [P, TILES, XBC]), s.sb("xbcT", [P, 4, COUT])
        for k in ("cum", "tot", "ecum", "dte", "dec"):
            W[k] = s.sb(k, [P, TILES, 2 * SH])
        W["cumT"] = s.sb("cumT", [2 * SH, TILES * P])
        conv_stage(nc, I, C, W, M)
        W["pick"], W["state"] = s.sb("pick", [2 * SH, 2 * SH, P]), s.sb("st", [P, 2, DSSM])
        with ExitStack() as load_ctx:
            pick_in = Scope(nc, load_ctx, "pick").sem("in")
            block = load_ctx.enter_context(nc.Block())

            @block.sync
            def _(sp):
                sp.dma_start(W["pick"][:], I["pick"]).then_inc(pick_in, 16)
                sp.wait_ge(pick_in, 16)

            @block.vector
            def _(dve):
                dve.memset(W["state"][:], 0.0)
        ssd_stage(nc, I, C, W, "ssdp", 1, lambda i, d: 0, lambda i, d: 0)
        state_stage(nc, I, C, W)
        ssd_stage(nc, I, C, W, "ssds", STILES, lambda i, d: i + 1 if d == 0 else i * -1 + STILES,
                  lambda i, d: i * P + (2 + P) if d == 0 else i * -P + (2 + STILES * P))


class Item:

    def __init__(self, t, h):
        self.step, self.t, self.h, self.buf = t, t.n, h, h % 2
        self.n = t.n * HEADS + h
        self.prompt = isinstance(t.n, int) and t.n == 0

    def next(self, last_tile):
        if self.h < HEADS - 1:
            return Item(self.step, self.h + 1)
        return None if last_tile else Item(self.step.next(), 0)


def attention_stage(nc, I, C, W, M):
    with ExitStack() as ctx:
        s = Scope(nc, ctx, "att")
        lam_rows, lam_prod = s.sb("lam_rows", [P, 4, QKD]), s.sb("lam_prod", [P, 2, QKD])
        lam_sum, lam_neg = s.sb("lam_sum", [P, 2]), s.sb("lam_neg", [P, 1])
        q_now = s.sb("q_now", [P, 2, HEADS, P])
        e = s.sb("e", [P, 2, 2, TILES * P])
        aT = s.sb("aT", [P, TILES * P])
        top, top2, shift = s.sb("top", [P, 2, 2]), s.sb("top2", [P, 2]), s.sb("shift", [P, 2, 2])
        total, inv, ratio = s.sb("total", [P, 2, 2]), s.sb("inv", [P, 2, 2]), s.sb("ratio", [P, 2, 1])
        sc = s.ps("sc", 5 * 512)
        turned = [s.ps(f"turned{b}") for b in range(2)]
        o_ps = s.ps("o")
        lam_in, lam_prod_done, lam_exp_done = s.sem("lam_in"), s.sem("lam_prod_done"), s.sem("lam_exp_done")
        q_staged, e_tail = s.sem("q_staged"), s.sem("e_tail")
        sc_done, shift_done, e_main = ([s.sem(f"{k}{m}") for m in range(2)] for k in ("sc_done", "shift_done", "e_main"))
        tail_done, a_done, o_done, o_read = s.sem("tail_done"), s.sem("a_done"), s.sem("o_done"), s.sem("o_read")
        t_done = [s.sem(f"t_done{g}") for g in range(3)]
        t_read = [s.sem(f"t_read{g}") for g in range(3)]
        block = ctx.enter_context(nc.Block())
        kT, qT, v_tok, o_tok = W["kT"], W["qT"], W["v_tok"], W["o_tok"]
        ident = C["ident"]

        def tail(m):
            return sc[:, 4 * 512 + m * P:4 * 512 + (m + 1) * P]

        def score_parts(it, m):
            if it.prompt:
                return [(sc[:, 2 * m * 512:2 * m * 512 + P], e[:, it.buf, m, 0:P], 0, P)]
            return [(sc[:, 2 * m * 512:(2 * m + 2) * 512], e[:, it.buf, m, 0:1024], P, P + 1024),
                    (tail(m), e[:, it.buf, m, 1024:1152], P + 1024, P + 1152)]

        def groups(it):
            return [range(0, 1)] if it.prompt else [range(0, 4), range(4, 8), range(8, 9)]

        def full_n(it):
            return it.n - HEADS

        def tiles(eng, first, body):
            first(Item(Step(0, 0), 0))
            body(Step(0, 0), False)
            with eng.Fori(0, STILES // 2 - 1) as i:
                body(Step(i, 1), False)
                body(Step(i, 2), False)
            body(Step(0, STILES - 1), False)
            body(Step(0, STILES), True)

        @block.sync
        def _(sp):
            for k, name in enumerate(("lambda_q1", "lambda_k1", "lambda_q2", "lambda_k2")):
                sp.dma_start(lam_rows[:, k], row_bcast(I[name][0])).then_inc(lam_in, 16)
            load_mixer(sp, I, W, M)

        @block.gpsimd
        def _(pool):
            def copy(t, buf):
                pool.wait_ge(sc_done[1], t * HEADS + HEADS)
                pool.tensor_copy(q_now[:, buf], qT[:, :, bass.ds(t * P, P)]).then_inc(q_staged, 1)
            copy(0, 0)
            copy(1, 1)
            pool.sem_inc(W["w_out_split"], 1)
            pool.wait_ge(W["gains_in"], 16 * 7)
            split_w_out(pool, W, range(0, 1))
            for t in (2, 3, 4):
                copy(t, t % 2)
                split_w_out(pool, W, range(3 * t - 5, min(3 * t - 2, KT)))
            with pool.Fori(2, STILES // 2) as i:
                copy(i * 2 + 1, 1)
                copy(i * 2 + 2, 0)

        @block.scalar
        def _(act):
            act.sem_inc(t_read[2], 1)
            act.wait_ge(lam_prod_done, 1)
            act.activation(lam_sum[:], lam_sum[:], ACT.Exp).then_inc(lam_exp_done, 1)

            def exponentials(it, m):
                if m == 0:
                    act.wait_ge(o_done, it.n + 1)
                act.wait_ge(shift_done[m], it.n + 1)
                bias = shift[:, it.buf, m:m + 1]
                for p, (scores, exps, _, _) in enumerate(score_parts(it, m)):
                    sums, done = (total, e_main[m]) if p == 0 else (inv, e_tail)
                    act.activation(exps, scores, ACT.Exp, bias=bias, scale=SCALE,
                                   accum_out=sums[:, it.buf, m:m + 1]).then_inc(done, 1)

            def evacuate(it, gs):
                for g, ks in enumerate(groups(it)):
                    if g in gs:
                        act.wait_ge(t_done[g], (it.n if g == 0 else full_n(it)) + 1)
                        act.copy(aT[:, ks[0] * P:(ks[-1] + 1) * P], turned[g % 2][:, 0:len(ks) * P]).then_inc(t_read[g], 1)

            def first(it):
                exponentials(it, 0)
                exponentials(it, 1)

            def body(t, last):
                for h in range(HEADS):
                    it = Item(t, h)
                    nxt = it.next(last)
                    act.wait_ge(o_done, it.n + 2)
                    evacuate(it, (0, 1))
                    if nxt:
                        exponentials(nxt, 0)
                    evacuate(it, (2,))
                    if nxt:
                        exponentials(nxt, 1)
            tiles(act, first, body)

        @block.vector
        def _(dve):
            dve.sem_inc(o_read, 1)
            dve.wait_ge(lam_in, 64)
            for k in range(2):
                dve.tensor_tensor(lam_prod[:, k], lam_rows[:, 2 * k], lam_rows[:, 2 * k + 1], ALU.mult)
            dve.drain()
            dve.tensor_reduce(lam_sum[:], lam_prod[:], AX, ALU.add).then_inc(lam_prod_done, 1)
            dve.wait_ge(lam_exp_done, 1)
            dve.tensor_tensor(lam_neg[:], lam_sum[:, 1:2], lam_sum[:, 0:1], ALU.subtract)
            dve.drain()
            dve.tensor_scalar(lam_neg[:], lam_neg[:], -LAM0, None, ALU.add)

            def maxima(it, m):
                dve.drain()
                dve.wait_ge(sc_done[m], it.n + (1 if m == 0 else 2 * HEADS + 1))
                top_m, other = top[:, it.buf, m:m + 1], top2[:, m:m + 1]
                dve.tensor_reduce(top_m, score_parts(it, m)[0][0], AX, ALU.max)
                if it.prompt:
                    other = top_m
                elif m == 0:
                    dve.tensor_reduce(top2[:], sc[:, 4 * 512:4 * 512 + 2 * P].rearrange("p (m k) -> p m k", m=2), AX, ALU.max)
                dve.drain()
                dve.tensor_scalar(shift[:, it.buf, m:m + 1], top_m, other, -SCALE, ALU.max, ALU.mult).then_inc(shift_done[m], 1)

            def combine(it):
                dve.drain()
                for m in range(2):
                    dve.wait_ge(e_main[m], it.n + 2)
                if not it.prompt:
                    dve.wait_ge(e_tail, full_n(it) * 2 + 4)
                tot = total[:, it.buf]
                if not it.prompt:
                    dve.tensor_tensor(tot, tot, inv[:, it.buf], ALU.add)
                    dve.drain()
                dve.reciprocal(inv[:, it.buf], tot)
                dve.drain()
                dve.tensor_scalar(ratio[:, it.buf], inv[:, it.buf, 1:2], tot[:, 0:1], lam_neg[:, 0:1], ALU.mult, ALU.mult)
                dve.drain()
                w = P if it.prompt else TILES * P
                dve.scalar_tensor_tensor(out=e[:, it.buf, 0, 0:w], in0=e[:, it.buf, 1, 0:w], scalar=ratio[:, it.buf, 0:1],
                                         in1=e[:, it.buf, 0, 0:w], op0=ALU.mult, op1=ALU.add).then_inc(a_done, 1)

            def finish(it):
                dve.wait_ge(o_done, it.n + 3)
                dve.tensor_scalar(o_tok[:, it.t, it.h * P:(it.h + 1) * P], o_ps[:, 0:P], inv[:, it.buf, 0:1], None,
                                  ALU.mult).then_inc(o_read, 1)

            def first(it):
                maxima(it, 0)
                maxima(it, 1)
                combine(it)

            def body(t, last):
                for h in range(HEADS):
                    it = Item(t, h)
                    nxt = it.next(last)
                    if nxt:
                        maxima(nxt, 0)
                        maxima(nxt, 1)
                    finish(it)
                    if nxt:
                        combine(nxt)
            tiles(dve, first, body)

        @block.tensor
        def _(pe):
            pe.sem_inc(sc_done[1], 2 * HEADS)
            pe.sem_inc(o_done, 2)
            for done, credit in ((e_main[0], 1), (e_main[1], 1), (e_tail, 2)):
                pe.sem_inc(done, credit)

            def score(it, m, dst, lo, hi):
                rows = slice(m * QKD, (m + 1) * QKD)
                return pe.matmul(dst, q_now[rows, it.step.buf, it.h, :], kT[rows, it.h, lo:hi], start=True, stop=True)

            def score_half(it, m, half):
                lo = P + half * 512
                return score(it, m, sc[:, (2 * m + half) * 512:(2 * m + half + 1) * 512], lo, lo + 512)

            def scores_first(it):
                pe.wait_ge(q_staged, it.t + 1)
                pe.wait_ge(e_main[0], it.n + 1)
                if it.prompt:
                    score(it, 0, sc[:, 0:P], 0, P).then_inc(sc_done[0], 1)
                    return
                score_half(it, 0, 0)
                pe.wait_ge(e_tail, full_n(it) * 2 + 2)
                score(it, 0, tail(0), P + 1024, P + 1152).then_inc(tail_done, 1)
                score_half(it, 0, 1)
                pe.wait_ge(tail_done, full_n(it) + 1)
                score(it, 1, tail(1), P + 1024, P + 1152).then_inc(sc_done[0], 1)

            def scores_second(it, half):
                if half == 0:
                    pe.wait_ge(e_main[1], it.n + 1)
                    if it.prompt:
                        score(it, 1, sc[:, 2 * 512:2 * 512 + P], 0, P).then_inc(sc_done[1], 1)
                    else:
                        score_half(it, 1, 0)
                elif not it.prompt:
                    score_half(it, 1, 1).then_inc(sc_done[1], 1)

            def turn(it, g):
                ks = groups(it)[g]
                bank = turned[g % 2]
                for j, k in enumerate(ks):
                    mm = pe.transpose(bank[:, j * P:(j + 1) * P], e[:, it.buf, 0, k * P:(k + 1) * P], ident[:])
                mm.then_inc(t_done[g], 1)

            def values(it, g):
                ks = groups(it)[g]
                n = it.n if g == 0 else full_n(it)
                pe.wait_ge(t_read[g], n + (2 if g == 2 else 1))
                last = groups(it)[-1][-1]
                for k in ks:
                    mm = pe.matmul(o_ps[:, 0:P], aT[:, k * P:(k + 1) * P],
                                   v_tok[:, k + (0 if it.prompt else 1), it.h * P:(it.h + 1) * P],
                                   start=(k == 0), stop=(k == last))
                return mm

            def first(it):
                scores_first(it)
                scores_second(it, 0)

            def item(it, nxt):
                if nxt:
                    scores_first(nxt)
                    scores_second(nxt, 0)
                pe.wait_ge(a_done, it.n + 1)
                if not it.prompt:
                    pe.wait_ge(t_read[2], full_n(it) + 1)
                turn(it, 0)
                if not it.prompt:
                    turn(it, 1)
                if nxt:
                    scores_second(nxt, 1)
                pe.wait_ge(o_read, it.n + 1)
                if it.prompt:
                    values(it, 0).then_inc(o_done, 1)
                    return
                values(it, 0)
                turn(it, 2)
                values(it, 1)
                values(it, 2).then_inc(o_done, 1)

            def body(t, last):
                for h in range(HEADS):
                    it = Item(t, h)
                    item(it, it.next(last))
            tiles(pe, first, body)


def refine(dve, r, ssq, scale, tmp):
    dve.drain()
    dve.tensor_scalar(tmp, ssq, scale, EPS, ALU.mult, ALU.add)
    dve.drain()
    dve.scalar_tensor_tensor(out=tmp, in0=tmp, scalar=-0.5, in1=r, op0=ALU.mult, op1=ALU.mult)
    dve.drain()
    dve.tensor_tensor(tmp, tmp, r, ALU.mult)
    dve.drain()
    dve.scalar_tensor_tensor(out=r, in0=tmp, scalar=1.5, in1=r, op0=ALU.add, op1=ALU.mult)
    dve.drain()


def load_mixer(sp, I, W, M):
    for k in range(HEADS):
        sp.dma_start(W["gcol"][:, k:k + 1], I["attn_subln_g"][0].unsqueeze(1)).then_inc(W["gains_in"], 16)
    sp.dma_start(W["gcol"][:, HEADS:KT], I["ssm_norm_g"][0].rearrange("(k p) -> p k", p=P),
                 allow_slow_non_contiguous=True).then_inc(W["gains_in"], 16)
    for cond in range(2):
        sp.dma_start(W["gate"][:, cond], row_bcast(M["mods"][cond, GATE1 * D:(GATE1 + 1) * D])).then_inc(W["gains_in"], 16)
    for k in range(KT):
        sp.wait_ge(W["w_out_split"], k + 1)
        sp.dma_start(W["w_out_raw"][:], I["w_out"][0, k * P:(k + 1) * P, :]).then_inc(W["w_out_in"], 16)


def split_w_out(pool, W, slices):
    for k in slices:
        pool.wait_ge(W["w_out_in"], 16 * k + 16)
        pool.tensor_scalar(W["w_out_raw"][:], W["w_out_raw"][:], W["gcol"][:, k:k + 1], 1.0 - LAM0 if k < HEADS else 1.0,
                           ALU.mult, ALU.mult)
        pool.drain()
        pool.tensor_copy(W["w_out_hi"][:, k], W["w_out_raw"][:])
        pool.drain()
        split_low(pool, W["w_out_lo"][:, k], W["w_out_raw"][:], W["w_out_hi"][:, k]).then_inc(W["w_out_split"], 1)


def mixer_stage(nc, I, C, W, M):
    with ExitStack() as ctx:
        s = Scope(nc, ctx, "mix")
        w_hi, w_lo, gate = (W[k] for k in ("w_out_hi", "w_out_lo", "gate"))
        amul, aadd = s.sb("amul", [P, 2, D]), s.sb("aadd", [P, 2, D])
        wr, br = s.sb("wr", [P, KT, NG + NE]), s.sb("br", [P, NG + NE])
        z, x = s.sb("z", [P, 2, DSSM]), s.sb("x", [P, 2, D])
        mix = s.sb("mix", [P, 2, D])
        mixT_hi, mixT_lo = (s.sb(k, [P, KT * P], F32R) for k in ("mixT_hi", "mixT_lo"))
        h2, h2T = s.sb("h2", [P, 2, D]), s.sb("h2T", [P, KT * P])
        junk = s.sb("junk", [P, DSSM])
        ssq, rstd, tmp = s.sb("ssq", [P, 2, 5]), s.sb("rstd", [P, 2, 5]), s.sb("tmp", [P, 5])
        ssq2, rstd2, tmp2 = s.sb("ssq2", [P, 2]), s.sb("rstd2", [P, 2]), s.sb("tmp2", [P, 1])
        epsc = s.sb("epsc", [P, 1])
        t1_ps, acc, t2_ps = s.ps("t1", D), s.ps("acc", D), s.ps("t2", D)
        lg_ps = s.ps("lg")
        gain = h2[:, 0]
        mods_in = s.sem("mods_in")
        g_in, eps_done = s.sem("g_in"), s.sem("eps_done")
        mixT_high = s.sem("mixT_high")
        z_in, x_in = [s.sem(f"z_in{u}") for u in range(2)], [s.sem(f"x_in{u}") for u in range(2)]
        silu_done, gated, sq_done, mix_done = s.sem("silu_done"), s.sem("gated"), s.sem("sq_done"), s.sem("mix_done")
        t1_done, mixT_done, acc_done, acc_read = s.sem("t1_done"), s.sem("mixT_done"), s.sem("acc_done"), s.sem("acc_read")
        x2_done, sq2_done, h2_scaled, h2_done = s.sem("x2_done"), s.sem("sq2_done"), s.sem("h2_scaled"), s.sem("h2_done")
        t2_done, h2T_done, lg_done, lg_read = s.sem("t2_done"), s.sem("h2T_done"), s.sem("lg_done"), s.sem("lg_read")
        h2_stored = [s.sem(f"h2_stored{u}") for u in range(2)]
        block = ctx.enter_context(nc.Block())
        y_tok, o_tok, x2, logits = W["y_tok"], W["o_tok"], W["x2"], W["logits"]

        def tiles(eng, first, body):
            first(Step(0, 0))
            body(Step(0, 0), True)
            with eng.Fori(0, STILES // 2 - 1) as i:
                body(Step(i, 1), True)
                body(Step(i, 2), True)
            body(Step(0, TILES - 2), True)
            body(Step(0, TILES - 1), False)

        def is_first(t):
            return isinstance(t.n, int) and t.n == 0

        @block.sync
        def _(sp):
            sp.dma_start(wr[:, :, 0:NG], I["w_group_router"][0].rearrange("(k p) n -> p k n", p=P)).then_inc(g_in, 16)
            sp.dma_start(wr[:, :, NG:], I["w_expert_router"][0].rearrange("(k p) n -> p k n", p=P)).then_inc(g_in, 16)
            sp.dma_start(br[:, 0:NG], row_bcast(I["b_group_router"][0])).then_inc(g_in, 16)
            sp.dma_start(br[:, NG:], row_bcast(I["b_expert_router"][0])).then_inc(g_in, 16)

            sp.dma_start(gain, row_bcast(I["norm_ffn_g"][0])).then_inc(mods_in, 16)

            def load(t):
                xrows = I["x_prompt"][0] if is_first(t) else I["x_sample"][0, bass.ds((t.n - 1) * P, P), :]
                sp.wait_ge(gated, t.n + 1)
                sp.dma_start(z[:, t.buf], M["z"][bass.ds(t.n * P, P), :]).then_inc(z_in[t.buf], 16)
                sp.wait_ge(x2_done, t.n + 1)
                sp.dma_start(x[:, t.buf], xrows).then_inc(x_in[t.buf], 16)

            def first(t):
                load(t)
                load(t.next())
                for cond in range(2):
                    for dst, sec in ((amul, SCALE2), (aadd, SHIFT2)):
                        sp.dma_start(dst[:, cond], row_bcast(M["mods"][cond, sec * D:(sec + 1) * D])).then_inc(mods_in, 16)

            def body(t, more):
                if not isinstance(t.n, int) or t.n + 2 < TILES:
                    load(t.next().next())
                sp.wait_ge(h2_done, t.n + 3)
                sp.dma_start(M["h2"][bass.ds(t.n * P, P), :], h2[:, t.buf]).then_inc(h2_stored[t.buf], 16)
            tiles(sp, first, body)
            sp.wait_ge(h2_stored[0], 16 * 6)
            sp.wait_ge(h2_stored[1], 16 * 5)

        @block.gpsimd
        def _(pool):
            pool.sem_inc(x2_done, 2)
            pool.sem_inc(h2_done, 2)

            def body(t, more):
                pool.wait_ge(x_in[t.buf], t.nth * 16 + 16)
                pool.wait_ge(acc_read, t.n + 2)
                pool.tensor_tensor(x2[:, t.n], x2[:, t.n], x[:, t.buf], ALU.add).then_inc(x2_done, 1)
                pool.wait_ge(h2_scaled, t.n + 1)
                pool.tensor_tensor(h2[:, t.buf], h2[:, t.buf], aadd[:, 0 if is_first(t) else 1], ALU.add).then_inc(h2_done, 1)
            tiles(pool, lambda t: None, body)

        @block.scalar
        def _(act):
            act.sem_inc(h2T_done, 1)
            act.wait_ge(eps_done, 1)

            def prepare(t):
                act.wait_ge(z_in[t.buf], t.nth * 16 + 16)
                act.activation(z[:, t.buf], z[:, t.buf], ACT.Silu).then_inc(silu_done, 1)
                for h in range(HEADS):
                    act.activation(junk[:, h * P:(h + 1) * P], o_tok[:, t.n, h * P:(h + 1) * P], ACT.Square,
                                   accum_out=ssq[:, t.buf, h:h + 1])
                act.drain()
                act.activation(rstd[:, t.buf, 0:HEADS], ssq[:, t.buf, 0:HEADS], ACT.Sqrt, bias=epsc[:, 0:1], scale=1.0 / P)
                act.wait_ge(gated, t.n + 3)
                act.activation(junk[:], mix[:, t.buf, DATT:], ACT.Square, accum_out=ssq[:, t.buf, HEADS:HEADS + 1])
                act.drain()
                act.activation(rstd[:, t.buf, HEADS:HEADS + 1], ssq[:, t.buf, HEADS:HEADS + 1], ACT.Sqrt, bias=epsc[:, 0:1],
                               scale=1.0 / DSSM).then_inc(sq_done, 1)

            def mix_high(t):
                act.wait_ge(acc_done, t.n + 2)
                act.wait_ge(t1_done, t.n + 3)
                act.copy(mixT_hi[:], t1_ps[:]).then_inc(mixT_high, 1)

            def first(t):
                prepare(t)
                mix_high(t)

            def evacuate(t):
                act.wait_ge(lg_done, t.n + 1)
                act.wait_ge(t2_done, t.n + 3)
                act.copy(h2T[:], t2_ps[:]).then_inc(h2T_done, 1)

            def body(t, more):
                if more:
                    prepare(t.next())
                if not is_first(t):
                    evacuate(Step(t.i, t.c - 1))
                if more:
                    mix_high(t.next())
                act.wait_ge(x2_done, t.n + 3)
                act.wait_ge(t2_done, t.n + 1)
                act.wait_ge(h2_stored[t.buf], t.nth * 16 + 16)
                act.activation(h2[:, t.buf], x2[:, t.n], ACT.Square, accum_out=ssq2[:, t.buf:t.buf + 1])
                act.drain()
                act.activation(rstd2[:, t.buf:t.buf + 1], ssq2[:, t.buf:t.buf + 1], ACT.Sqrt, bias=epsc[:, 0:1],
                               scale=1.0 / D).then_inc(sq2_done, 1)
            tiles(act, first, body)
            evacuate(Step(0, TILES - 1))

        @block.vector
        def _(dve):
            dve.memset(epsc[:], EPS).then_inc(eps_done, 1)
            dve.sem_inc(gated, 2)
            dve.sem_inc(mixT_done, 1)
            dve.sem_inc(acc_read, 1)
            dve.sem_inc(lg_read, 1)
            for u in range(2):
                dve.sem_inc(h2_stored[u], 16)
            dve.wait_ge(g_in, 16 * 4)
            dve.wait_ge(W["gains_in"], 16 * 7)

            def prepare(t):
                dve.drain()
                dve.wait_ge(silu_done, t.n + 1)
                dve.wait_ge(t1_done, t.n + 1)
                dve.tensor_tensor(mix[:, t.buf, DATT:], z[:, t.buf], y_tok[:, t.n], ALU.mult).then_inc(gated, 1)
                dve.wait_ge(sq_done, t.n + 1)
                r = rstd[:, t.buf]
                dve.reciprocal(r, r)
                refine(dve, r[:, 0:HEADS], ssq[:, t.buf, 0:HEADS], 1.0 / P, tmp[:, 0:HEADS])
                refine(dve, r[:, HEADS:], ssq[:, t.buf, HEADS:], 1.0 / DSSM, tmp[:, HEADS:])
                dve.tensor_tensor(mix[:, t.buf, 0:DATT].rearrange("p (h d) -> p h d", h=HEADS),
                                  o_tok[:, t.n].rearrange("p (h d) -> p h d", h=HEADS), bcast(r[:, 0:HEADS], P, 2), ALU.mult)
                dve.tensor_scalar(mix[:, t.buf, DATT:], mix[:, t.buf, DATT:], r[:, HEADS:], None, ALU.mult).then_inc(mix_done, 1)

            def mix_low(t):
                dve.wait_ge(mixT_high, t.n + 1)
                split_low(dve, mixT_lo[:], t1_ps[:], mixT_hi[:]).then_inc(mixT_done, 1)

            def router(t):
                dve.wait_ge(lg_done, t.n + 2)
                dve.tensor_tensor(logits[:, t.n], lg_ps[:, 0:NG + NE], br[:], ALU.add).then_inc(lg_read, 1)

            def first(t):
                prepare(t)
                mix_low(t)
                dve.wait_ge(mods_in, 16 * 5)
                for cond in range(2):
                    dve.scalar_tensor_tensor(out=amul[:, cond], in0=amul[:, cond], scalar=1.0, in1=gain, op0=ALU.add, op1=ALU.mult)

            def body(t, more):
                cond = 0 if is_first(t) else 1
                if more:
                    prepare(t.next())
                dve.wait_ge(acc_done, t.n + 3)
                dve.tensor_tensor(x2[:, t.n], acc[:], gate[:, cond], ALU.mult).then_inc(acc_read, 1)
                if more:
                    mix_low(t.next())
                dve.wait_ge(sq2_done, t.n + 1)
                r = rstd2[:, t.buf:t.buf + 1]
                dve.reciprocal(r, r)
                refine(dve, r, ssq2[:, t.buf:t.buf + 1], 1.0 / D, tmp2[:])
                dve.wait_ge(t2_done, t.n + 1)
                dve.wait_ge(h2_stored[t.buf], t.nth * 16 + 16)
                dve.scalar_tensor_tensor(out=h2[:, t.buf], in0=x2[:, t.n], scalar=r, in1=amul[:, cond], op0=ALU.mult,
                                         op1=ALU.mult).then_inc(h2_scaled, 1)
                if not is_first(t):
                    router(Step(t.i, t.c - 1))

            tiles(dve, first, body)
            router(Step(0, TILES - 1))

        @block.tensor
        def _(pe):
            ident = C["ident"]
            pe.sem_inc(t1_done, 2)
            pe.sem_inc(acc_done, 2)
            pe.sem_inc(lg_done, 1)
            pe.sem_inc(t2_done, 2)
            pe.wait_ge(W["w_out_split"], KT + 1)

            def turn_mix(t):
                pe.wait_ge(mix_done, t.n + 1)
                pe.wait_ge(mixT_done, t.n + 1)
                for k in range(KT):
                    mm = pe.transpose(t1_ps[:, k * P:(k + 1) * P], mix[:, t.buf, k * P:(k + 1) * P], ident[:])
                mm.then_inc(t1_done, 1)

            def turn_h2(t):
                pe.wait_ge(h2_done, t.n + 3)
                pe.wait_ge(h2T_done, t.n + 1)
                for k in range(KT):
                    mm = pe.transpose(t2_ps[:, k * P:(k + 1) * P], h2[:, t.buf, k * P:(k + 1) * P], ident[:])
                mm.then_inc(t2_done, 1)

            def route(t):
                pe.wait_ge(h2T_done, t.n + 2)
                pe.wait_ge(lg_read, t.n + 1)
                for k in range(KT):
                    mm = pe.matmul(lg_ps[:, 0:NG + NE], h2T[:, k * P:(k + 1) * P], wr[:, k], start=(k == 0), stop=(k == KT - 1))
                mm.then_inc(lg_done, 1)

            def body(t, more):
                pe.wait_ge(mixT_done, t.n + 2)
                pe.wait_ge(acc_read, t.n + 1)
                for half in range(2):
                    for k in range(KT):
                        rows, cols = slice(k * P, (k + 1) * P), slice(half * 512, (half + 1) * 512)
                        mm = split_product(pe, acc[:, cols], mixT_hi[:, rows], mixT_lo[:, rows], w_hi[:, k, cols],
                                           w_lo[:, k, cols], k == 0, k == KT - 1)
                    if half == 0 and not is_first(t):
                        turn_h2(Step(t.i, t.c - 1))
                mm.then_inc(acc_done, 1)
                if more:
                    turn_mix(t.next())
                if not is_first(t):
                    route(Step(t.i, t.c - 1))
            tiles(pe, turn_mix, body)
            turn_h2(Step(0, TILES - 1))
            route(Step(0, TILES - 1))


def routing_stage(nc, I, C, W, M):
    with ExitStack() as ctx:
        s = Scope(nc, ctx, "route")
        T = TILES
        steps, tokens = s.sb("steps", [P, BLOCKS]), s.sb("tokens", [P, T])
        ones, zeros = s.sb("ones", [P, P]), s.sb("zeros", [P, 2 * BLOCKS])
        gmax, gdiff, gsum, pg = s.sb("gmax", [P, T]), s.sb("gdiff", [P, T, NG]), s.sb("gsum", [P, T]), s.sb("pg", [P, T])
        ohg, oh = s.sb("ohg", [P, T, NG]), s.sb("oh", [P, 2, T, EPG])
        seen, left = s.sb("seen", [P, T]), s.sb("left", [P, T])
        prod, esel, esel2 = s.sb("prod", [P, T, NG, EPG]), s.sb("esel", [P, T, EPG]), s.sb("esel2", [P, T, EPG])
        top = s.sb("top", [P, 2, T])
        ediff, wsum = s.sb("ediff", [P, T]), s.sb("wsum", [P, T])
        pick = s.sb("pick", [P, 2, T, NE])
        both, place, weighed = s.sb("both", [P, T, NE]), s.sb("place", [P, T, NE]), s.sb("weighed", [P, T, NE])
        before, count = s.sb("before", [P, T, NE]), s.sb("count", [P, NE])
        more, nblk, bend, bones = s.sb("more", [P, NE, T]), s.sb("nblk", [P, NE]), s.sb("bend", [P, NE]), s.sb("bones", [P, NE])
        fresh, sign, buffer = (s.sb(k, [P, BLOCKS]) for k in ("fresh", "sign", "buffer"))
        past, of_block = s.sb("past", [P, BLOCKS, NE]), s.sb("of_block", [P, BLOCKS])
        slot_f = s.sb("slot_f", [P, T])
        slot_u = [[s.sb(f"slot{c}_{t}", [P, 1], U32) for t in range(T)] for c in range(2)]
        value = s.sb("value", [P, 2, T, 2])
        table = s.sb("table", [P, BLOCKS, 2])
        rank_ps, sum_ps = s.ps("rank"), s.ps("sum")
        c_in, z_done, z_stored = s.sem("c_in"), s.sem("z_done"), s.sem("z_stored")
        g_done, gexp_done, e_done, eexp_done = s.sem("g_done"), s.sem("gexp_done"), s.sem("e_done"), s.sem("eexp_done")
        both_done, ranked, slots_done, scattered, table_in = (s.sem(k) for k in
                                                              ("both_done", "ranked", "slots_done", "scattered", "table_in"))
        block = ctx.enter_context(nc.Block())
        logits = W["logits"]
        lg = logits[:, :, 0:NG]
        le = logits[:, :, NG:].rearrange("p t (g e) -> p t g e", g=NG)

        @block.sync
        def _(sp):
            sp.dma_start(steps[:], row_bcast(I["steps"])).then_inc(c_in, 16)
            sp.dma_start(tokens[:], I["tokens"]).then_inc(c_in, 16)
            sp.wait_ge(z_done, 1)
            sp.dma_start(M["slots"].rearrange("(p b) c -> p (b c)", p=P), zeros[:]).then_inc(z_stored, 16)
            sp.wait_ge(scattered, 16 * 2 * T)
            sp.dma_start(table[:], M["slots"].rearrange("(b p) c -> p b c", p=P)).then_inc(table_in, 16)

        @block.gpsimd
        def _(pool):
            pool.memset(zeros[:], 0.0).then_inc(z_done, 1)
            pool.wait_ge(z_stored, 16)
            pool.wait_ge(slots_done, 1)
            for c in range(2):
                for t in range(T):
                    pool.indirect_dma_start(M["slots"], bass.IndirectOffsetOnAxis(ap=slot_u[c][t][:], axis=0),
                                            value[:, c, t, :], None).then_inc(scattered, 16)
            pool.wait_ge(scattered, 16 * 2 * T)

        @block.scalar
        def _(act):
            act.wait_ge(g_done, 1)
            act.activation(gdiff[:], gdiff[:], ACT.Exp).then_inc(gexp_done, 1)
            act.wait_ge(e_done, 1)
            act.activation(ediff[:], ediff[:], ACT.Exp).then_inc(eexp_done, 1)

        @block.tensor
        def _(pe):
            pe.wait_ge(both_done, 1)
            v = both[:].rearrange("p t e -> p (t e)")
            pe.matmul(rank_ps[:, 0:T * NE], C["tri_lt"][:], v, start=True, stop=True)
            pe.matmul(sum_ps[:, 0:T * NE], ones[:], v, start=True, stop=True).then_inc(ranked, 1)

        @block.vector
        def _(dve):
            def tt(out, a, b, op):
                dve.tensor_tensor(out, a, b, op)
                dve.drain()

            def keep_first(v, n):
                dve.tensor_copy(seen[:], v[:, :, 0])
                dve.drain()
                for j in range(1, n):
                    dve.tensor_scalar(left[:], seen[:], -1.0, 1.0, ALU.mult, ALU.add)
                    dve.drain()
                    tt(v[:, :, j], v[:, :, j], left[:], ALU.mult)
                    tt(seen[:], seen[:], v[:, :, j], ALU.max)

            dve.memset(ones[:], 1.0)
            dve.memset(bones[:], 1.0)
            dve.tensor_reduce(gmax[:], lg, AX, ALU.max)
            dve.drain()
            dve.tensor_tensor(gdiff[:], lg, bcast(gmax[:], NG, 2), ALU.subtract).then_inc(g_done, 1)
            tt(ohg[:], lg, bcast(gmax[:], NG, 2), ALU.is_equal)
            keep_first(ohg[:], NG)
            tt(prod[:], le, bcast(ohg[:], EPG, 3), ALU.mult)
            dve.tensor_reduce(esel[:], prod[:].rearrange("p t g e -> p t e g"), AX, ALU.add)
            dve.drain()
            dve.tensor_reduce(top[:, 0], esel[:], AX, ALU.max)
            dve.drain()
            tt(oh[:, 0], esel[:], bcast(top[:, 0], EPG, 2), ALU.is_equal)
            keep_first(oh[:, 0], EPG)
            dve.scalar_tensor_tensor(out=esel2[:].rearrange("p t e -> p (t e)"), in0=oh[:, 0].rearrange("p t e -> p (t e)"),
                                     scalar=-3.0e38, in1=esel[:].rearrange("p t e -> p (t e)"), op0=ALU.mult, op1=ALU.add)
            dve.drain()
            dve.tensor_reduce(top[:, 1], esel2[:], AX, ALU.max)
            dve.drain()
            dve.tensor_tensor(ediff[:], top[:, 1], top[:, 0], ALU.subtract).then_inc(e_done, 1)
            tt(oh[:, 1], esel2[:], bcast(top[:, 1], EPG, 2), ALU.is_equal)
            keep_first(oh[:, 1], EPG)
            dve.wait_ge(gexp_done, 1)
            dve.tensor_reduce(gsum[:], gdiff[:], AX, ALU.add)
            dve.wait_ge(eexp_done, 1)
            dve.tensor_scalar(wsum[:], ediff[:], 1.0, None, ALU.add)
            dve.drain()
            tt(pg[:], gsum[:], wsum[:], ALU.mult)
            dve.reciprocal(pg[:], pg[:])
            dve.drain()
            dve.tensor_copy(value[:, 0, :, 1], pg[:])
            dve.tensor_tensor(value[:, 1, :, 1], pg[:], ediff[:], ALU.mult)
            dve.wait_ge(c_in, 32)
            for c in range(2):
                dve.tensor_copy(value[:, c, :, 0], tokens[:])
                dve.tensor_tensor(pick[:, c].rearrange("p t (g e) -> p t g e", g=NG), bcast(ohg[:], EPG, 3),
                                  bcast(oh[:, c], NG, 2), ALU.mult)
            dve.drain()
            dve.tensor_tensor(both[:], pick[:, 0], pick[:, 1], ALU.add).then_inc(both_done, 1)
            dve.memset(before[:, 0], 0.0)
            dve.drain()
            dve.wait_ge(ranked, 1)
            for t in range(1, T):
                tt(before[:, t], before[:, t - 1], sum_ps[:, (t - 1) * NE:t * NE], ALU.add)
            tt(count[:], before[:, T - 1], sum_ps[:, (T - 1) * NE:T * NE], ALU.add)
            tt(place[:], before[:], rank_ps[:, 0:T * NE].rearrange("p (t e) -> p t e", t=T), ALU.add)
            dve.tensor_scalar(count[:], count[:], 1.0 / P, None, ALU.mult)
            dve.drain()
            tt(more[:], bcast(count[:], T, 2), bcast(steps[:, 0:T], NE, 1), ALU.is_gt)
            dve.tensor_reduce(nblk[:], more[:], AX, ALU.add)
            dve.drain()
            dve.tensor_tensor_scan(bend[:], bones[:], nblk[:], 0.0, ALU.mult, ALU.add)
            dve.drain()
            tt(past[:], bcast(steps[:], NE, 2), bcast(bend[:], BLOCKS, 1), ALU.is_ge)
            dve.tensor_reduce(of_block[:], past[:], AX, ALU.add)
            dve.drain()
            dve.tensor_scalar(of_block[:], of_block[:], float(NE - 1), None, ALU.min)
            dve.drain()
            dve.tensor_copy(W["block_expert"][:], of_block[:])
            dve.memset(fresh[:, 0:1], 1.0)
            dve.tensor_tensor(fresh[:, 1:], of_block[:, 1:], of_block[:, 0:BLOCKS - 1], ALU.not_equal)
            dve.drain()
            dve.tensor_copy(W["block_new"][:], fresh[:])
            dve.tensor_scalar(sign[:], fresh[:], 2.0, -1.0, ALU.mult, ALU.add)
            dve.drain()
            dve.tensor_tensor_scan(buffer[:], fresh[:], sign[:], 0.0, ALU.subtract, ALU.mult)
            dve.drain()
            dve.tensor_copy(W["block_buf"][:], buffer[:])
            tt(nblk[:], bend[:], nblk[:], ALU.subtract)
            dve.tensor_scalar(nblk[:], nblk[:], float(P), None, ALU.mult)
            dve.drain()
            tt(place[:], place[:], bcast(nblk[:], T, 1), ALU.add)
            for c in range(2):
                tt(weighed[:], pick[:, c], place[:], ALU.mult)
                dve.tensor_reduce(slot_f[:], weighed[:], AX, ALU.add)
                dve.drain()
                for t in range(T):
                    dve.tensor_copy(slot_u[c][t][:], slot_f[:, t:t + 1])
                op = dve.tensor_copy(W["slot_of"][:, :, c], slot_f[:])
                dve.drain()
            dve.tensor_copy(slot_f[:], slot_f[:]).then_inc(slots_done, 1)
            dve.wait_ge(table_in, 16)
            dve.tensor_copy(W["block_token"][:], table[:, :, 0])
            dve.tensor_copy(W["block_weight"][:], table[:, :, 1])


def expert_stage(nc, I, C, W, M):
    with ExitStack() as ctx:
        s = Scope(nc, ctx, "moe")
        wgu, wd = s.sb("wgu", [P, 2, KT, 2 * FF]), s.sb("wd", [P, 2, 2, D])
        wgu_hi, wgu_lo = (s.sb(k, [P, 2, KT, 2 * FF], F32R) for k in ("wgu_hi", "wgu_lo"))
        wd_hi, wd_lo = (s.sb(k, [P, 2, 2, D], F32R) for k in ("wd_hi", "wd_lo"))
        idx = [s.sb(f"idx{u}", [P, 1], U32) for u in range(2)]
        xg = s.sb("xg", [P, 2, D])
        xT_hi, xT_lo = (s.sb(k, [P, KT * P], F32R) for k in ("xT_hi", "xT_lo"))
        act_g, hid = s.sb("act_g", [P, FF]), s.sb("hid", [P, FF])
        hidT_hi, hidT_lo = (s.sb(k, [P, FF], F32R) for k in ("hidT_hi", "hidT_lo"))
        y = s.sb("y", [P, D])
        x_ps, gu_ps, h_ps, y_ps = s.ps("x", D), [s.ps(f"gu{u}") for u in range(2)], s.ps("h"), s.ps("y", D)
        gu_in, d_in, xg_in = ([s.sem(f"{k}{u}") for u in range(2)] for k in ("gu_in", "d_in", "xg_in"))
        y_out = s.sem("y_out")
        gu_hi_done, gu_lo_done, d_hi_done, d_lo_done = (s.sem(k) for k in ("gu_hi_done", "gu_lo_done", "d_hi_done", "d_lo_done"))
        idx_done, started, x_turned, x_hi_done, x_lo_done = (s.sem(k) for k in ("idx_done", "started", "x_turned", "x_hi_done", "x_lo_done"))
        gu_done, silu_done, hid_done, h_turned = (s.sem(k) for k in ("gu_done", "silu_done", "hid_done", "h_turned"))
        hidT_done, y_done, y_read = (s.sem(k) for k in ("hidT_done", "y_done", "y_read"))
        block = ctx.enter_context(nc.Block())
        expert, token, weight = W["block_expert"], W["block_token"], W["block_weight"]

        def blocks(eng, body):
            assert BLOCKS % 2 == 1
            body(Step(0, 0), 3)
            with eng.Fori(0, (BLOCKS - 5) // 2) as i:
                body(Step(i, 1), 3)
                body(Step(i, 2), 3)
            for n in range(BLOCKS - 4, BLOCKS):
                body(Step(0, n), BLOCKS - 1 - n)

        def weight_buffer(eng, k):
            return eng.value_load(W["block_buf"][0:1, bass.ds(k.n, 1)], min_val=0, max_val=1)

        def block_values(eng, k):
            return (eng.value_load(expert[0:1, bass.ds(k.n, 1)], min_val=0, max_val=NE - 1), weight_buffer(eng, k),
                    eng.value_load(W["block_new"][0:1, bass.ds(k.n, 1)], min_val=0, max_val=1))

        @block.sync
        def _(sp):
            def load_gu(k):
                e, buf, new = block_values(sp, k)
                sp.wait_ge(gu_lo_done, k.n + 1)
                sp.dma_start(wgu[:, buf, :, 0:FF], I["w_exp_gate"][0, e].rearrange("(k p) f -> p k f", p=P), cond=new).then_inc(gu_in[k.buf], 16)
                sp.dma_start(wgu[:, buf, :, FF:], I["w_exp_up"][0, e].rearrange("(k p) f -> p k f", p=P), cond=new).then_inc(gu_in[k.buf], 16)

            def load_d(k):
                e, buf, new = block_values(sp, k)
                sp.wait_ge(d_lo_done, k.n + 1)
                sp.dma_start(wd[:, buf], I["w_exp_down"][0, e].rearrange("(k p) d -> p k d", p=P), cond=new).then_inc(d_in[k.buf], 16)

            def body(t, left):
                if left >= 3:
                    load_gu(t.next().next().next())
                if not (isinstance(t.n, int) and t.n == 0):
                    store(Step(t.i, t.c - 1))
                if left >= 2:
                    load_d(t.next().next())

            def store(t):
                sp.wait_ge(y_read, t.n + 2)
                sp.dma_start(M["y_slots"][bass.ds(t.n * P, P), :], y[:]).then_inc(y_out, 16)

            load_gu(Step(0, 0))
            load_d(Step(0, 0))
            load_gu(Step(0, 1))
            load_d(Step(0, 1))
            load_gu(Step(0, 2))
            blocks(sp, body)
            store(Step(0, BLOCKS - 1))
            sp.wait_ge(y_out, 16 * (BLOCKS + 1))

        @block.gpsimd
        def _(pool):
            pool.sem_inc(d_lo_done, 2)

            def gather(k):
                pool.wait_ge(x_turned, k.n + 1)
                pool.tensor_copy(idx[k.buf][:], token[:, bass.ds(k.n, 1)]).then_inc(idx_done, 1)
                pool.wait_ge(idx_done, k.n + 1)
                pool.sem_inc(started, 1)
                pool.indirect_dma_start(xg[:, k.buf], None, M["h2"],
                                        bass.IndirectOffsetOnAxis(ap=idx[k.buf][:], axis=0)).then_inc(xg_in[k.buf], 16)

            def body(t, left):
                if left >= 2:
                    gather(t.next().next())
                buf = weight_buffer(pool, t)
                pool.wait_ge(d_hi_done, t.n + 1)
                for half in range(2):
                    op = split_low(pool, wd_lo[:, t.buf, half], wd[:, buf, half], wd_hi[:, t.buf, half])
                op.then_inc(d_lo_done, 1)
            gather(Step(0, 0))
            gather(Step(0, 1))
            blocks(pool, body)

        @block.tensor
        def _(pe):
            ident = C["ident"]
            pe.sem_inc(y_done, 2)
            pe.sem_inc(x_turned, 2)
            pe.sem_inc(gu_done, 2)
            pe.sem_inc(h_turned, 2)

            def turn_x(k):
                pe.wait_ge(xg_in[k.buf], k.nth * 16 + 16)
                pe.wait_ge(x_lo_done, k.n + 1)
                for j in range(KT):
                    mm = pe.transpose(x_ps[:, j * P:(j + 1) * P], xg[:, k.buf, j * P:(j + 1) * P], ident[:])
                mm.then_inc(x_turned, 1)

            def gate_up(k):
                pe.wait_ge(x_lo_done, k.n + 2)
                pe.wait_ge(gu_lo_done, k.n + 3)
                pe.wait_ge(hid_done, k.n + 1)
                for j in range(KT):
                    cols = slice(j * P, (j + 1) * P)
                    mm = split_product(pe, gu_ps[k.buf][:], xT_hi[:, cols], xT_lo[:, cols],
                                       wgu_hi[:, k.buf, j], wgu_lo[:, k.buf, j], j == 0, j == KT - 1)
                mm.then_inc(gu_done, 1)

            def body(t, left):
                if left >= 1:
                    gate_up(t.next())
                pe.wait_ge(hid_done, t.n + 3)
                pe.wait_ge(hidT_done, t.n + 1)
                for j in range(2):
                    mm = pe.transpose(h_ps[:, j * P:(j + 1) * P], hid[:, j * P:(j + 1) * P], ident[:])
                mm.then_inc(h_turned, 1)
                if left >= 2:
                    turn_x(t.next().next())
                pe.wait_ge(hidT_done, t.n + 2)
                pe.wait_ge(d_lo_done, t.n + 3)
                pe.wait_ge(y_read, t.n + 1)
                for half in range(2):
                    cols = slice(half * 512, (half + 1) * 512)
                    for j in range(2):
                        mm = split_product(pe, y_ps[:, cols], hidT_hi[:, j * P:(j + 1) * P], hidT_lo[:, j * P:(j + 1) * P],
                                           wd_hi[:, t.buf, j, cols], wd_lo[:, t.buf, j, cols], j == 0, j == 1)
                mm.then_inc(y_done, 1)

            turn_x(Step(0, 0))
            gate_up(Step(0, 0))
            turn_x(Step(0, 1))
            blocks(pe, body)

        @block.scalar
        def _(act):
            act.sem_inc(y_read, 1)
            act.sem_inc(y_out, 16)

            def gu_high(k):
                buf = weight_buffer(act, k)
                act.wait_ge(gu_in[k.buf], k.nth * 32 + 32)
                act.wait_ge(gu_done, k.n + 1)
                for j in range(0, KT, 2):
                    act.copy(wgu_hi[:, k.buf, j:j + 2], wgu[:, buf, j:j + 2]).then_inc(gu_hi_done, 1)

            def d_high(k):
                buf = weight_buffer(act, k)
                act.wait_ge(d_in[k.buf], k.nth * 16 + 16)
                act.wait_ge(y_done, k.n + 1)
                act.copy(wd_hi[:, k.buf], wd[:, buf]).then_inc(d_hi_done, 1)

            def x_high(k):
                act.wait_ge(x_turned, k.n + 3)
                act.wait_ge(gu_done, k.n + 2)
                act.copy(xT_hi[:], x_ps[:]).then_inc(x_hi_done, 1)

            def silu(k):
                act.wait_ge(gu_done, k.n + 3)
                act.wait_ge(hid_done, k.n + 2)
                act.activation(act_g[:], gu_ps[k.buf][:, 0:FF], ACT.Silu).then_inc(silu_done, 1)

            def evacuate(t):
                act.wait_ge(y_done, t.n + 3)
                act.wait_ge(y_out, t.n * 16 + 16)
                act.copy(y[:], y_ps[:]).then_inc(y_read, 1)

            def body(t, left):
                if left >= 2:
                    gu_high(t.next().next())
                if not (isinstance(t.n, int) and t.n == 0):
                    evacuate(Step(t.i, t.c - 1))
                if left >= 1:
                    d_high(t.next())
                    silu(t.next())
                if left >= 2:
                    x_high(t.next().next())

            gu_high(Step(0, 0))
            x_high(Step(0, 0))
            gu_high(Step(0, 1))
            d_high(Step(0, 0))
            silu(Step(0, 0))
            x_high(Step(0, 1))
            blocks(act, body)
            evacuate(Step(0, BLOCKS - 1))

        @block.vector
        def _(dve):
            dve.sem_inc(gu_lo_done, 2)
            dve.sem_inc(x_lo_done, 1)
            dve.sem_inc(hid_done, 2)
            dve.sem_inc(hidT_done, 1)

            def gu_low(k):
                buf = weight_buffer(dve, k)
                for j in range(0, KT, 2):
                    dve.wait_ge(gu_hi_done, k.n * (KT // 2) + (j // 2 + 1))
                    op = split_low(dve, wgu_lo[:, k.buf, j:j + 2], wgu[:, buf, j:j + 2], wgu_hi[:, k.buf, j:j + 2])
                op.then_inc(gu_lo_done, 1)

            def x_low(k):
                dve.wait_ge(x_hi_done, k.n + 1)
                split_low(dve, xT_lo[:], x_ps[:], xT_hi[:]).then_inc(x_lo_done, 1)

            def hidden(k):
                dve.wait_ge(silu_done, k.n + 1)
                dve.wait_ge(h_turned, k.n + 2)
                dve.scalar_tensor_tensor(out=hid[:], in0=gu_ps[k.buf][:, FF:2 * FF], scalar=weight[:, bass.ds(k.n, 1)],
                                         in1=act_g[:], op0=ALU.mult, op1=ALU.mult).then_inc(hid_done, 1)

            def body(t, left):
                hidden(t)
                if left >= 2:
                    gu_low(t.next().next())
                dve.wait_ge(h_turned, t.n + 3)
                dve.wait_ge(y_done, t.n + 2)
                dve.tensor_copy(hidT_hi[:], h_ps[:, 0:FF])
                dve.drain()
                split_low(dve, hidT_lo[:], h_ps[:, 0:FF], hidT_hi[:]).then_inc(hidT_done, 1)
                if left >= 2:
                    x_low(t.next().next())

            gu_low(Step(0, 0))
            x_low(Step(0, 0))
            gu_low(Step(0, 1))
            x_low(Step(0, 1))
            blocks(dve, body)


def final_stage(nc, I, C, W, M):
    NB = 3
    with ExitStack() as ctx:
        s = Scope(nc, ctx, "fin")
        gate, gain = s.sb("gate", [P, 2, D]), s.sb("gain", [P, D])
        ya, yb = s.sb("ya", [P, NB, D]), s.sb("yb", [P, NB, D])
        idx = [[s.sb(f"idx{c}{u}", [P, 1], U32) for u in range(NB)] for c in range(2)]
        out, junk = s.sb("out", [P, NB, D]), s.sb("junk", [P, D])
        ssq, rstd, tmp, epsc = s.sb("ssq", [P, NB]), s.sb("rstd", [P, NB]), s.sb("tmp", [P, 1]), s.sb("epsc", [P, 1])
        g_in, idx_done = s.sem("g_in"), s.sem("idx_done")
        y_in = [s.sem(f"y_in{u}") for u in range(NB)]
        x3_done, sq_done, out_done, out_stored = s.sem("x3_done"), s.sem("sq_done"), s.sem("out_done"), [s.sem(f"out_stored{u}") for u in range(NB)]
        block = ctx.enter_context(nc.Block())
        started = s.sem("started")
        x2, slot_of = W["x2"], W["slot_of"]

        def tiles(eng, body, first=lambda t: None):
            first(Step(0, 0, NB))
            body(Step(0, 0, NB), True)
            loops = (TILES - 2) // NB
            with eng.Fori(0, loops) as i:
                for c in range(1, NB + 1):
                    body(Step(i, c, NB), True)
            for n in range(loops * NB + 1, TILES):
                body(Step(0, n, NB), n < TILES - 1)

        def is_first(t):
            return isinstance(t.n, int) and t.n == 0

        @block.sync
        def _(sp):
            for cond in range(2):
                sp.dma_start(gate[:, cond], row_bcast(M["mods"][cond, GATE2 * D:(GATE2 + 1) * D])).then_inc(g_in, 16)
            sp.dma_start(gain[:], row_bcast(I["final_norm_g"])).then_inc(g_in, 16)

            def body(t, more):
                dst = I["y_prompt"][0] if is_first(t) else I["y_sample"][0, bass.ds((t.n - 1) * P, P), :]
                sp.wait_ge(out_done, t.n + 1)
                sp.dma_start(dst, out[:, t.buf]).then_inc(out_stored[t.buf], 16)
            tiles(sp, body)
            for u in range(NB):
                sp.wait_ge(out_stored[u], 16 * (TILES // NB + 1))

        @block.gpsimd
        def _(pool):
            def body(t, more):
                pool.wait_ge(x3_done, t.n + 1)
                for c in range(2):
                    pool.tensor_copy(idx[c][t.buf][:], slot_of[:, t.n, c:c + 1]).then_inc(idx_done, 1)
                pool.wait_ge(idx_done, t.n * 2 + 2)
                pool.sem_inc(started, 1)
                for c, dst in enumerate((ya, yb)):
                    pool.indirect_dma_start(dst[:, t.buf], None, M["y_slots"],
                                            bass.IndirectOffsetOnAxis(ap=idx[c][t.buf][:], axis=0)).then_inc(y_in[t.buf], 16)
            tiles(pool, body)

        @block.scalar
        def _(act):
            def body(t, more):
                act.wait_ge(x3_done, t.n + 1 + NB)
                act.activation(junk[:], x2[:, t.n], ACT.Square, accum_out=ssq[:, t.buf:t.buf + 1])
                act.drain()
                act.activation(rstd[:, t.buf:t.buf + 1], ssq[:, t.buf:t.buf + 1], ACT.Sqrt, bias=epsc[:, 0:1],
                               scale=1.0 / D).then_inc(sq_done, 1)
            tiles(act, body)

        @block.vector
        def _(dve):
            dve.memset(epsc[:], EPS)
            dve.sem_inc(x3_done, NB)
            for u in range(NB):
                dve.sem_inc(out_stored[u], 16)
            dve.wait_ge(g_in, 48)

            def residual(t):
                cond = 0 if is_first(t) else 1
                dve.wait_ge(y_in[t.buf], t.nth * 32 + 32)
                dve.tensor_tensor(ya[:, t.buf], ya[:, t.buf], yb[:, t.buf], ALU.add)
                dve.drain()
                dve.tensor_tensor(ya[:, t.buf], ya[:, t.buf], gate[:, cond], ALU.mult)
                dve.drain()
                dve.tensor_tensor(x2[:, t.n], x2[:, t.n], ya[:, t.buf], ALU.add).then_inc(x3_done, 1)

            def body(t, more):
                if more:
                    residual(t.next())
                r = rstd[:, t.buf:t.buf + 1]
                dve.wait_ge(sq_done, t.n + 1)
                dve.reciprocal(r, r)
                refine(dve, r, ssq[:, t.buf:t.buf + 1], 1.0 / D, tmp[:])
                dve.wait_ge(out_stored[t.buf], t.nth * 16 + 16)
                dve.scalar_tensor_tensor(out=out[:, t.buf], in0=x2[:, t.n], scalar=r, in1=gain[:], op0=ALU.mult,
                                         op1=ALU.mult).then_inc(out_done, 1)
            tiles(dve, body, residual)


def load_stage(nc, tag, loads):
    with ExitStack() as ctx:
        loaded = Scope(nc, ctx, tag).sem("done")
        block = ctx.enter_context(nc.Block())

        @block.sync
        def _(sp):
            for dst, src in loads:
                sp.dma_start(dst, src).then_inc(loaded, 16)
            sp.wait_ge(loaded, 16 * len(loads))


def build(nc, I, M):
    with ExitStack() as ctx:
        s = Scope(nc, ctx, "all")
        C = {"ident": s.sb("ident", [P, P]), "cond": s.sb("cond", [P, KT, 2])}
        load_stage(nc, "load_ident", [(C["ident"][:], I["ident"])])
        W = {}
        with ExitStack() as mix_ctx:
            with ExitStack() as att_ctx:
                right = Scope(nc, att_ctx, "att_in")
                ada_stage(nc, I, C, W, M)
                W["dt_tok"] = right.sb("dt_tok", [P, TILES, 2 * SH], side="right")
                with ExitStack() as proj_ctx:
                    ps = Scope(nc, proj_ctx, "proj")
                    W["amul1"], W["aadd1"] = ps.sb("amul1", [P, 2, D]), ps.sb("aadd1", [P, 2, D])
                    projection_stage(nc, I, C, W, M, "zx")
                    W["kT"] = right.sb("kT", [P, HEADS, (TILES + 1) * P], side="right")
                    W["qT"] = right.sb("qT", [P, HEADS, TILES * P], side="right")
                    W["v_tok"] = right.sb("v_tok", [P, TILES + 1, 512], side="right")
                    projection_stage(nc, I, C, W, M, "qkv")
                for name in ("tri_le", "tri_ge", "tri_lt"):
                    C[name] = s.sb(name, [P, P])
                load_stage(nc, "load_tri", [(C[name][:], I[name]) for name in ("tri_le", "tri_ge", "tri_lt")])
                m = Scope(nc, mix_ctx, "mix_in")
                W["y_tok"] = m.sb("y_tok", [P, TILES, DSSM])
                scan_stages(nc, I, C, W, M)
                W["o_tok"] = m.sb("o_tok", [P, TILES, DATT])
                W["w_out_hi"], W["w_out_lo"] = m.sb("w_out_hi", [P, KT, D], F32R), m.sb("w_out_lo", [P, KT, D], F32R)
                W["gcol"] = m.sb("gcol", [P, KT])
                W["gate"] = m.sb("gate", [P, 2, D])
                W["w_out_in"], W["gains_in"], W["w_out_split"] = m.sem("w_out_in"), m.sem("gains_in"), m.sem("w_out_split")
                with ExitStack() as raw_ctx:
                    W["w_out_raw"] = Scope(nc, raw_ctx, "mix_w").sb("raw", [P, D])
                    attention_stage(nc, I, C, W, M)
            r = Scope(nc, ctx, "moe_in")
            W["x2"] = r.sb("x2", [P, TILES, D], side="right")
            W["logits"] = r.sb("logits", [P, TILES, NG + NE], side="right")
            mixer_stage(nc, I, C, W, M)
        W["block_expert"] = s.sb("block_expert", [P, BLOCKS], I32)
        W["block_new"], W["block_buf"] = s.sb("block_new", [P, BLOCKS], I32), s.sb("block_buf", [P, BLOCKS], I32)
        W["block_token"] = s.sb("block_token", [P, BLOCKS], U32)
        W["block_weight"] = s.sb("block_weight", [P, BLOCKS])
        W["slot_of"] = s.sb("slot_of", [P, TILES, 2], U32)
        routing_stage(nc, I, C, W, M)
        expert_stage(nc, I, C, W, M)
        final_stage(nc, I, C, W, M)


_INS = ['x_prompt', 'x_sample', 'cache_k', 'cache_v', 'state_ssm_fwd', 'state_ssm_bwd', 'c', 'c_ctx', 'w_ada', 'b_ada',
        'norm_mix_g', 'w_in', 'w_out', 'lambda_q1', 'lambda_k1', 'lambda_q2', 'lambda_k2', 'attn_subln_g', 'conv_w',
        'conv_b', 'a_log_fwd', 'a_log_bwd', 'dt_bias_fwd', 'dt_bias_bwd', 'ssm_d', 'ssm_norm_g', 'norm_ffn_g',
        'w_group_router', 'b_group_router', 'w_expert_router', 'b_expert_router', 'w_exp_gate', 'w_exp_up',
        'w_exp_down', 'final_norm_g']
_OUTS = {'y_prompt': (1, P, D), 'y_sample': (1, STILES * P, D), 'new_k': (1, 1, P, HEADS, 2, QKD),
         'new_v': (1, 1, P, HEADS, P), 'new_hf': (1, 1, SH, 64, P), 'new_hb': (1, 1, SH, 64, P)}
_SCRATCH = {'mods': (2, 6 * D), 'z': (TILES * P, 512), 'xbc': (TILES * P, XBC),
            'h2': (TILES * P, D), 'slots': (SLOTS, 2), 'y_slots': (SLOTS, D)}
_DEBUG = []


def shape_constants():
    i = np.arange(P)
    c = {
        'ident': np.eye(P, dtype=np.float32),
        'tri_le': (i[:, None] <= i[None, :]).astype(np.float32),
        'tri_ge': (i[:, None] >= i[None, :]).astype(np.float32),
        'tri_lt': (i[:, None] < i[None, :]).astype(np.float32),
        'pick': np.repeat(np.eye(2 * SH, dtype=np.float32)[:, :, None], P, axis=2),
    }
    c['steps'] = np.arange(BLOCKS, dtype=np.float32)
    c['tokens'] = (i[:, None] + P * np.arange(TILES)[None, :]).astype(np.float32)
    pos = np.arange(STILES * P)
    freqs = np.float32(10000.0) ** (-np.arange(16, dtype=np.float32) / np.float32(16))
    rope = np.zeros((TILES, P, 2, 2, 2, 16), np.float32)
    rope[0, :, 0] = 1.0
    for axis, ids in enumerate((pos // 64, pos % 64)):
        ang = (ids.astype(np.float32)[:, None] * freqs).reshape(STILES, P, 16)
        rope[1:, :, 0, axis, 0] = rope[1:, :, 0, axis, 1] = np.cos(ang)
        rope[1:, :, 1, axis, 0] = -np.sin(ang)
        rope[1:, :, 1, axis, 1] = np.sin(ang)
    c['rope'] = rope.reshape(TILES, P, 2, QKD)
    return c


def kernel(**inputs):
    import concourse.bacc as _bacc
    from concourse.bass_utils import run_bass_kernel_spmd as _run

    nc = _bacc.Bacc("TRN2", target_bir_lowering=False, num_devices=1)
    arrays, io = {}, {}
    for name in _INS:
        arrays[f"in_{name}"] = np.ascontiguousarray(inputs[name])
    for name, a in shape_constants().items():
        arrays[f"in_{name}"] = a
    for name, a in arrays.items():
        io[name[3:]] = nc.dram_tensor(name, a.shape, F32, kind="ExternalInput").ap()
    for name, shape in _OUTS.items():
        io[name] = nc.dram_tensor(f"out_{name}", shape, F32, kind="ExternalOutput").ap()
    scratch = {name: nc.dram_tensor(f"scratch_{name}", shape, F32,
                                    kind="ExternalOutput" if name in _DEBUG else "Internal").ap()
               for name, shape in _SCRATCH.items()}
    build(nc, io, scratch)
    r = _run(nc, [arrays], core_ids=[0])
    if _DEBUG:
        return tuple(r.results[0][f"scratch_{n}"] if n in _SCRATCH else r.results[0][f"out_{n}"] for n in _DEBUG)
    return tuple(r.results[0][f"out_{name}"] for name in _OUTS)
```
